# Optimizing a Trainium2 kernel written in Bass

```python
import jax, jax.numpy as jnp
from jax import lax
import numpy as np
import math

D_MODEL = 1024
BATCH = 1
SEQ = 512
DEPTH = 1

CHUNK = 64
Q_BLOCK = 128
POOL_WIDTH = D_MODEL // 2
POOL_WINDOWS = (2, 4, 8, 16)
N_POOL_GROUPS = len(POOL_WINDOWS)
POOL_GROUP = POOL_WIDTH // N_POOL_GROUPS
SB_HEAD_DIM = 64
SB_HEADS = (D_MODEL // 2) // SB_HEAD_DIM
SB_WIDTH = SB_HEADS * SB_HEAD_DIM
IN_WIDTH = POOL_WIDTH + 3 * SB_WIDTH
N_BRANCHES = 2
D_FF = 4 * D_MODEL
RMS_EPS = 1e-6


def rmsnorm(x, gain):
    xf = x.astype(jnp.float32)
    y = xf * lax.rsqrt(jnp.mean(xf * xf, axis=-1, keepdims=True) + RMS_EPS)
    return (y * gain.astype(jnp.float32)).astype(x.dtype)

def multiscale_pool(u, w_pool_mix, pool_scale):
    S = u.shape[1]
    uf = u.astype(jnp.float32)
    cs = jnp.concatenate([jnp.zeros_like(uf[:, :1]), jnp.cumsum(uf, axis=1)], axis=1)
    hi = jnp.arange(S) + 1
    outs = []
    for g, w in enumerate(POOL_WINDOWS):
        c0, c1 = g * POOL_GROUP, (g + 1) * POOL_GROUP
        lo = jnp.maximum(hi - w, 0)
        csg = cs[:, :, c0:c1]
        win_sum = csg[:, hi] - csg[:, lo]
        count = (hi - lo).astype(jnp.float32)[None, :, None]
        pooled = win_sum / count - uf[:, :, c0:c1]
        outs.append(jnp.einsum('bsc,cd->bsd', pooled.astype(u.dtype), w_pool_mix[g]))
    y = jnp.concatenate(outs, axis=-1)
    return y * pool_scale

def stick_breaking_attention(q, k, v):
    S = q.shape[2]
    scale = SB_HEAD_DIM ** -0.5
    outs = []
    for blk in range(S // Q_BLOCK):
        t0, t1 = blk * Q_BLOCK, (blk + 1) * Q_BLOCK
        qb, kb, vb = q[:, :, t0:t1], k[:, :, :t1], v[:, :, :t1]
        z = jnp.einsum('bhqd,bhkd->bhqk', qb, kb).astype(jnp.float32) * scale
        mask = jnp.arange(t1)[None, :] < jnp.arange(t0, t1)[:, None]
        log_1mb = jnp.where(mask, jax.nn.log_sigmoid(-z), 0.0)
        tail = lax.cumsum(log_1mb, axis=3, reverse=True) - log_1mb
        attn = jnp.where(mask, jnp.exp(jax.nn.log_sigmoid(z) + tail), 0.0)
        outs.append(jnp.einsum('bhqk,bhkd->bhqd', attn.astype(vb.dtype), vb))
    return jnp.concatenate(outs, axis=2)

def first_inputs(seed: int = 0) -> dict:
    key = jax.random.key(seed)
    ks = jax.random.split(key, 20)
    f32 = jnp.float32
    nrm = lambda k, shape, fan_in: jax.random.normal(k, shape, f32) * (fan_in ** -0.5)
    gain = lambda k, n: 1.0 + 0.02 * jax.random.normal(k, (n,), f32)
    return {
        "x": jax.random.normal(ks[0], (BATCH, SEQ, D_MODEL), f32),
        "g_pre_mix": gain(ks[1], D_MODEL),
        "w_in": nrm(ks[2], (D_MODEL, IN_WIDTH), D_MODEL),
        "w_pool_mix": nrm(ks[3], (N_POOL_GROUPS, POOL_GROUP, POOL_GROUP), POOL_GROUP),
        "pool_scale": gain(ks[4], POOL_WIDTH),
        "w_br_pool": nrm(ks[5], (POOL_WIDTH, D_MODEL), POOL_WIDTH),
        "w_br_sb": nrm(ks[6], (SB_WIDTH, D_MODEL), SB_WIDTH),
        "w_gate": nrm(ks[7], (D_MODEL, N_BRANCHES * D_MODEL), D_MODEL),
        "b_gate": 0.01 * jax.random.normal(ks[8], (N_BRANCHES * D_MODEL,), f32),
        "w_out": nrm(ks[9], (D_MODEL, D_MODEL), D_MODEL),
        "g_post_mix": gain(ks[10], D_MODEL),
        "g_pre_mlp": gain(ks[11], D_MODEL),
        "w_up": nrm(ks[12], (D_MODEL, D_FF), D_MODEL),
        "w_down": nrm(ks[13], (D_FF, D_MODEL), D_FF),
        "g_post_mlp": gain(ks[14], D_MODEL),
    }

def first_block(x, g_pre_mix, w_in, w_pool_mix, pool_scale, w_br_pool, w_br_sb,
              w_gate, b_gate, w_out, g_post_mix, g_pre_mlp, w_up, w_down, g_post_mlp):
    B, S, _ = x.shape
    for _layer in range(DEPTH):
        h = rmsnorm(x, g_pre_mix)
        proj = jnp.einsum('bsd,de->bse', h, w_in)
        u_pool = proj[..., :POOL_WIDTH]
        qkv = proj[..., POOL_WIDTH:].reshape(B, S, 3, SB_HEADS, SB_HEAD_DIM)
        q, k, v = (jnp.transpose(qkv[:, :, i], (0, 2, 1, 3)) for i in range(3))

        y_pool = jnp.einsum('bsc,cd->bsd', multiscale_pool(u_pool, w_pool_mix, pool_scale), w_br_pool)
        o_sb = stick_breaking_attention(q, k, v)
        o_sb = jnp.transpose(o_sb, (0, 2, 1, 3)).reshape(B, S, SB_WIDTH)
        y_sb = jnp.einsum('bsc,cd->bsd', o_sb, w_br_sb)

        gates = jax.nn.sigmoid(jnp.einsum('bsd,de->bse', h, w_gate) + b_gate)
        merged = gates[..., :D_MODEL] * y_pool + gates[..., D_MODEL:] * y_sb
        mix = jnp.einsum('bsd,de->bse', merged, w_out)
        x = x + rmsnorm(mix, g_post_mix)

        h2 = rmsnorm(x, g_pre_mlp)
        a = jnp.square(jax.nn.relu(jnp.einsum('bsd,df->bsf', h2, w_up)))
        ff = jnp.einsum('bsf,fd->bsd', a, w_down)
        x = x + rmsnorm(ff, g_post_mlp)
    return x


DEPTH_2 = 2

N_META = 16
N_A_LAYERS = DEPTH_2 // 2
N_B_LAYERS = DEPTH_2 - N_A_LAYERS
NORM_EPS = 1e-6

GDN_QK_HEADS = 8
GDN_V_HEADS = 16
GDN_DK = 128
GDN_DV = 128
GDN_CONV = 4
GDN_CHUNK = 64
GDN_QK_W = GDN_QK_HEADS * GDN_DK
GDN_V_W = GDN_V_HEADS * GDN_DV
GDN_CONV_W = 2 * GDN_QK_W + GDN_V_W
GDN_IN_W = GDN_CONV_W + GDN_V_W + 2 * GDN_V_HEADS

MLA_HEADS = 16
MLA_NOPE = 128
MLA_ROPE = 64
MLA_V = 128
MLA_Q_RANK = 256
MLA_KV_RANK = 128
MLA_QK = MLA_NOPE + MLA_ROPE
MLA_V_W = MLA_HEADS * MLA_V
MLA_IN_W = MLA_Q_RANK + MLA_V_W
ROPE_THETA = 10000.0


def rmsnorm_2(x, g):
    xf = x.astype(jnp.float32)
    y = xf * lax.rsqrt(jnp.mean(xf * xf, axis=-1, keepdims=True) + NORM_EPS)
    return (y * g.astype(jnp.float32)).astype(x.dtype)

def l2norm(x):
    xf = x.astype(jnp.float32)
    return (xf * lax.rsqrt(jnp.sum(xf * xf, axis=-1, keepdims=True) + NORM_EPS)).astype(x.dtype)

def causal_depthwise_conv(x, w):
    k_len, ch = w.shape
    return lax.conv_general_dilated(x, w[:, None, :].astype(x.dtype), window_strides=(1,),
                                    padding=[(k_len - 1, 0)],
                                    dimension_numbers=('NWC', 'WIO', 'NWC'),
                                    feature_group_count=ch)

def rope_tables(length):
    inv = ROPE_THETA ** (-jnp.arange(0, MLA_ROPE, 2, dtype=jnp.float32) / MLA_ROPE)
    ang = jnp.arange(length, dtype=jnp.float32)[:, None] * inv[None, :]
    return jnp.cos(ang), jnp.sin(ang)

def apply_rope(x, cos, sin):
    xf = x.astype(jnp.float32)
    half = MLA_ROPE // 2
    x1, x2 = xf[..., :half], xf[..., half:]
    return jnp.concatenate([x1 * cos - x2 * sin, x2 * cos + x1 * sin], axis=-1).astype(x.dtype)

def gated_delta_rule_chunked(q, k, v, beta, g):
    B, L, H, dk = q.shape
    dv = v.shape[-1]
    C = GDN_CHUNK
    pad = (-L) % C
    n_chunks = (L + pad) // C

    def blocks(t):
        t = jnp.pad(t.astype(jnp.float32), [(0, 0), (pad, 0)] + [(0, 0)] * (t.ndim - 2))
        t = t.reshape((B, n_chunks, C) + t.shape[2:])
        return jnp.moveaxis(t, 3, 1)

    q, k, v, beta, g = blocks(q), blocks(k), blocks(v), blocks(beta), blocks(g)
    gc = jnp.cumsum(g, axis=-1)
    idx = jnp.arange(C)
    incl = idx[:, None] >= idx[None, :]
    strict = idx[:, None] > idx[None, :]
    decay = jnp.exp(jnp.where(incl, gc[..., :, None] - gc[..., None, :], -jnp.inf))

    kb = k * beta[..., None]
    vb = v * beta[..., None]
    m = jnp.einsum('bhnid,bhnjd->bhnij', kb, k) * jnp.where(strict, decay, 0.0)
    eye = jnp.eye(C, dtype=jnp.float32)
    rhs = jnp.concatenate([vb, kb * jnp.exp(gc)[..., None]], axis=-1)
    sol = lax.linalg.triangular_solve(m + eye, rhs, left_side=True, lower=True, unit_diagonal=True)
    u, w = sol[..., :dv], sol[..., dv:]

    attn = jnp.einsum('bhnid,bhnjd->bhnij', q, k) * decay
    q_dec = q * jnp.exp(gc)[..., None]
    k_dec = k * jnp.exp(gc[..., -1:] - gc)[..., None]
    g_last = jnp.exp(gc[..., -1])

    def step(state, xs):
        u_c, w_c, qd_c, kd_c, a_c, gl_c = xs
        v_new = u_c - jnp.einsum('bhcd,bhde->bhce', w_c, state)
        o_c = jnp.einsum('bhcd,bhde->bhce', qd_c, state) + jnp.einsum('bhij,bhje->bhie', a_c, v_new)
        state = state * gl_c[..., None, None] + jnp.einsum('bhcd,bhce->bhde', kd_c, v_new)
        return state, o_c

    xs = tuple(jnp.moveaxis(t, 2, 0) for t in (u, w, q_dec, k_dec, attn, g_last))
    s0 = jnp.zeros((B, H, dk, dv), jnp.float32)
    _, o = lax.scan(step, s0, xs)
    o = jnp.transpose(o, (1, 0, 3, 2, 4)).reshape(B, n_chunks * C, H, dv)
    return o[:, pad:]

def gdn_mixer(h, w_in, conv_w, a_log, dt_bias, out_norm, w_out):
    B, L, _ = h.shape
    proj = h @ w_in
    s1, s2, s3 = GDN_CONV_W, GDN_CONV_W + GDN_V_W, GDN_CONV_W + GDN_V_W + GDN_V_HEADS
    qkv, z, b, a = proj[..., :s1], proj[..., s1:s2], proj[..., s2:s3], proj[..., s3:]
    qkv = jax.nn.silu(causal_depthwise_conv(qkv, conv_w))
    q = l2norm(qkv[..., :GDN_QK_W].reshape(B, L, GDN_QK_HEADS, GDN_DK)) * (GDN_DK ** -0.5)
    k = l2norm(qkv[..., GDN_QK_W:2 * GDN_QK_W].reshape(B, L, GDN_QK_HEADS, GDN_DK))
    v = qkv[..., 2 * GDN_QK_W:].reshape(B, L, GDN_V_HEADS, GDN_DV)
    rep = GDN_V_HEADS // GDN_QK_HEADS
    q = jnp.repeat(q, rep, axis=2)
    k = jnp.repeat(k, rep, axis=2)
    beta = jax.nn.sigmoid(b.astype(jnp.float32))
    g = -jnp.exp(a_log.astype(jnp.float32)) * jax.nn.softplus(a.astype(jnp.float32) + dt_bias.astype(jnp.float32))
    o = gated_delta_rule_chunked(q, k, v, beta, g)
    o = rmsnorm_2(o, out_norm) * jax.nn.silu(z.astype(jnp.float32).reshape(B, L, GDN_V_HEADS, GDN_DV))
    return o.reshape(B, L, GDN_V_W).astype(h.dtype) @ w_out

def mla_shared_kv(h, kv_norm, kv_w_down, kv_latent_norm, kv_w_up, cos, sin):
    B, L, _ = h.shape
    ckr = rmsnorm_2(h, kv_norm) @ kv_w_down
    c_kv = rmsnorm_2(ckr[..., :MLA_KV_RANK], kv_latent_norm)
    k_rope = apply_rope(ckr[..., MLA_KV_RANK:], cos, sin)
    kv = (c_kv @ kv_w_up).reshape(B, L, MLA_HEADS, MLA_NOPE + MLA_V)
    return kv[..., :MLA_NOPE], k_rope, kv[..., MLA_NOPE:]

def causal_block_attention(q_nope, q_rope, k_nope, k_rope, v):
    B, L, H, _ = q_nope.shape
    n_blocks = -(-L // Q_BLOCK)
    pad = n_blocks * Q_BLOCK - L

    def blocks(t):
        t = jnp.pad(t, [(0, 0), (0, pad)] + [(0, 0)] * (t.ndim - 2))
        return jnp.moveaxis(t.reshape((B, n_blocks, Q_BLOCK) + t.shape[2:]), 1, 0)

    scale = MLA_QK ** -0.5
    k_pos = jnp.arange(L)

    def one_block(args):
        qn_b, qr_b, blk = args
        s = (jnp.einsum('bqhd,bkhd->bhqk', qn_b, k_nope, preferred_element_type=jnp.float32)
             + jnp.einsum('bqhr,bkr->bhqk', qr_b, k_rope, preferred_element_type=jnp.float32))
        q_pos = blk * Q_BLOCK + jnp.arange(Q_BLOCK)
        s = jnp.where(q_pos[:, None] >= k_pos[None, :], s * scale, -jnp.inf)
        p = jax.nn.softmax(s, axis=-1)
        return jnp.einsum('bhqk,bkhd->bqhd', p.astype(v.dtype), v)

    o = lax.map(one_block, (blocks(q_nope), blocks(q_rope), jnp.arange(n_blocks)))
    return jnp.moveaxis(o, 0, 1).reshape(B, n_blocks * Q_BLOCK, H, MLA_V)[:, :L]

def mla_mixer(h, w_in, q_latent_norm, w_q_up, w_out, k_nope, k_rope, v, cos, sin):
    B, L, _ = h.shape
    proj = h @ w_in
    c_q = rmsnorm_2(proj[..., :MLA_Q_RANK], q_latent_norm)
    z = proj[..., MLA_Q_RANK:]
    q = (c_q @ w_q_up).reshape(B, L, MLA_HEADS, MLA_QK)
    q_nope = q[..., :MLA_NOPE]
    q_rope = apply_rope(q[..., MLA_NOPE:], cos[:, None, :], sin[:, None, :])
    o = causal_block_attention(q_nope, q_rope, k_nope, k_rope, v).reshape(B, L, MLA_V_W)
    return (o * jax.nn.silu(z)) @ w_out

def second_inputs(seed: int = 0) -> dict:
    key = jax.random.key(seed)
    ks = jax.random.split(key, 20)
    nrm = lambda k, shape, s: jax.random.normal(k, shape, jnp.float32) * s
    gain = lambda k, shape: 1.0 + 0.02 * jax.random.normal(k, shape, jnp.float32)
    dt = jnp.exp(jax.random.uniform(ks[5], (N_A_LAYERS, GDN_V_HEADS), jnp.float32,
                                    math.log(1e-3), math.log(1e-1)))
    return {
        "x": nrm(ks[0], (BATCH, SEQ, D_MODEL), 1.0),
        "meta_tokens": nrm(ks[1], (N_META, D_MODEL), 1.0),
        "pre_norm": gain(ks[2], (DEPTH_2, D_MODEL)),
        "post_norm": gain(ks[3], (DEPTH_2, D_MODEL)),
        "gdn_w_in": nrm(ks[4], (N_A_LAYERS, D_MODEL, GDN_IN_W), D_MODEL ** -0.5),
        "gdn_conv_w": nrm(ks[6], (N_A_LAYERS, GDN_CONV, GDN_CONV_W), GDN_CONV ** -0.5),
        "gdn_a_log": jnp.log(jax.random.uniform(ks[7], (N_A_LAYERS, GDN_V_HEADS), jnp.float32, 1.0, 16.0)),
        "gdn_dt_bias": dt + jnp.log(-jnp.expm1(-dt)),
        "gdn_out_norm": gain(ks[8], (N_A_LAYERS, GDN_DV)),
        "gdn_w_out": nrm(ks[9], (N_A_LAYERS, GDN_V_W, D_MODEL), GDN_V_W ** -0.5),
        "kv_norm": gain(ks[10], (D_MODEL,)),
        "kv_w_down": nrm(ks[11], (D_MODEL, MLA_KV_RANK + MLA_ROPE), D_MODEL ** -0.5),
        "kv_latent_norm": gain(ks[12], (MLA_KV_RANK,)),
        "kv_w_up": nrm(ks[13], (MLA_KV_RANK, MLA_HEADS * (MLA_NOPE + MLA_V)), MLA_KV_RANK ** -0.5),
        "mla_w_in": nrm(ks[14], (N_B_LAYERS, D_MODEL, MLA_IN_W), D_MODEL ** -0.5),
        "mla_q_latent_norm": gain(ks[15], (N_B_LAYERS, MLA_Q_RANK)),
        "mla_w_q_up": nrm(ks[16], (N_B_LAYERS, MLA_Q_RANK, MLA_HEADS * MLA_QK), MLA_Q_RANK ** -0.5),
        "mla_w_out": nrm(ks[17], (N_B_LAYERS, MLA_V_W, D_MODEL), MLA_V_W ** -0.5),
    }

def second_block(x, meta_tokens, pre_norm, post_norm, gdn_w_in, gdn_conv_w, gdn_a_log, gdn_dt_bias,
              gdn_out_norm, gdn_w_out, kv_norm, kv_w_down, kv_latent_norm, kv_w_up,
              mla_w_in, mla_q_latent_norm, mla_w_q_up, mla_w_out):
    B = x.shape[0]
    meta = jnp.broadcast_to(meta_tokens[None].astype(x.dtype), (B, N_META, D_MODEL))
    h = jnp.concatenate([meta, x], axis=1)
    cos, sin = rope_tables(h.shape[1])
    shared_kv = None
    for layer in range(DEPTH_2):
        hn = rmsnorm_2(h, pre_norm[layer])
        if layer < N_A_LAYERS:
            y = gdn_mixer(hn, gdn_w_in[layer], gdn_conv_w[layer], gdn_a_log[layer], gdn_dt_bias[layer],
                          gdn_out_norm[layer], gdn_w_out[layer])
        else:
            if layer == N_A_LAYERS:
                shared_kv = mla_shared_kv(h, kv_norm, kv_w_down, kv_latent_norm, kv_w_up, cos, sin)
            j = layer - N_A_LAYERS
            k_nope, k_rope, v = shared_kv
            y = mla_mixer(hn, mla_w_in[j], mla_q_latent_norm[j], mla_w_q_up[j], mla_w_out[j],
                          k_nope, k_rope, v, cos, sin)
        h = h + rmsnorm_2(y, post_norm[layer])
    return h[:, N_META:]


def setup_inputs(seed=0):
    out = dict(first_inputs(seed))
    for name, value in second_inputs(seed + 1).items():
        if name != "x":
            out[name + "_2"] = value
    return out


def reference(
    x, g_pre_mix, w_in, w_pool_mix, pool_scale, w_br_pool, w_br_sb, w_gate, b_gate, w_out,
    g_post_mix, g_pre_mlp, w_up, w_down, g_post_mlp, meta_tokens_2, pre_norm_2, post_norm_2,
    gdn_w_in_2, gdn_conv_w_2, gdn_a_log_2, gdn_dt_bias_2, gdn_out_norm_2, gdn_w_out_2,
    kv_norm_2, kv_w_down_2, kv_latent_norm_2, kv_w_up_2, mla_w_in_2, mla_q_latent_norm_2,
    mla_w_q_up_2, mla_w_out_2,
):
    x = first_block(
        x, g_pre_mix, w_in, w_pool_mix, pool_scale, w_br_pool, w_br_sb, w_gate, b_gate, w_out,
        g_post_mix, g_pre_mlp, w_up, w_down, g_post_mlp,
    )
    return second_block(
        x, meta_tokens_2, pre_norm_2, post_norm_2, gdn_w_in_2, gdn_conv_w_2, gdn_a_log_2,
        gdn_dt_bias_2, gdn_out_norm_2, gdn_w_out_2, kv_norm_2, kv_w_down_2, kv_latent_norm_2,
        kv_w_up_2, mla_w_in_2, mla_q_latent_norm_2, mla_w_q_up_2, mla_w_out_2,
    )


_drawn_inputs = setup_inputs


def setup_inputs(seed=0):
    import zlib

    import numpy as np

    out = dict(_drawn_inputs(seed))
    spreads = {}
    factors = {'pool_scale': 3.732,
     'b_gate': 8.0,
     'g_post_mix': 3.021,
     'g_pre_mlp': 3.278,
     'g_post_mlp': 3.426,
     'pre_norm_2': 2.696,
     'post_norm_2': 3.822,
     'gdn_out_norm_2': 5.064,
     'kv_norm_2': 5.725,
     'kv_latent_norm_2': 5.904,
     'mla_q_latent_norm_2': 8.0}
    for name, (base, spread) in spreads.items():
        noise = np.random.default_rng([zlib.crc32(name.encode()), seed]).standard_normal(out[name].shape)
        drawn = base * np.exp(spread * noise) if base else spread * noise
        out[name] = __import__('jax').numpy.asarray(drawn.astype(out[name].dtype))
    for name, factor in factors.items():
        out[name] = (out[name] * factor).astype(out[name].dtype)
    return out
```

```python
import concourse.bass as bass
import numpy as np
from concourse import mybir
from contextlib import ExitStack

F32 = mybir.dt.float32
FR = mybir.dt.float32r
BF16 = mybir.dt.bfloat16
ALU = mybir.AluOpType
ACT = mybir.ActivationFunctionType
AX = mybir.AxisListType

P = 128
D = 1024
KT = D // P
SEQ, META = 512, 16
T = META + SEQ
HALF = T // 2
PW = KT * P
RING = 4
AHEAD = 2
NG = 4
HG = 4
CHUNKS = 5
BIG = 1.0e18

P_U = 0
P_PAIR = P_U + 4
P_GATE = P_PAIR + 16
P_BR = P_GATE + 12
P_OUT = P_BR + 8
P_FF = P_OUT + 8
P_GDN = P_FF + 64
P_KV = P_GDN + 64
P_MLA = P_KV + 5
PANELS = P_MLA + 48
STREAM = PANELS + AHEAD

NAMES = ("g_pre_mix", "pool_scale", "b_gate", "g_post_mix", "g_pre_mlp", "g_post_mlp",
         "pre_norm_0", "post_norm_0", "pre_norm_1", "post_norm_1", "kv_norm",
         "kv_latent_norm", "q_latent_norm", "out_norm", "eps", "inverse")
WIDTHS = (8, 4, 16, 8, 8, 8, 8, 8, 8, 8, 8, 1, 2, 1, 1, 16)
COL = {n: sum(WIDTHS[:i]) for i, n in enumerate(NAMES)}
NCOL = sum(WIDTHS)
(IDENT, TRI_U, NEG_TRI, NEG_ONES, ONES, MASK_SB, MASK_MLA, MEAN_D, MEAN_128, MEAN_256,
 LEVEL) = range(11)
LEVELS = 7
NMAT = LEVEL + LEVELS

STEPS = [(l, c) for l in range(1, LEVELS) for c in range(CHUNKS) if c or l < 4]
NS = len(STEPS)


def tokens(c):
    return (0, META) if c == 0 else (META + P * (c - 1), P)


def two(ap):
    return ap.rearrange("p (a b) -> p a b", a=2)


def build(nc, A, out):
    ctx = ExitStack()
    with ctx:
        def sb(name, cols, dt=F32):
            return ctx.enter_context(nc.sbuf_tensor(name, [P, cols], dt))

        raw = sb("raw", RING * PW)[:].rearrange("p (s n) -> p s n", s=RING)
        wsp = sb("wsp", RING * 2 * PW, FR)[:].rearrange("p (s h n) -> p s h n", s=RING, h=2)
        X = sb("x_res", KT * T)[:].rearrange("p (k t) -> p k t", k=KT)
        mats = sb("mats", NMAT * P)[:].rearrange("p (m n) -> p m n", m=NMAT)
        cols = sb("cols", NCOL)
        conv_w = sb("conv_w", NG * 32)
        rows_ab = sb("rows_ab", 32)
        rope = sb("rope", 2 * T)[:].rearrange("p (a t) -> p a t", a=2)
        small = sb("small", 768)
        with nc.sbuf_tensor("wp_s", [P, 1024], FR) as wpt:
            wp_s = wpt[:].rearrange("p (h n) -> p h n", h=2)
        qs_f = sb("qs_f", 1024)
        wba_s = sb("wba_s", 2 * 256, FR)[:].rearrange("p (h k n) -> p h k n", h=2, k=KT)
        ones_r = sb("ones_r", 2 * P, FR)[:].rearrange("p (m n) -> p m n", m=2)
        mats_b = sb("mats_b", 3 * P, BF16)[:].rearrange("p (m n) -> p m n", m=3)
        HS = sb("h_split", 2 * KT * T, FR)[:].rearrange("p (h k t) -> p h k t", h=2, k=KT)
        sm = sb("sm", 6 * CHUNKS * 16)[:].rearrange("p (a c n) -> p a c n", a=6, c=CHUNKS)
        smg = sb("smg", 6 * CHUNKS * HG)[:].rearrange("p (a c n) -> p a c n", a=6, c=CHUNKS)
        cwg = sb("cwg", 32)
        negb = sb("negb", 16)
        tiny = sb("tiny", 16)
        F = sb("work", 9408)
        with nc.sbuf_tensor("y_split", [P, 2 * KT * T], FR) as yt:
            Y = yt[:].rearrange("p (h k t) -> p h k t", h=2, k=KT)
        OV = sb("ov", 2 * KT * T)
        with nc.sbuf_tensor("aux", [P, 3200], FR) as AUX:
            pass
        AX2 = sb("aux_f", 3200)

        wp_raw = small[:, 0:512]
        wba_raw = small[:, 512:768]
        krope = small[:, 0:T]

        PS = ctx.enter_context(nc.psum_tensor("ps", [P, 8, 512], F32))

        def acc2(b):
            return PS[:, b:b + 2, 0:HALF]

        def norm_scratch(t, base, n):
            v = [t[:, base + i * T:base + i * T + n] for i in range(6)]
            return dict(sq=v[0:2], sum=v[2], rs=v[3], tmp=v[4:6])
        N1 = norm_scratch(F, 6208, SEQ)
        N2 = norm_scratch(OV, 0, T)
        N2r = norm_scratch(OV, 0, SEQ)

        gates = F[:, 0:8192].rearrange("p (m t) -> p m t", m=16)
        att = F[:, 2048:8192].rearrange("p (m t) -> p m t", t=SEQ)
        qf, kf, vf, vtf, ab0, ab1, sp0, sp1 = (att[:, i, :] for i in range(8))
        vt = vtf.rearrange("p (s c) -> p s c", s=4)
        aprob = F[:, 2048 + 8 * SEQ:2048 + 8 * SEQ + 1280]
        ABS, SPF = (ab0, ab1), (sp0, sp1)
        ge = (F[:, 8192:8704], F[:, 8704:9216])
        TRI_OFF = [0, 512, 896, 1152]
        sph = AUX[:, 0:1280]
        spl = AUX[:, 1280:2560]
        PADC = 16
        pa = F[:, 2048:2048 + PADC + SEQ]
        pb = F[:, 2600:2600 + PADC + SEQ]
        pool_r = F[:, 3200:3712]
        pc = F[:, 3800:3800 + PADC + SEQ]
        pool_c = (AUX[:, 0:512], AUX[:, 512:1024])
        mixf = F[:, 0:4096].rearrange("p (k t) -> p k t", k=KT)
        acc1 = F[:, 0:4096].rearrange("p (k t) -> p k t", k=KT)
        relu = (F[:, 4096:4608], F[:, 4608:5120])
        relu2 = (F[:, 5120:5632], F[:, 5632:6144])
        br_a = (AX2[:, 0:512], AX2[:, 512:1024])
        br_b = (AX2[:, 1024:1536], AX2[:, 1536:2048])

        accT = F[:, 0:KT * T].rearrange("p (k t) -> p k t", k=KT)
        QKV = F[:, KT * T:2 * KT * T].rearrange("p (k t) -> p k t", k=KT)
        xp = (OV[:, 0:3 + T], OV[:, 532:532 + 3 + T])
        cv = (OV[:, 1064:1064 + T], OV[:, 1592:1592 + T])
        ee = (OV[:, 2120:2120 + T], OV[:, 2648:2648 + T])
        l2s = (OV[:, 3176:3176 + T], OV[:, 3704:3704 + T])
        l2r = (OV[:, 4232:4232 + T], OV[:, 4760:4760 + T])

        def quad(t, at):
            return t[:, at:at + 512].rearrange("p (h n) -> p h n", h=HG)
        M = [quad(OV, 512 * c) for c in range(CHUNKS)]
        TN = [quad(OV, 2560 + 512 * c) for c in range(CHUNKS)]
        AT = [quad(OV, 5120 + 512 * c) for c in range(CHUNKS)]
        U = [quad(AX2, 512 * c) for c in range(CHUNKS)]
        S = quad(OV, 7680)
        E = quad(F, 8448)
        CL = (E, quad(AX2, 2560))
        QS = (quad(qs_f, 0), quad(qs_f, 512))
        VB, KD, R, VN, QD, SQO, RO = (quad(OV, 512 * i) for i in range(7))
        zz = (OV[:, 8448 - 2 * T:8448 - T], OV[:, 8448 - T:8448])

        KN = F[:, 4224:4224 + 4 * T].rearrange("p (h t) -> p h t", h=HG)
        QN = F[:, 6336:6336 + 4 * SEQ].rearrange("p (h t) -> p h t", h=HG)
        QR = F[:, 8384:8384 + 2 * SEQ].rearrange("p (h t) -> p h t", h=2)
        VT = OV[:, 4224:4224 + 5 * 512].rearrange("p (c n) -> p c n", c=CHUNKS)
        PR = (OV[:, 0:T], OV[:, T:2 * T])
        PT = tuple(OV[:, 1100 + 640 * i:1740 + 640 * i].rearrange("p (c n) -> p c n", c=CHUNKS)
                   for i in range(2))
        rt = (OV[:, 2400:2400 + T], OV[:, 2930:2930 + T])
        rk = (OV[:, 3600:3600 + T], OV[:, 5000:5000 + T])
        ckv = AUX[:, 0:2 * T].rearrange("p (h t) -> p h t", h=2)
        cq = AUX[:, 2 * T:2 * T + 4 * SEQ].rearrange("p (h k t) -> p h k t", h=2, k=2)
        ba_e = OV[:, 3200:3440].rearrange("p (a c n) -> p a c n", a=3, c=CHUNKS)
        al_e = OV[:, 3440:3456]
        zm = (OV[:, 7000:7512], OV[:, 7512:8024])

        sems = {}

        def sem(name):
            if name not in sems:
                sems[name] = ctx.enter_context(nc.semaphore(name))
            return sems[name]

        landed = [sem(f"landed{i}") for i in range(RING)]
        hi_ready = sem("hi_ready")
        lo_ready = sem("lo_ready")
        used = sem("panel_used")

        def mat(i, n=P):
            return mats[0:n, i, 0:n]

        def col(name, i=0, n=P):
            return cols[0:n, COL[name] + i:COL[name] + i + 1]

        def turn(p, i, length):
            return p if i is None else p + i * length

        def split_high(act, p, i=None, length=0):
            s = p % RING
            rounds = 16 * (p // RING + 1)
            act.wait_ge(landed[s], rounds if i is None else rounds + i * (16 * length // RING))
            if p >= RING:
                act.wait_ge(used, turn(p - RING + 1, i, length))
            act.activation(wsp[:, s, 0, :], raw[:, s, :], ACT.Copy).then_inc(hi_ready, 1)

        def split_low(pool, p, i=None, length=0):
            s = p % RING
            pool.wait_ge(hi_ready, turn(p + 1, i, length))
            pool.tensor_tensor(wsp[:, s, 1, :], raw[:, s, :], wsp[:, s, 0, :].bitcast(F32),
                               ALU.subtract).then_inc(lo_ready, 1)

        def mm3(pe, o, wh, wl, xh, xl, start, stop):
            pe.matmul(o, wh, xh, start=start, stop=False)
            pe.matmul(o, wh, xl, start=False, stop=False)
            return pe.matmul(o, wl, xh, start=False, stop=stop)

        def mm3t(pe, b, wh, wl, x, k, start, stop):
            for a in range(2):
                c = slice(a * HALF, (a + 1) * HALF)
                last = mm3(pe, PS[:, b + a, 0:HALF], wh, wl, x[:, 0, k, c], x[:, 1, k, c], start, stop)
            return last

        def panel(p, kt):
            s = p % RING
            c = slice(kt * P, (kt + 1) * P)
            return wsp[:, s, 0, c], wsp[:, s, 1, c]

        def tile_512(pe, p, b, x, i=None, length=0, x_ready=None, signal=True):
            pe.wait_ge(lo_ready, turn(p + 1, i, length))
            for kt in range(KT):
                if x_ready is not None:
                    pe.wait_ge(*split_ready(x_ready, kt + 1))
                last = mm3(pe, PS[:, b, :], *panel(p, kt), x[:, 0, kt, META:T], x[:, 1, kt, META:T],
                           kt == 0, kt == KT - 1)
            last.then_inc(used, 1)

        def tile_T(pe, p, b, x, i=None, length=0, x_ready=None):
            pe.wait_ge(lo_ready, turn(p + 1, i, length))
            for kt in range(KT):
                if x_ready is not None:
                    pe.wait_ge(*split_ready(x_ready, kt + 1))
                last = mm3t(pe, b, *panel(p, kt), x, kt, kt == 0, kt == KT - 1)
            last.then_inc(used, 1)

        NORMS = ["n1", "nA", "n2", "nB", "n3", "nC", "n4", "nD"]
        SPLITS = ["n1", "n2", "n3", "n4", "n5"]
        ADDS = ["nA", "nB", "nC", "nD"]

        def nth(tag, k, per=KT, among=NORMS):
            return per * among.index(tag) + k

        def split_ready(tag, k):
            return sem("norm_lo"), nth(tag, k, among=SPLITS)

        def added(tag, k):
            return sem("norm_added"), nth(tag, k, among=ADDS)

        def norm_squares(act, tag, src, N, ready=None):
            for kt in range(KT):
                if ready is not None:
                    act.wait_ge(*ready(kt))
                if kt >= 2:
                    act.wait_ge(sem("norm_sum"), nth(tag, max(1, kt - 2), KT - 1))
                act.activation(N["sq"][kt % 2], src(kt), ACT.Square).then_inc(sem("norm_sq"), 1)

        def norm_sum(dve, tag, N):
            for kt in range(1, KT):
                dve.wait_ge(sem("norm_sq"), nth(tag, kt + 1))
                if kt > 1:
                    dve.wait_ge(sem("norm_sum"), nth(tag, kt - 1, KT - 1))
                dve.tensor_tensor(N["sum"], N["sq"][0] if kt == 1 else N["sum"], N["sq"][kt % 2],
                                  ALU.add).then_inc(sem("norm_sum"), 1)

        def norm_mean(pe, tag, N, wide, b=4, m=MEAN_D):
            pe.wait_ge(sem("norm_sum"), nth(tag, KT - 1, KT - 1))
            if wide:
                pe.matmul(PS[:, b, 0:HALF], mat(m), N["sum"][:, 0:HALF], start=True, stop=True)
                last = pe.matmul(PS[:, b + 1, 0:HALF], mat(m), N["sum"][:, HALF:T], start=True, stop=True)
            else:
                last = pe.matmul(PS[:, b, :], mat(m), N["sum"], start=True, stop=True)
            last.then_inc(sem("norm_mean"), 1)

        def norm_rsqrt(act, tag, N, wide, b=4):
            act.wait_ge(sem("norm_mean"), nth(tag, 1, 1))
            src = acc2(b) if wide else PS[:, b, :]
            dst = two(N["rs"]) if wide else N["rs"]
            act.activation(dst, src, ACT.Ln, bias=col("eps")).then_inc(sem("norm_ln"), 1)
            act.wait_ge(sem("norm_ln"), nth(tag, 1, 1))
            act.activation(N["rs"], N["rs"], ACT.Exp, scale=-0.5).then_inc(sem("norm_rs"), 1)

        def norm_apply(dve, tag, src, gain, N, lo_at, need=None):
            dve.wait_ge(sem("norm_rs"), nth(need or tag, 1, 1))
            for kt in range(KT + 1):
                if kt < KT:
                    if kt >= 2:
                        dve.wait_ge(*split_ready(tag, kt - 1))
                    dve.scalar_tensor_tensor(out=N["tmp"][kt % 2], in0=src(kt), scalar=col(gain, kt),
                                             in1=N["rs"], op0=ALU.mult, op1=ALU.mult)\
                       .then_inc(sem("norm_scaled"), 1)
                if kt:
                    dve.wait_ge(sem("norm_hi"), nth(tag, kt, among=SPLITS))
                    dve.tensor_tensor(lo_at(1, kt - 1), N["tmp"][(kt - 1) % 2],
                                      lo_at(0, kt - 1).bitcast(F32), ALU.subtract)\
                       .then_inc(sem("norm_lo"), 1)

        def norm_high(act, tag, N, at):
            for kt in range(KT):
                act.wait_ge(sem("norm_scaled"), nth(tag, kt + 1, among=SPLITS))
                act.activation(at(0, kt), N["tmp"][kt % 2], ACT.Copy).then_inc(sem("norm_hi"), 1)

        def norm_add(dve, tag, src, gain, N, c):
            dve.wait_ge(sem("norm_rs"), nth(tag, 1, 1))
            for kt in range(KT):
                if kt >= 2:
                    dve.wait_ge(*added(tag, kt - 1))
                dve.scalar_tensor_tensor(out=N["tmp"][kt % 2], in0=src(kt), scalar=col(gain, kt),
                                         in1=N["rs"], op0=ALU.mult, op1=ALU.mult)\
                   .then_inc(sem("norm_branch"), 1)
                dve.wait_ge(sem("norm_branch"), nth(tag, kt + 1, among=ADDS))
                dve.tensor_tensor(X[:, kt, c], X[:, kt, c], N["tmp"][kt % 2], ALU.add)\
                   .then_inc(sem("norm_added"), 1)

        REAL, ALL = slice(META, T), slice(0, T)

        def hs(c):
            return lambda part, kt: HS[:, part, kt, c]

        def nth_conv(g, t):
            return gst(g, 12, 16 + t + 1)

        def nth_z(g, t):
            return gst(g, 12, 16 + 8 + t + 1)

        def nth_mz(g, t):
            return gst(g, 4, 16 + 48 + t + 1)

        def clamp(dve, count, buf):
            dve.wait_ge(sem("sig_exp"), count)
            dve.tensor_scalar(buf, buf, BIG, None, ALU.min).then_inc(sem("sig_min"), 1)

        def sigmoid(act, count, buf, out_ap):
            act.wait_ge(sem("sig_min"), count)
            act.activation(buf, buf, ACT.Ln, bias=1.0).then_inc(sem("sig_ln"), 1)
            act.wait_ge(sem("sig_ln"), count)
            act.activation(out_ap, buf, ACT.Exp, scale=-1.0).then_inc(sem("sigmoid"), 1)

        def carry_wait(pe, n):
            if n < P:
                pe.ldweights(mats_b[:, 0, :], tile_position=(0, 0))

        def gst(i, n, k):
            return i * n + k

        block = ctx.enter_context(nc.Block())

        @block.sync
        def _(sp):
            sp.dma_start(X[:, :, META:T], A["x"]).then_inc(sem("x_in"), 16)
            sp.dma_start(cols[:, :], A["cols"]).then_inc(sem("consts_in"), 16)
            sp.dma_start(mats, A["mats"]).then_inc(sem("consts_in"), 16)
            for p in range(RING):
                sp.dma_start(raw[:, p, :], A["w"][p]).then_inc(landed[p], 16)
            sp.dma_start(wp_raw, A["w_pool"]).then_inc(sem("small_in"), 16)
            sp.dma_start(wba_raw, A["w_ba"]).then_inc(sem("small_in"), 16)
            sp.dma_start(X[:, :, 0:META], A["meta"]).then_inc(sem("late_in"), 16)
            sp.dma_start(conv_w[:, :], A["conv"]).then_inc(sem("late_in"), 16)
            sp.dma_start(rows_ab[:, :], A["rows"]).then_inc(sem("late_in"), 16)
            sp.dma_start(rope, A["rope"]).then_inc(sem("late_in"), 16)
            rounds = STREAM // RING
            with sp.Fori(0, rounds - 1) as i:
                for s in range(RING):
                    sp.wait_ge(lo_ready, i * RING + s + 1)
                    sp.dma_start(raw[:, s, :], A["w"][bass.ds(i * RING + RING + s, 1)]
                                 .rearrange("a p n -> p (a n)")).then_inc(landed[s], 16)
            for p in range(rounds * RING, STREAM):
                sp.wait_ge(lo_ready, p - RING + 1)
                sp.dma_start(raw[:, p % RING, :], A["w"][p]).then_inc(landed[p % RING], 16)
            for k in range(KT):
                sp.wait_ge(*added("nD", k + 1))
                sp.dma_start(out[:, k, :], X[:, k, META:T]).then_inc(sem("stored"), 16)
            sp.wait_ge(sem("stored"), 16 * KT)

        @block.gpsimd
        def _(pool):
            for p in range(P_PAIR + AHEAD):
                split_low(pool, p)
            with pool.Fori(0, (P_GDN - P_PAIR) // RING) as i:
                for j in range(RING):
                    split_low(pool, P_PAIR + AHEAD + j, i, RING)
            with pool.Fori(0, NG) as g:
                for j in range(8):
                    split_low(pool, P_GDN + AHEAD + j, g, 16)
                for c in range(CHUNKS):
                    n = tokens(c)[1]
                    if c == 0:
                        pool.wait_ge(sem("g_at2"), gst(g, CHUNKS, CHUNKS))
                    if c >= 2:
                        pool.wait_ge(sem("g_t0"), gst(g, CHUNKS, c - 1))
                        pool.wait_ge(sem("g_u0ps"), gst(g, CHUNKS, c - 1))
                    pool.tensor_tensor(CL[c % 2][0:n, :, 0:n], M[c][0:n, :, 0:n],
                                       mats[0:n, LEVEL, 0:n].unsqueeze(1).to_broadcast([n, HG, n]),
                                       ALU.mult).then_inc(sem("g_c0"), 1)
                for s, (l, c) in enumerate(STEPS):
                    n = tokens(c)[1]
                    if s == 0:
                        pool.wait_ge(sem("g_u0ps"), gst(g, CHUNKS, CHUNKS))
                        pool.wait_ge(sem("g_t0"), gst(g, CHUNKS, CHUNKS))
                    if s >= 2:
                        pool.wait_ge(sem("g_q"), gst(g, NS, s - 1))
                    pool.tensor_tensor(CL[s % 2][0:n, :, 0:n], M[c][0:n, :, 0:n],
                                       mats[0:n, LEVEL + l, 0:n].unsqueeze(1).to_broadcast([n, HG, n]),
                                       ALU.mult).then_inc(sem("g_cl"), 1)
                for j in range(8, 16):
                    split_low(pool, P_GDN + AHEAD + j, g, 16)
            for p in range(P_KV + AHEAD, P_MLA + AHEAD):
                split_low(pool, p)
            with pool.Fori(0, NG) as g:
                for j in range(12):
                    split_low(pool, P_MLA + AHEAD + j, g, 12)

        @block.scalar
        def _(act):
            act.preload_act_table_set("natural_log_exp_and_others")
            act.wait_ge(sem("consts_in"), 32)
            act.activation(ones_r[:, 0, :], mats[:, NEG_TRI, :], ACT.Copy).then_inc(sem("const_act"), 1)
            act.activation(ones_r[:, 1, :], mats[:, NEG_ONES, :], ACT.Copy).then_inc(sem("const_act"), 1)
            act.activation(mats_b[:, 0, :], mats[:, IDENT, :], ACT.Copy).then_inc(sem("const_act"), 1)
            act.activation(mats_b[:, 1, :], mats[:, MASK_SB, :], ACT.Copy).then_inc(sem("const_act"), 1)
            act.activation(mats_b[:, 2, :], mats[:, MASK_MLA, :], ACT.Copy).then_inc(sem("const_act"), 1)
            act.wait_ge(sem("x_in"), 16)
            norm_squares(act, "n1", lambda k: X[:, k, REAL], N1)
            for p in range(AHEAD):
                split_high(act, p)
            act.wait_ge(sem("small_in"), 32)
            act.activation(wp_s[:, 0, :], wp_raw, ACT.Copy).then_inc(sem("wp_hi"), 1)
            act.activation(wba_s[:, 0, :, :], wba_raw.rearrange("p (k n) -> p k n", k=KT), ACT.Copy)\
               .then_inc(sem("wp_hi"), 1)
            norm_rsqrt(act, "n1", N1, False)
            norm_high(act, "n1", N1, hs(REAL))
            for g in range(4):
                split_high(act, P_U + g + AHEAD)
                act.wait_ge(used, P_U + g + 1)
                if g:
                    act.wait_ge(sem("pool_lo"), g)
                act.activation(pa[:, PADC:], PS[:, g % 2, :], ACT.Copy).then_inc(sem("proj_ev"), 1)
                act.wait_ge(sem("pooled"), g + 1)
                if g:
                    act.wait_ge(sem("pool_mm"), g)
                act.activation(pool_c[0], pool_r, ACT.Copy).then_inc(sem("pool_hi"), 1)
                act.wait_ge(sem("pool_scaled"), g + 1)
                act.activation(Y[:, 0, g, REAL], pool_r, ACT.Copy).then_inc(sem("pool_y"), 1)
            with act.Fori(0, 4) as i:
                for j, dst in enumerate((qf, kf, vf)):
                    split_high(act, P_PAIR + AHEAD + j, i, 4)
                    act.wait_ge(used, turn(P_PAIR + j + 1, i, 4))
                    if j == 0:
                        act.wait_ge(sem("pool_y_lo"), 4)
                    act.activation(dst, PS[:, j, :], ACT.Copy, scale=0.125 if j == 0 else 1.0)\
                       .then_inc(sem("proj_ev"), 1)
                split_high(act, P_PAIR + AHEAD + 3, i, 4)
                act.wait_ge(used, turn(P_PAIR + 4, i, 4))
                act.activation(ge[0], PS[:, 0, :], ACT.Exp, scale=-1.0, bias=negb[:, bass.ds(i, 1)])\
                   .then_inc(sem("sig_exp"), 1)
                sigmoid(act, i + 1, ge[0], gates[:, bass.ds(i, 1), :].rearrange("p a t -> p (a t)"))
                for j in range(2):
                    for k in range(4):
                        st = 3 - k
                        n = SEQ - P * st
                        z = PS[:, 4 + st, P * st:SEQ]
                        c8 = gst(i, 8, 4 * j + k + 1)
                        act.wait_ge(sem("z_ready"), c8)
                        if 4 * j + k >= 2:
                            act.wait_ge(sem("att_sp"), gst(i, 8, 4 * j + k - 1))
                        ab = ABS[k % 2][:, 0:n]
                        act.activation(ab, z, ACT.Abs).then_inc(sem("att_abs"), 1)
                        act.wait_ge(sem("att_abs"), c8)
                        act.activation(ab, ab, ACT.Exp, scale=-1.0).then_inc(sem("att_e"), 1)
                        act.wait_ge(sem("att_e"), c8)
                        act.activation(ab, ab, ACT.Ln, bias=1.0).then_inc(sem("att_ln"), 1)
                        act.wait_ge(sem("att_sp"), c8)
                        act.activation(sph[:, TRI_OFF[st]:TRI_OFF[st] + n], SPF[k % 2][:, 0:n], ACT.Copy)\
                           .then_inc(sem("att_hi"), 1)
                    for k in range(4):
                        st = 3 - k
                        act.wait_ge(sem("att_tri"), gst(i, 8, 4 * j + k + 1))
                        act.activation(aprob[:, TRI_OFF[st]:TRI_OFF[st] + SEQ - P * st],
                                       PS[:, 4 + st, P * st:SEQ], ACT.Exp).then_inc(sem("att_p"), 1)
                act.wait_ge(sem("att_pv"), gst(i, 2, 2))
                act.activation(Y[:, 0, bass.ds(4 + i, 1), REAL].rearrange("p a t -> p (a t)"),
                               PS[:, 3, :], ACT.Copy).then_inc(sem("o_hi"), 1)
            with act.Fori(0, 3) as i:
                for j in range(4):
                    b = j % 2
                    split_high(act, P_GATE + AHEAD + j, i, 4)
                    act.wait_ge(used, turn(P_GATE + j + 1, i, 4))
                    act.activation(ge[b], PS[:, b, :], ACT.Exp, scale=-1.0, bias=negb[:, bass.ds(4 + 4 * i + j, 1)])\
                       .then_inc(sem("sig_exp"), 1)
                    sigmoid(act, gst(i, 4, 4 + j + 1), ge[b],
                            gates[:, bass.ds(4 + 4 * i + j, 1), :].rearrange("p a t -> p (a t)"))
            with act.Fori(0, 2) as i:
                for j in range(4):
                    split_high(act, P_BR + AHEAD + j, i, 4)
                    act.wait_ge(sem("br_sum"), gst(i, 4, j + 1))
                    act.activation(HS[:, 0, bass.ds(4 * i + j, 1), REAL].rearrange("p a t -> p (a t)"),
                                   br_a[j % 2], ACT.Copy).then_inc(sem("br_hi"), 1)
            with act.Fori(0, 2) as i:
                for j in range(4):
                    split_high(act, P_OUT + AHEAD + j, i, 4)
            norm_squares(act, "nA", lambda k: mixf[:, k, :], N1, ready=lambda k: (sem("mix_ev"), 2 + k + 1))
            norm_rsqrt(act, "nA", N1, False)
            norm_squares(act, "n2", lambda k: X[:, k, REAL], N1, ready=lambda k: added("nA", k + 1))
            norm_rsqrt(act, "n2", N1, False)
            norm_high(act, "n2", N1, hs(REAL))
            with act.Fori(0, 4) as r:
                for m in range(8):
                    b = m % 2
                    c = gst(r, 8, m + 1)
                    split_high(act, P_FF + AHEAD + m, r, 16)
                    act.wait_ge(used, turn(P_FF + m + 1, r, 16))
                    if m >= 2:
                        act.wait_ge(sem("ff_sq"), gst(r, 8, m - 1))
                    act.activation(relu[b], PS[:, b, :], ACT.Relu).then_inc(sem("ff_relu"), 1)
                    act.wait_ge(sem("ff_relu"), c)
                    act.activation(Y[:, 0, m, REAL], relu[b], ACT.Square).then_inc(sem("ff_hi"), 1)
                for m in range(8):
                    split_high(act, P_FF + AHEAD + 8 + m, r, 16)
            norm_squares(act, "nB", lambda k: acc1[:, k, :], N1, ready=lambda k: (sem("ff_add"), 8 + 24 + k + 1))
            norm_rsqrt(act, "nB", N1, False)

            act.wait_ge(sem("late_in"), 64)
            norm_squares(act, "n3", lambda k: X[:, k, :], N2, ready=lambda k: added("nB", k + 1))
            norm_rsqrt(act, "n3", N2, True)
            norm_high(act, "n3", N2, hs(ALL))
            act.wait_ge(sem("ba_pe"), 1)
            act.activation(ba_e[:, 0, :, :], PS[:, 6, 0:160].rearrange("p (c n) -> p c n", c=CHUNKS)[:, :, 0:16],
                           ACT.Exp, scale=-1.0).then_inc(sem("ba_act"), 1)
            act.activation(al_e, rows_ab[:, 0:16], ACT.Exp).then_inc(sem("ba_act"), 1)
            act.wait_ge(sem("ba_dve"), 1)
            act.activation(ba_e[:, 2, :, :], ba_e[:, 1, :, :], ACT.Abs).then_inc(sem("ba_act"), 1)
            act.wait_ge(sem("ba_act"), 3)
            act.activation(ba_e[:, 2, :, :], ba_e[:, 2, :, :], ACT.Exp, scale=-1.0).then_inc(sem("ba_act"), 1)
            act.wait_ge(sem("ba_act"), 4)
            act.activation(ba_e[:, 2, :, :], ba_e[:, 2, :, :], ACT.Ln, bias=1.0).then_inc(sem("ba_act"), 1)
            act.wait_ge(sem("ba_pe"), 2)
            gcp = PS[:, 6, 0:160].rearrange("p (c a n) -> p c a n", c=CHUNKS, a=2)
            act.activation(sm[:, 2, :, :], gcp[:, :, 0, :], ACT.Copy).then_inc(sem("ba_act"), 1)
            act.activation(sm[:, 5, :, :], gcp[:, :, 1, :], ACT.Exp).then_inc(sem("ba_act"), 1)
            act.wait_ge(sem("ba_act"), 7)
            act.activation(sm[:, 3, :, :], sm[:, 2, :, :], ACT.Exp).then_inc(sem("ba_act"), 1)
            act.wait_ge(sem("ba_dve"), 7)
            act.activation(sm[:, 4, :, :], sm[:, 4, :, :], ACT.Exp).then_inc(sem("ba_act"), 1)

            with act.Fori(0, NG) as g:
                def lnexp(t):
                    sigmoid(act, nth_conv(g, t), ee[t % 2], ee[t % 2])
                for t in range(8):
                    split_high(act, P_GDN + AHEAD + t, g, 16)
                    act.wait_ge(used, turn(P_GDN + t + 1, g, 16))
                    if t >= 2:
                        act.wait_ge(sem("g_conv"), gst(g, 8, t - 1))
                    act.activation(two(xp[t % 2][:, 3:]), acc2(2 * (t % 2)), ACT.Copy)\
                       .then_inc(sem("g_xp"), 1)
                    if t:
                        lnexp(t - 1)
                    act.wait_ge(sem("g_conv"), gst(g, 8, t + 1))
                    if t >= 2:
                        act.wait_ge(sem("g_act"), gst(g, 8, t - 1))
                    act.activation(ee[t % 2], cv[t % 2], ACT.Exp, scale=-1.0).then_inc(sem("sig_exp"), 1)
                lnexp(7)
                for t in range(4):
                    c = gst(g, 4, t + 1)
                    act.wait_ge(sem("g_act"), gst(g, 8, 8 if t == 0 else 8))
                    if t >= 2:
                        act.wait_ge(sem("l2_ps"), gst(g, 4, t - 1))
                    act.activation(l2s[t % 2], QKV[:, t, :], ACT.Square).then_inc(sem("l2_sq"), 1)
                    act.wait_ge(sem("l2_ps"), c)
                    if t >= 2:
                        act.wait_ge(sem("l2_done"), gst(g, 4, t - 1))
                    act.activation(two(l2r[t % 2]), acc2(4 + 2 * (t % 2)), ACT.Ln, bias=col("eps"))\
                       .then_inc(sem("l2_ln"), 1)
                    act.wait_ge(sem("l2_ln"), c)
                    act.activation(l2r[t % 2], l2r[t % 2], ACT.Exp, scale=-0.5).then_inc(sem("l2_rs"), 1)
                for c in range(CHUNKS):
                    n = tokens(c)[1]
                    at = gst(g, CHUNKS, c + 1)
                    e = E[0:n, :, 0:n]
                    act.wait_ge(sem("g_d"), at)
                    act.activation(e, e, ACT.Abs).then_inc(sem("g_eabs"), 1)
                    act.wait_ge(sem("g_eabs"), at)
                    act.activation(e, e, ACT.Exp, scale=-1.0).then_inc(sem("g_e"), 1)
                for s, (l, c) in enumerate(STEPS):
                    n = tokens(c)[1]
                    act.wait_ge(sem("g_q"), gst(g, NS, s + 1))
                    if s >= 2:
                        act.wait_ge(sem("g_d2"), gst(g, NS, s - 1))
                    act.activation(QS[s % 2][0:n, :, 0:n],
                                   PS[0:n, s % 2, :].rearrange("p (h n) -> p h n", h=HG)[:, :, 0:n],
                                   ACT.Copy).then_inc(sem("g_qs"), 1)
                for c in range(CHUNKS):
                    o, n = tokens(c)
                    at = gst(g, CHUNKS, c + 1)

                    def bank(b, w=n):
                        return PS[:, b, :].rearrange("p (h n) -> p h n", h=HG)[:, :, 0:w]
                    act.wait_ge(sem("g_gr2"), at)
                    if c:
                        act.wait_ge(sem("g_o"), at - 1)
                    act.activation(QD[:, :, 0:n], bank(2), ACT.Exp).then_inc(sem("g_eg"), 1)
                    act.wait_ge(sem("g_vn"), at)
                    if c:
                        act.wait_ge(sem("g_su"), at - 1)
                    act.activation(VN[0:n, :, :], PS[0:n, 4, :].rearrange("p (h n) -> p h n", h=HG),
                                   ACT.Copy).then_inc(sem("g_vns"), 1)
                    act.wait_ge(sem("g_o"), at)
                    act.activation(SQO[:, :, 0:n], bank(5), ACT.Square).then_inc(sem("g_sqo"), 1)
                    act.wait_ge(sem("g_on"), at)
                    if c:
                        act.wait_ge(sem("g_store"), at - 1)
                    act.activation(RO[:, :, 0:n], bank(7), ACT.Ln, bias=col("eps")).then_inc(sem("g_oln"), 1)
                    act.wait_ge(sem("g_oln"), at)
                    act.activation(RO[:, :, 0:n], RO[:, :, 0:n], ACT.Exp, scale=-0.5)\
                       .then_inc(sem("g_ro"), 1)
                for t in range(4):
                    split_high(act, P_GDN + AHEAD + 8 + t, g, 16)
                    c = gst(g, 4, t + 1)
                    act.wait_ge(used, turn(P_GDN + 8 + t + 1, g, 16))
                    if t == 0:
                        act.wait_ge(sem("g_store"), gst(g, CHUNKS, CHUNKS))
                    if t >= 2:
                        act.wait_ge(sem("z_lo"), gst(g, 4, t - 1))
                    act.activation(two(zz[t % 2]), acc2(2 * (t % 2)), ACT.Exp, scale=-1.0)\
                       .then_inc(sem("sig_exp"), 1)
                    sigmoid(act, nth_z(g, t), zz[t % 2], zz[t % 2])
                    act.wait_ge(sem("z_y"), c)
                    act.activation(Y[:, 0, t, :], zz[t % 2], ACT.Copy).then_inc(sem("z_hi"), 1)
                for t in range(4):
                    split_high(act, P_GDN + AHEAD + 12 + t, g, 16)
            norm_squares(act, "nC", lambda k: accT[:, k, :], N2, ready=lambda k: (sem("g_add"), 8 * (NG + 1)))
            norm_rsqrt(act, "nC", N2, True)
            norm_squares(act, "n4", lambda k: X[:, k, :], N2, ready=lambda k: added("nC", k + 1))
            norm_rsqrt(act, "n4", N2, True)
            norm_high(act, "n4", N2, hs(ALL))
            split_high(act, P_KV + AHEAD)
            act.wait_ge(used, P_KV + 1)
            act.activation(two(N2["sq"][0]), acc2(0), ACT.Square).then_inc(sem("lat_act"), 1)
            act.wait_ge(sem("lat_pe"), 1)
            act.activation(two(rt[0]), acc2(6), ACT.Ln, bias=col("eps")).then_inc(sem("lat_act"), 1)
            act.wait_ge(sem("lat_act"), 2)
            act.activation(rt[0], rt[0], ACT.Exp, scale=-0.5).then_inc(sem("lat_act"), 1)
            act.wait_ge(sem("lat_dve"), 1)
            act.activation(ckv[:, 0, :], rt[1], ACT.Copy).then_inc(sem("lat_act"), 1)
            split_high(act, P_KV + AHEAD + 1)
            split_high(act, P_KV + AHEAD + 2)
            act.wait_ge(used, P_KV + 3)
            norm_high(act, "n5", N2, hs(ALL))
            for t in range(2):
                split_high(act, P_KV + AHEAD + 3 + t)
                act.wait_ge(used, P_KV + 3 + t + 1)
                act.activation(N2r["sq"][t], PS[:, t, :], ACT.Square).then_inc(sem("lat_act"), 1)
            act.wait_ge(sem("lat_pe"), 2)
            act.activation(N2r["rs"], PS[:, 4, :], ACT.Ln, bias=col("eps")).then_inc(sem("lat_act"), 1)
            act.wait_ge(sem("lat_act"), 7)
            act.activation(N2r["rs"], N2r["rs"], ACT.Exp, scale=-0.5).then_inc(sem("lat_act"), 1)
            for t in range(2):
                act.wait_ge(sem("lat_dve"), 6 + 2 * t)
                act.activation(cq[:, 0, t, :], N2r["tmp"][t], ACT.Copy).then_inc(sem("lat_act"), 1)

            SCALE = float(192 ** -0.5)
            with act.Fori(0, NG) as g:
                split_high(act, P_MLA + AHEAD, g, 12)
                act.wait_ge(sem("m_kn"), g + 1)
                for h in range(HG):
                    act.activation(two(KN[:, h, :]), acc2(2 * h), ACT.Copy).then_inc(sem("kn_ev"), 1)
                split_high(act, P_MLA + AHEAD + 1, g, 12)
                act.wait_ge(used, turn(P_MLA + 2, g, 12))
                for h in range(HG):
                    act.activation(QN[:, h, :], PS[:, (5 + h) % 8, :], ACT.Copy, scale=SCALE)\
                       .then_inc(sem("qn_ev"), 1)
                split_high(act, P_MLA + AHEAD + 2, g, 12)
                for u in range(18):
                    if u < 16:
                        b, i = u % 2, u % 4
                        act.wait_ge(sem("m_nmx"), gst(g, 16, u + 1))
                        if u >= 2:
                            act.wait_ge(sem("m_pt"), gst(g, 16, u - 1))
                        if i < 3:
                            s_ap = PS[:, 4 + 2 * b, 0:META + P * (i + 1)]
                            p_ap = PR[b][:, 0:META + P * (i + 1)]
                        else:
                            s_ap, p_ap = acc2(4 + 2 * b), two(PR[b])
                        act.activation(p_ap, s_ap, ACT.Exp, bias=tiny[:, b:b + 1],
                                       accum_out=tiny[:, 2 + b:3 + b]).then_inc(sem("m_p"), 1)
                    if 1 <= u <= 16:
                        v = u - 1
                        b = v % 2
                        act.wait_ge(sem("m_pt"), gst(g, 16, v + 1))
                        if v >= 2:
                            act.wait_ge(sem("m_o"), gst(g, 16, v - 1))
                        act.activation(PT[b][0:META, 0, :], PS[0:META, 1 + 2 * b, 0:P], ACT.Copy)\
                           .then_inc(sem("m_pt0"), 1)
                    if u >= 2:
                        v = u - 2
                        b, h, i = v % 2, v // 4, v % 4
                        act.wait_ge(sem("m_o"), gst(g, 16, v + 1))
                        act.activation(QN[:, h, P * i:P * i + P], PS[:, 1 + 2 * b, 256:256 + P], ACT.Copy)\
                           .then_inc(sem("m_oev"), 1)
                for t in range(4):
                    split_high(act, P_MLA + AHEAD + 3 + t, g, 12)
                    c = gst(g, 4, t + 1)
                    act.wait_ge(used, turn(P_MLA + 3 + t + 1, g, 12))
                    if t >= 2:
                        act.wait_ge(sem("z_lo"), gst(g, 4, 16 + t - 1))
                    act.activation(zm[t % 2], PS[:, t % 2, :], ACT.Exp, scale=-1.0).then_inc(sem("sig_exp"), 1)
                    sigmoid(act, nth_mz(g, t), zm[t % 2], zm[t % 2])
                    act.wait_ge(sem("z_y"), 16 + c)
                    act.activation(Y[:, 0, t, REAL], zm[t % 2], ACT.Copy).then_inc(sem("z_hi"), 1)
                for t in range(5):
                    split_high(act, P_MLA + AHEAD + 7 + t, g, 12)
            norm_squares(act, "nD", lambda k: accT[:, k, REAL], N2r, ready=lambda k: (sem("m_add"), 8 * (NG + 1)))
            norm_rsqrt(act, "nD", N2r, False)

        @block.vector
        def _(dve):
            def heads(ap, n, w):
                return ap.unsqueeze(2).to_broadcast([n, HG, w])

            def mat_h(i, n):
                return mats[0:n, i, 0:n].unsqueeze(1).to_broadcast([n, HG, n])

            def pairs(ap, n, w):
                return ap.unsqueeze(2).to_broadcast([n, 2, 2, w])

            def by_pair(ap):
                return ap.rearrange("p (a b) n -> p a b n", a=2)

            def bank(b, n, w, parts=HG):
                return PS[0:n, b, 0:parts * P].rearrange("p (h n) -> p h n", h=parts)[:, :, 0:w]

            dve.memset(tiny[:, 8:9], 0.0).then_inc(sem("br_free"), 2)
            dve.memset(tiny[:, 9:10], 0.0).then_inc(sem("mix_ev"), 2)
            norm_sum(dve, "n1", N1)
            dve.wait_ge(sem("consts_in"), 32)
            dve.tensor_scalar(negb[:, :], cols[:, COL["b_gate"]:COL["b_gate"] + 16], -1.0, None, ALU.mult)\
               .then_inc(sem("negb"), 1)
            dve.wait_ge(sem("wp_hi"), 2)
            dve.tensor_tensor(wp_s[:, 1, :], wp_raw, wp_s[:, 0, :].bitcast(F32), ALU.subtract)\
               .then_inc(sem("wp_lo"), 1)
            dve.tensor_tensor(wba_s[:, 1, :, :], wba_raw.rearrange("p (k n) -> p k n", k=KT),
                              wba_s[:, 0, :, :].bitcast(F32), ALU.subtract).then_inc(sem("wp_lo"), 1)
            norm_apply(dve, "n1", lambda k: X[:, k, REAL], "g_pre_mix", N1, hs(REAL))
            for r in (pa, pb, pc):
                dve.memset(r[:, 0:PADC], 0.0).then_inc(sem("pads"), 1)
            dve.wait_ge(sem("pads"), 3)
            steps = 0
            for g in range(4):
                dve.wait_ge(sem("proj_ev"), g + 1)
                src, w = pa, 1
                for k in range(g + 1):
                    dst = (pb, pc)[k % 2]
                    if k:
                        dve.wait_ge(sem("double"), steps)
                    dve.tensor_tensor(dst[:, PADC:], src[:, PADC:], src[:, PADC - w:PADC - w + SEQ], ALU.add)\
                       .then_inc(sem("double"), 1)
                    steps += 1
                    src, w = dst, 2 * w
                dve.wait_ge(sem("double"), steps)
                if g:
                    dve.wait_ge(sem("pool_y"), g)
                dve.scalar_tensor_tensor(out=pool_r, in0=src[:, PADC:], scalar=1.0 / w, in1=pa[:, PADC:],
                                         op0=ALU.mult, op1=ALU.subtract).then_inc(sem("pool_a"), 1)
                dve.wait_ge(sem("pool_a"), 2 * g + 1)
                dve.tensor_tensor(src[:, PADC:PADC + w], src[:, PADC:PADC + w],
                                  cols[:, COL["inverse"]:COL["inverse"] + w], ALU.mult)\
                   .then_inc(sem("pool_a"), 1)
                dve.wait_ge(sem("pool_a"), 2 * g + 2)
                dve.tensor_tensor(pool_r[:, 0:w], src[:, PADC:PADC + w], pa[:, PADC:PADC + w], ALU.subtract)\
                   .then_inc(sem("pooled"), 1)
                dve.wait_ge(sem("pool_hi"), g + 1)
                dve.tensor_tensor(pool_c[1], pool_r, pool_c[0].bitcast(F32), ALU.subtract)\
                   .then_inc(sem("pool_lo"), 1)
                dve.wait_ge(sem("pool_mm"), g + 1)
                dve.tensor_scalar(pool_r, PS[:, 2, :], col("pool_scale", g), None, ALU.mult)\
                   .then_inc(sem("pool_scaled"), 1)
                dve.wait_ge(sem("pool_y"), g + 1)
                dve.tensor_tensor(Y[:, 1, g, REAL], pool_r, Y[:, 0, g, REAL].bitcast(F32), ALU.subtract)\
                   .then_inc(sem("pool_y_lo"), 1)
            with dve.Fori(0, 4) as i:
                clamp(dve, i + 1, ge[0])
                dve.wait_ge(sem("vt_ps"), i + 1)
                dve.tensor_copy(vt, PS[:, 1, :].rearrange("p (s c) -> p s c", s=4)).then_inc(sem("vt_sb"), 1)
                for j in range(2):
                    for k in range(4):
                        st = 3 - k
                        n = SEQ - P * st
                        c8 = gst(i, 8, 4 * j + k + 1)
                        dve.wait_ge(sem("att_ln"), c8)
                        dve.scalar_tensor_tensor(out=SPF[k % 2][:, 0:n], in0=PS[:, 4 + st, P * st:SEQ],
                                                 scalar=0.0, in1=ABS[k % 2][:, 0:n], op0=ALU.max, op1=ALU.add)\
                           .then_inc(sem("att_sp"), 1)
                        dve.wait_ge(sem("att_hi"), c8)
                        o = TRI_OFF[st]
                        dve.tensor_tensor(spl[:, o:o + n], SPF[k % 2][:, 0:n], sph[:, o:o + n].bitcast(F32),
                                          ALU.subtract).then_inc(sem("att_lo"), 1)
                dve.wait_ge(sem("o_hi"), i + 1)
                dve.tensor_tensor(Y[:, 1, bass.ds(4 + i, 1), REAL].rearrange("p a t -> p (a t)"), PS[:, 3, :],
                                  Y[:, 0, bass.ds(4 + i, 1), REAL].rearrange("p a t -> p (a t)").bitcast(F32),
                                  ALU.subtract).then_inc(sem("o_lo"), 1)
            with dve.Fori(0, 3) as i:
                for j in range(4):
                    clamp(dve, gst(i, 4, 4 + j + 1), ge[j % 2])
            dve.wait_ge(sem("sigmoid"), 16)
            with dve.Fori(0, 2) as i:
                for j in range(4):
                    b, c = j % 2, gst(i, 4, j + 1)

                    def gate(at):
                        return gates[:, bass.ds(4 * i + j + at, 1), :].rearrange("p a t -> p (a t)")
                    dve.wait_ge(used, turn(P_BR + j + 1, i, 4))
                    dve.tensor_tensor(br_a[b], PS[:, 2 * b, :], gate(0), ALU.mult).then_inc(sem("br_t"), 1)
                    dve.tensor_tensor(br_b[b], PS[:, 2 * b + 1, :], gate(8), ALU.mult)\
                       .then_inc(sem("br_free"), 1)
                    dve.wait_ge(sem("br_t"), c)
                    dve.wait_ge(sem("br_free"), gst(i, 4, 2 + j + 1))
                    dve.tensor_tensor(br_a[b], br_a[b], br_b[b], ALU.add).then_inc(sem("br_sum"), 1)
                    dve.wait_ge(sem("br_hi"), c)

                    def at(part):
                        return HS[:, part, bass.ds(4 * i + j, 1), REAL].rearrange("p a t -> p (a t)")
                    dve.tensor_tensor(at(1), br_a[b], at(0).bitcast(F32), ALU.subtract)\
                       .then_inc(sem("br_lo"), 1)
            with dve.Fori(0, 2) as i:
                for j in range(4):
                    dve.wait_ge(used, turn(P_OUT + j + 1, i, 4))
                    dve.tensor_copy(mixf[:, bass.ds(4 * i + j, 1), :].rearrange("p a t -> p (a t)"),
                                    PS[:, j % 2, :]).then_inc(sem("mix_ev"), 1)
            norm_sum(dve, "nA", N1)
            norm_add(dve, "nA", lambda k: mixf[:, k, :], "g_post_mix", N1, REAL)
            norm_sum(dve, "n2", N1)
            norm_apply(dve, "n2", lambda k: X[:, k, REAL], "g_pre_mlp", N1, hs(REAL))
            for k in range(KT):
                dve.memset(acc1[:, k, :], 0.0).then_inc(sem("ff_add"), 1)
            with dve.Fori(0, 4) as r:
                for m in range(8):
                    b, c = m % 2, gst(r, 8, m + 1)
                    dve.wait_ge(sem("ff_relu"), c)
                    dve.tensor_tensor(relu2[b], relu[b], relu[b], ALU.mult).then_inc(sem("ff_sq"), 1)
                    dve.wait_ge(sem("ff_sq"), c)
                    dve.wait_ge(sem("ff_hi"), c)
                    dve.tensor_tensor(Y[:, 1, m, REAL], relu2[b], Y[:, 0, m, REAL].bitcast(F32), ALU.subtract)\
                       .then_inc(sem("ff_lo"), 1)
                for m in range(8):
                    dve.wait_ge(used, turn(P_FF + 8 + m + 1, r, 16))
                    dve.wait_ge(sem("ff_add"), gst(r, 8, m + 1))
                    dve.tensor_tensor(acc1[:, m, :], acc1[:, m, :], PS[:, m % 2, :], ALU.add)\
                       .then_inc(sem("ff_add"), 1)
            norm_sum(dve, "nB", N1)
            norm_add(dve, "nB", lambda k: acc1[:, k, :], "g_post_mlp", N1, REAL)

            norm_sum(dve, "n3", N2)
            dve.wait_ge(sem("late_in"), 64)
            norm_apply(dve, "n3", lambda k: X[:, k, :], "pre_norm_0", N2, hs(ALL))
            ba = PS[:, 6, 0:160].rearrange("p (c n) -> p c n", c=CHUNKS)
            dve.wait_ge(sem("ba_act"), 1)
            dt_row = rows_ab[:, 16:32].unsqueeze(1).to_broadcast([P, CHUNKS, 16])
            dve.tensor_tensor(ba_e[:, 1, :, :], ba[:, :, 16:32], dt_row, ALU.add).then_inc(sem("ba_dve"), 1)
            dve.tensor_scalar(ba_e[:, 0, :, :], ba_e[:, 0, :, :], 1.0, None, ALU.add).then_inc(sem("ba_dve"), 1)
            dve.wait_ge(sem("ba_dve"), 2)
            dve.reciprocal(sm[:, 0, :, :], ba_e[:, 0, :, :]).then_inc(sem("ba_dve"), 1)
            dve.wait_ge(sem("ba_act"), 5)
            dve.wait_ge(sem("ba_dve"), 1)
            dve.scalar_tensor_tensor(out=ba_e[:, 1, :, :], in0=ba_e[:, 1, :, :], scalar=0.0,
                                     in1=ba_e[:, 2, :, :], op0=ALU.max, op1=ALU.add).then_inc(sem("ba_dve"), 1)
            dve.wait_ge(sem("ba_dve"), 4)
            dve.wait_ge(sem("ba_act"), 2)
            dve.tensor_tensor(ba_e[:, 1, :, :], ba_e[:, 1, :, :],
                              al_e.unsqueeze(1).to_broadcast([P, CHUNKS, 16]), ALU.mult).then_inc(sem("ba_dve"), 1)
            dve.wait_ge(sem("ba_dve"), 5)
            dve.tensor_scalar(sm[:, 1, :, :], ba_e[:, 1, :, :], -1.0, None, ALU.mult).then_inc(sem("ba_dve"), 1)
            gcp = PS[:, 6, 0:160].rearrange("p (c a n) -> p c a n", c=CHUNKS, a=2)
            dve.wait_ge(sem("ba_act"), 7)
            dve.tensor_tensor(sm[:, 4, :, :], gcp[:, :, 1, :], sm[:, 2, :, :], ALU.subtract)\
               .then_inc(sem("ba_dve"), 1)
            dve.wait_ge(sem("ba_act"), 8)
            dve.tensor_tensor(sm[:, 3, :, :], sm[:, 3, :, :], sm[:, 0, :, :], ALU.mult).then_inc(sem("ba_dve"), 1)
            dve.wait_ge(sem("ba_dve"), 8)
            dve.wait_ge(sem("ba_act"), 9)
            for k in range(KT):
                dve.memset(accT[:, k, :], 0.0).then_inc(sem("g_add"), 1)

            with dve.Fori(0, NG) as g:
                dve.tensor_copy(smg[:, :, :, :].rearrange("p a c n -> p (a c) n"),
                                sm[:, :, :, bass.ds(4 * g, 4)].rearrange("p a c n -> p (a c) n"))\
                   .then_inc(sem("g_smg"), 1)
                dve.tensor_copy(cwg[:, :], conv_w[:, bass.ds(32 * g, 32)]).then_inc(sem("g_smg"), 1)
                dve.wait_ge(sem("g_smg"), gst(g, 2, 2))
                for b in range(2):
                    dve.memset(xp[b][:, 0:3], 0.0).then_inc(sem("xp_pad"), 1)
                dve.wait_ge(sem("xp_pad"), gst(g, 2, 2))

                def gated(t):
                    dve.wait_ge(sem("sigmoid"), nth_conv(g, t))
                    dve.tensor_tensor(QKV[:, t, :], cv[t % 2], ee[t % 2], ALU.mult).then_inc(sem("g_act"), 1)
                for t in range(8):
                    x, y = xp[t % 2], cv[t % 2]
                    if t >= 2:
                        dve.wait_ge(sem("g_act"), gst(g, 8, t - 1))
                    dve.wait_ge(sem("g_xp"), gst(g, 8, t + 1))
                    dve.tensor_scalar(y, x[:, 0:T], cwg[:, 4 * t:4 * t + 1], None, ALU.mult)\
                       .then_inc(sem("g_taps"), 1)
                    for k in range(1, 4):
                        dve.wait_ge(sem("g_taps"), gst(g, 24, 3 * t + k))
                        dve.scalar_tensor_tensor(out=y, in0=x[:, k:k + T], scalar=cwg[:, 4 * t + k:4 * t + k + 1],
                                                 in1=y, op0=ALU.mult, op1=ALU.add)\
                           .then_inc(sem("g_taps") if k < 3 else sem("g_conv"), 1)
                    if t:
                        gated(t - 1)
                    clamp(dve, nth_conv(g, t), ee[t % 2])
                gated(7)
                for t in range(4):
                    dve.wait_ge(sem("l2_rs"), gst(g, 4, t + 1))
                    dve.wait_ge(sem("g_act"), gst(g, 8, 8))
                    dve.scalar_tensor_tensor(out=QKV[:, t, :], in0=QKV[:, t, :],
                                             scalar=float(128 ** -0.5) if t < 2 else 1.0, in1=l2r[t % 2],
                                             op0=ALU.mult, op1=ALU.mult).then_inc(sem("l2_done"), 1)
                dve.memset(S, 0.0).then_inc(sem("g_s"), 1)
                for c in range(CHUNKS):
                    n = tokens(c)[1]
                    at = gst(g, CHUNKS, c + 1)
                    e = E[0:n, :, 0:n]
                    dve.wait_ge(sem("g_gr"), at)
                    if c:
                        dve.wait_ge(sem("g_at2"), at - 1)
                    dve.tensor_tensor(e, bank(4, n, n), heads(smg[0:n, 2, c, :], n, n), ALU.subtract)\
                       .then_inc(sem("g_d"), 1)
                    dve.wait_ge(sem("g_kk"), at)
                    dve.wait_ge(sem("g_e"), at)
                    kk = bank(5, n, n)
                    m, a = M[c][0:n, :, 0:n], AT[c][0:n, :, 0:n]
                    dve.tensor_tensor(by_pair(m), pairs(kk[:, 0:2, :], n, n), by_pair(e), ALU.mult)\
                       .then_inc(sem("g_m1"), 1)
                    dve.tensor_tensor(by_pair(a), pairs(kk[:, 2:4, :], n, n), by_pair(e), ALU.mult)\
                       .then_inc(sem("g_at"), 1)
                    dve.wait_ge(sem("g_m1"), at)
                    dve.tensor_tensor(m, m, heads(smg[0:n, 0, c, :], n, n), ALU.mult)
                    dve.wait_ge(sem("g_at"), at)
                    dve.tensor_tensor(a, a, mat_h(TRI_U, n), ALU.mult).then_inc(sem("g_at2"), 1)
                for c in range(CHUNKS):
                    n = tokens(c)[1]
                    at = gst(g, CHUNKS, c + 1)
                    dve.wait_ge(sem("g_c0"), at)
                    dve.tensor_tensor(TN[c][0:n, :, 0:n], mat_h(IDENT, n), CL[c % 2][0:n, :, 0:n], ALU.subtract)\
                       .then_inc(sem("g_t0"), 1)
                    dve.wait_ge(sem("g_u0ps"), at)
                    dve.tensor_tensor(U[c][0:n, :, 0:n], mat_h(IDENT, n), bank(6 + c % 2, n, n), ALU.subtract)\
                       .then_inc(sem("g_u0"), 1)
                prev = {}
                for s, (l, c) in enumerate(STEPS):
                    n = tokens(c)[1]
                    last = l == (3 if c == 0 else LEVELS - 1)
                    dve.wait_ge(sem("g_d2"), gst(g, NS, s + 1))
                    if c in prev:
                        dve.wait_ge(sem("g_u"), gst(g, NS, prev[c] + 1))
                    else:
                        dve.wait_ge(sem("g_u0"), gst(g, CHUNKS, CHUNKS))
                        dve.wait_ge(sem("g_t0"), gst(g, CHUNKS, CHUNKS))
                    prev[c] = s
                    u, t = U[c][0:n, :, 0:n], TN[c][0:n, :, 0:n]
                    op = dve.tensor_tensor(u, u, bank(2 + s % 2, n, n), ALU.subtract)
                    if not last:
                        op = dve.tensor_tensor(t, t, bank(4 + s % 2, n, n), ALU.subtract)
                    op.then_inc(sem("g_u"), 1)
                for c in range(CHUNKS):
                    o, n = tokens(c)
                    at = gst(g, CHUNKS, c + 1)
                    if c:
                        dve.wait_ge(sem("g_r"), at - 1)
                    dve.wait_ge(sem("g_kt"), at)
                    dve.tensor_tensor(VB[0:n, :, :], bank(1, n, P), heads(smg[0:n, 0, c, :], n, P), ALU.mult)\
                       .then_inc(sem("g_vb"), 1)
                    if c:
                        dve.wait_ge(sem("g_su"), at - 1)
                    for q in range(2):
                        dve.tensor_tensor(KD[0:n, 2 * q:2 * q + 2, :],
                                          PS[0:n, 0, q * P:(q + 1) * P].unsqueeze(1).to_broadcast([n, 2, P]),
                                          smg[0:n, 4, c, 2 * q:2 * q + 2].unsqueeze(2).to_broadcast([n, 2, P]),
                                          ALU.mult).then_inc(sem("g_kd"), 1)
                    dve.wait_ge(sem("g_eg"), at)
                    dve.tensor_tensor(by_pair(QD[:, :, 0:n]), by_pair(QD[:, :, 0:n]),
                                      pairs(QKV[:, 0:2, o:o + n], P, n), ALU.mult).then_inc(sem("g_qd"), 1)
                    dve.wait_ge(sem("g_ks"), at)
                    dve.tensor_tensor(R[0:n, :, :], bank(3, n, P), heads(smg[0:n, 3, c, :], n, P), ALU.mult)\
                       .then_inc(sem("g_r1"), 1)
                    dve.wait_ge(sem("g_r1"), at)
                    dve.wait_ge(sem("g_vb"), at)
                    dve.tensor_tensor(R[0:n, :, :], VB[0:n, :, :], R[0:n, :, :], ALU.subtract)\
                       .then_inc(sem("g_r"), 1)
                    dve.wait_ge(sem("g_su"), at)
                    dve.wait_ge(sem("g_s"), gst(g, CHUNKS + 1, c + 1))
                    dve.tensor_tensor(S, S, heads(smg[:, 5, c, :], P, P), ALU.mult).then_inc(sem("g_s1"), 1)
                    dve.wait_ge(sem("g_s1"), at)
                    dve.tensor_tensor(S, S, bank(6, P, P), ALU.add).then_inc(sem("g_s"), 1)
                    dve.wait_ge(sem("g_ro"), at)
                    dve.tensor_tensor(QKV[:, 4:8, o:o + n], bank(5, P, n), RO[:, :, 0:n], ALU.mult)\
                       .then_inc(sem("g_store"), 1)
                for t in range(4):
                    b, c = t % 2, gst(g, 4, t + 1)
                    clamp(dve, nth_z(g, t), zz[b])
                    dve.wait_ge(sem("sigmoid"), nth_z(g, t))
                    dve.tensor_tensor(two(zz[b]), acc2(2 * b), two(zz[b]), ALU.mult).then_inc(sem("z_silu"), 1)
                    dve.wait_ge(sem("z_silu"), c)
                    if t == 0:
                        dve.wait_ge(sem("g_store"), gst(g, CHUNKS, CHUNKS))
                    dve.scalar_tensor_tensor(out=zz[b], in0=QKV[:, 4 + t, :], scalar=col("out_norm"), in1=zz[b],
                                             op0=ALU.mult, op1=ALU.mult).then_inc(sem("z_y"), 1)
                    dve.wait_ge(sem("z_hi"), c)
                    dve.tensor_tensor(Y[:, 1, t, :], zz[b], Y[:, 0, t, :].bitcast(F32), ALU.subtract)\
                       .then_inc(sem("z_lo"), 1)
                for m in range(8):
                    if m % 2 == 0:
                        dve.wait_ge(used, turn(P_GDN + 12 + m // 2 + 1, g, 16))
                    dve.wait_ge(sem("g_add"), gst(g, 8, m + 1))
                    dve.tensor_tensor(two(accT[:, m, :]), two(accT[:, m, :]), acc2(2 * (m % 2)), ALU.add)\
                       .then_inc(sem("g_add"), 1)
            norm_sum(dve, "nC", N2)
            norm_add(dve, "nC", lambda k: accT[:, k, :], "post_norm_0", N2, ALL)
            norm_sum(dve, "n4", N2)
            norm_apply(dve, "n4", lambda k: X[:, k, :], "kv_norm", N2, hs(ALL))
            dve.wait_ge(sem("lat_act"), 3)
            dve.scalar_tensor_tensor(out=two(rt[1]), in0=acc2(0), scalar=col("kv_latent_norm"), in1=two(rt[0]),
                                     op0=ALU.mult, op1=ALU.mult).then_inc(sem("lat_dve"), 1)
            dve.wait_ge(sem("lat_act"), 4)
            dve.tensor_tensor(ckv[:, 1, :], rt[1], ckv[:, 0, :].bitcast(F32), ALU.subtract)\
               .then_inc(sem("lat_dve"), 1)
            dve.wait_ge(used, P_KV + 3)
            dve.tensor_tensor(two(rk[0]), acc2(2), two(rope[:, 0, :]), ALU.mult).then_inc(sem("lat_dve"), 1)
            dve.tensor_tensor(two(rk[1]), acc2(4), two(rope[:, 1, :]), ALU.mult).then_inc(sem("lat_dve"), 1)
            dve.wait_ge(sem("lat_dve"), 4)
            dve.tensor_tensor(krope, rk[0], rk[1], ALU.add).then_inc(sem("lat_dve"), 1)
            norm_apply(dve, "n5", lambda k: X[:, k, :], "pre_norm_1", N2, hs(ALL), need="n4")
            for t in range(2):
                dve.wait_ge(sem("lat_act"), 8)
                dve.scalar_tensor_tensor(out=N2r["tmp"][t], in0=PS[:, t, :], scalar=col("q_latent_norm", t),
                                         in1=N2r["rs"], op0=ALU.mult, op1=ALU.mult).then_inc(sem("lat_dve"), 1)
                dve.wait_ge(sem("lat_act"), 9 + t)
                dve.tensor_tensor(cq[:, 1, t, :], N2r["tmp"][t], cq[:, 0, t, :].bitcast(F32), ALU.subtract)\
                   .then_inc(sem("lat_dve"), 1)
            for k in range(KT):
                dve.memset(accT[:, k, :], 0.0).then_inc(sem("m_add"), 1)

            with dve.Fori(0, NG) as g:
                dve.wait_ge(used, turn(P_MLA + 1, g, 12))
                for c in range(CHUNKS):
                    n = tokens(c)[1]
                    dve.tensor_copy(VT[0:n, c, :], PS[0:n, c, :]).then_inc(sem("v_ev"), 1)
                dve.wait_ge(used, turn(P_MLA + 3, g, 12))
                for q in range(2):
                    if q:
                        dve.wait_ge(sem("qr_done"), gst(g, 2, 1))
                    dve.scalar_tensor_tensor(out=rt[0][:, 0:SEQ], in0=PS[:, 1 + q, :], scalar=float(192 ** -0.5),
                                             in1=rope[:, 0, META:T], op0=ALU.mult, op1=ALU.mult)\
                       .then_inc(sem("qr_t"), 1)
                    dve.scalar_tensor_tensor(out=rt[1][:, 0:SEQ], in0=PS[:, 3 + q, :], scalar=float(192 ** -0.5),
                                             in1=rope[:, 1, META:T], op0=ALU.mult, op1=ALU.mult)\
                       .then_inc(sem("qr_t"), 1)
                    dve.wait_ge(sem("qr_t"), gst(g, 4, 2 * q + 2))
                    dve.tensor_tensor(QR[:, q, :], rt[0][:, 0:SEQ], rt[1][:, 0:SEQ], ALU.add)\
                       .then_inc(sem("qr_done"), 1)
                for u in range(17):
                    if u < 16:
                        b, i, at = u % 2, u % 4, gst(g, 16, u + 1)
                        dve.wait_ge(sem("m_s"), at)
                        s_ap = PS[:, 4 + 2 * b, 0:META + P * (i + 1)] if i < 3 else acc2(4 + 2 * b)
                        dve.tensor_reduce(tiny[:, 4 + b:5 + b], s_ap, AX.X if i < 3 else AX.XY, ALU.max)\
                           .then_inc(sem("m_mx"), 1)
                        dve.wait_ge(sem("m_mx"), at)
                        dve.tensor_scalar(tiny[:, b:b + 1], tiny[:, 4 + b:5 + b], -1.0, None, ALU.mult)\
                           .then_inc(sem("m_nmx"), 1)
                        dve.wait_ge(sem("m_p"), at)
                        dve.reciprocal(tiny[:, 6 + b:7 + b], tiny[:, 2 + b:3 + b]).then_inc(sem("m_rd"), 1)
                        dve.wait_ge(sem("m_rd"), at)
                        w = META + P * (i + 1)
                        dve.tensor_scalar(PR[b][:, 0:w], PR[b][:, 0:w], tiny[:, 6 + b:7 + b], None, ALU.mult)\
                           .then_inc(sem("m_pn"), 1)
                    if u:
                        v = u - 1
                        b, i = v % 2, v % 4
                        dve.wait_ge(sem("m_pt"), gst(g, 16, v + 1))
                        if v >= 2:
                            dve.wait_ge(sem("m_o"), gst(g, 16, v - 1))
                        dve.tensor_copy(PT[b][:, 1:i + 2, :],
                                        PS[:, 2 * b, 0:P * (i + 1)].rearrange("p (c n) -> p c n", n=P))\
                           .then_inc(sem("m_pts"), 1)
                for t in range(4):
                    b, c = t % 2, gst(g, 4, t + 1)
                    clamp(dve, nth_mz(g, t), zm[b])
                    dve.wait_ge(sem("sigmoid"), nth_mz(g, t))
                    dve.tensor_tensor(zm[b], PS[:, b, :], zm[b], ALU.mult).then_inc(sem("z_silu"), 1)
                    dve.wait_ge(sem("z_silu"), 16 + c)
                    if t == 0:
                        dve.wait_ge(sem("m_oev"), gst(g, 16, 16))
                    dve.tensor_tensor(zm[b], QN[:, t, :], zm[b], ALU.mult).then_inc(sem("z_y"), 1)
                    dve.wait_ge(sem("z_hi"), 16 + c)
                    dve.tensor_tensor(Y[:, 1, t, REAL], zm[b], Y[:, 0, t, REAL].bitcast(F32), ALU.subtract)\
                       .then_inc(sem("z_lo"), 1)
                for m in range(8):
                    if m % 2 == 0:
                        dve.wait_ge(used, turn(P_MLA + 7 + m // 2 + 1, g, 12))
                    dve.wait_ge(sem("m_add"), gst(g, 8, m + 1))
                    dve.tensor_tensor(accT[:, m, REAL], accT[:, m, REAL], PS[:, m % 4, :], ALU.add)\
                       .then_inc(sem("m_add"), 1)
            norm_sum(dve, "nD", N2r)
            norm_add(dve, "nD", lambda k: accT[:, k, REAL], "post_norm_1", N2r, REAL)

        @block.tensor
        def _(pe):
            def quads(b, h, n, w):
                return PS[0:n, b, h * P:h * P + w]

            def pool_map(g):
                pe.wait_ge(sem("wp_lo"), 1)
                pe.wait_ge(sem("pool_lo"), g + 1)
                c = slice(g * P, (g + 1) * P)
                mm3(pe, PS[:, 2, :], wp_s[:, 0, c], wp_s[:, 1, c], pool_c[0], pool_c[1], True, True)\
                    .then_inc(sem("pool_mm"), 1)

            pe.wait_ge(sem("consts_in"), 32)
            norm_mean(pe, "n1", N1, False)
            for g in range(4):
                if g >= 2:
                    pe.wait_ge(sem("proj_ev"), g - 1)
                tile_512(pe, P_U + g, g % 2, HS, x_ready="n1" if g == 0 else None)
                if g:
                    pool_map(g - 1)
            pool_map(3)
            pe.wait_ge(sem("pool_scaled"), 4)
            pe.wait_ge(sem("proj_ev"), 4)
            pe.wait_ge(sem("const_act"), 5)
            with pe.Fori(0, 4) as i:
                for j in range(3):
                    tile_512(pe, P_PAIR + j, j, HS, i, 4)
                pe.wait_ge(sem("proj_ev"), gst(i, 3, 4 + 3))
                tile_512(pe, P_PAIR + 3, 0, HS, i, 4)
                for st in range(4):
                    last = pe.transpose(PS[:, 1, st * P:(st + 1) * P], vf[:, st * P:(st + 1) * P], mat(IDENT))
                last.then_inc(sem("vt_ps"), 1)

                def scores(j):
                    r = slice(64 * j, 64 * j + 64)
                    for k in range(4):
                        st = 3 - k
                        if j:
                            pe.wait_ge(sem("att_p"), gst(i, 8, k + 1))
                        pe.matmul(PS[:, 4 + st, P * st:SEQ], kf[r, st * P:(st + 1) * P], qf[r, P * st:SEQ],
                                  start=True, stop=True)
                        pe.matmul(PS[:, 4 + st, P * st:P * st + P], mats_b[:, 0, :], mats_b[:, 1, :],
                                  start=False, stop=True, skip_group_check=True).then_inc(sem("z_ready"), 1)

                def tails(j):
                    for k in range(4):
                        st = 3 - k
                        pe.wait_ge(sem("att_lo"), gst(i, 8, 4 * j + k + 1))
                        for part in (sph, spl):
                            for s2 in range(st, 4):
                                x = part[:, TRI_OFF[s2]:TRI_OFF[s2] + SEQ - P * s2]
                                last = pe.matmul(PS[:, 4 + st, P * s2:SEQ], ones_r[:, 0 if s2 == st else 1, :], x,
                                                 start=False, stop=True, skip_group_check=True)
                        last.then_inc(sem("att_tri"), 1)

                def values(j):
                    pe.wait_ge(sem("att_p"), gst(i, 8, 4 * j + 4))
                    pe.wait_ge(sem("vt_sb"), i + 1)
                    for st in range(4):
                        last = pe.matmul(PS[64 * j:64 * j + 64, 3, P * st:SEQ], vt[:, st, 64 * j:64 * j + 64],
                                         aprob[:, TRI_OFF[st]:TRI_OFF[st] + SEQ - P * st],
                                         start=st == 0, stop=st == 3, skip_group_check=True)
                    last.then_inc(sem("att_pv"), 1)
                scores(0)
                tails(0)
                scores(1)
                values(0)
                tails(1)
                values(1)
            with pe.Fori(0, 3) as i:
                for j in range(4):
                    pe.wait_ge(sem("sig_exp"), gst(i, 4, 4 + j - 1))
                    tile_512(pe, P_GATE + j, j % 2, HS, i, 4)
            pe.wait_ge(sem("sig_exp"), 16)
            pe.wait_ge(sem("pool_y_lo"), 4)
            pe.wait_ge(sem("o_lo"), 4)
            with pe.Fori(0, 2) as i:
                for j in range(4):
                    pe.wait_ge(lo_ready, turn(P_BR + j + 1, i, 4))
                    pe.wait_ge(sem("br_free"), gst(i, 4, j + 1))
                    for kt in range(KT):
                        last = mm3(pe, PS[:, 2 * (j % 2) + kt // 4, :], *panel(P_BR + j, kt),
                                   Y[:, 0, kt, REAL], Y[:, 1, kt, REAL], kt % 4 == 0, kt % 4 == 3)
                    last.then_inc(used, 1)
            pe.wait_ge(sem("br_lo"), 8)
            with pe.Fori(0, 2) as i:
                for j in range(4):
                    pe.wait_ge(sem("mix_ev"), gst(i, 4, j + 1))
                    tile_512(pe, P_OUT + j, j % 2, HS, i, 4)
            norm_mean(pe, "nA", N1, False)
            norm_mean(pe, "n2", N1, False)
            pe.wait_ge(*split_ready("n2", 8))
            with pe.Fori(0, 4) as r:
                for m in range(8):
                    if m >= 2:
                        pe.wait_ge(sem("ff_relu"), gst(r, 8, m - 1))
                    else:
                        pe.wait_ge(sem("ff_add"), gst(r, 8, m + 7))
                    tile_512(pe, P_FF + m, m % 2, HS, r, 16)
                pe.wait_ge(sem("ff_lo"), gst(r, 8, 8))
                for m in range(8):
                    if m >= 2:
                        pe.wait_ge(sem("ff_add"), gst(r, 8, 8 + m - 1))
                    tile_512(pe, P_FF + 8 + m, m % 2, Y, r, 16)
            norm_mean(pe, "nB", N1, False)

            norm_mean(pe, "n3", N2, True)
            pe.wait_ge(*split_ready("n3", 8))
            for c in range(CHUNKS):
                o = tokens(c)[0]
                for kt in range(KT):
                    last = mm3(pe, PS[:, 6, 32 * c:32 * c + 32], HS[:, 0, kt, o:o + P], HS[:, 1, kt, o:o + P],
                               wba_s[:, 0, kt, :], wba_s[:, 1, kt, :], kt == 0, kt == KT - 1)
            last.then_inc(sem("ba_pe"), 1)
            pe.wait_ge(sem("ba_dve"), 6)
            for c in range(CHUNKS):
                n = tokens(c)[1]
                pe.matmul(PS[:, 6, 32 * c:32 * c + 16], mats[0:n, TRI_U, :], sm[0:n, 1, c, :], start=True, stop=True)
                last = pe.matmul(PS[:, 6, 32 * c + 16:32 * c + 32], mats[0:n, ONES, :], sm[0:n, 1, c, :],
                                 start=True, stop=True)
            last.then_inc(sem("ba_pe"), 1)

            with pe.Fori(0, NG) as g:
                for t in range(8):
                    if t < 2:
                        pe.wait_ge(sem("g_add"), gst(g, 8, 8))
                    else:
                        pe.wait_ge(sem("g_xp"), gst(g, 8, t - 1))
                    tile_T(pe, P_GDN + t, 2 * (t % 2), HS, g, 16)
                for t in range(4):
                    pe.wait_ge(sem("l2_sq"), gst(g, 4, t + 1))
                    if t >= 2:
                        pe.wait_ge(sem("l2_ln"), gst(g, 4, t - 1))
                    for a in range(2):
                        last = pe.matmul(PS[:, 4 + 2 * (t % 2) + a, 0:HALF], mat(ONES),
                                         l2s[t % 2][:, a * HALF:(a + 1) * HALF], start=True, stop=True)
                    last.then_inc(sem("l2_ps"), 1)
                pe.wait_ge(sem("l2_done"), gst(g, 4, 4))
                pe.wait_ge(sem("g_smg"), gst(g, 2, 2))

                def decay_rows(b, c):
                    n = tokens(c)[1]
                    for h in range(HG):
                        last = pe.matmul(quads(b, h, P, n), smg[0:n, 1, c, h:h + 1].to_broadcast([n, P]),
                                         mat(TRI_U, n), start=True, stop=True)
                    return last
                for c in range(CHUNKS):
                    o, n = tokens(c)
                    at = gst(g, CHUNKS, c + 1)
                    if c:
                        pe.wait_ge(sem("g_d"), at - 1)
                    decay_rows(4, c).then_inc(sem("g_gr"), 1)
                    if c:
                        pe.wait_ge(sem("g_m1"), at - 1)
                        pe.wait_ge(sem("g_at"), at - 1)
                    for q in range(2):
                        k = QKV[:, 2 + q, o:o + n]
                        pe.matmul(quads(5, q, n, n), k, k, start=True, stop=True)
                        last = pe.matmul(quads(5, 2 + q, n, n), k, QKV[:, q, o:o + n], start=True, stop=True)
                    last.then_inc(sem("g_kk"), 1)
                for c in range(CHUNKS):
                    n = tokens(c)[1]
                    pe.wait_ge(sem("g_c0"), gst(g, CHUNKS, c + 1))
                    if c >= 2:
                        pe.wait_ge(sem("g_u0"), gst(g, CHUNKS, c - 1))
                    carry_wait(pe, n)
                    for h in range(HG):
                        last = pe.matmul(quads(6 + c % 2, h, n, n), CL[c % 2][0:n, h, 0:n], mat(IDENT, n),
                                         start=True, stop=True)
                    last.then_inc(sem("g_u0ps"), 1)
                last_of = {}

                def join(s):
                    l, c = STEPS[s]
                    n = tokens(c)[1]
                    b = s % 2
                    pe.wait_ge(sem("g_qs"), gst(g, NS, s + 1))
                    if s >= 2:
                        pe.wait_ge(sem("g_u"), gst(g, NS, s - 1))
                    carry_wait(pe, n)
                    for h in range(HG):
                        last = pe.matmul(quads(2 + b, h, n, n), TN[c][0:n, h, 0:n], QS[b][0:n, h, 0:n],
                                         start=True, stop=True)
                    if l != (3 if c == 0 else LEVELS - 1):
                        for h in range(HG):
                            last = pe.matmul(quads(4 + b, h, n, n), QS[b][0:n, h, 0:n], TN[c][0:n, h, 0:n],
                                             start=True, stop=True)
                    last.then_inc(sem("g_d2"), 1)
                for s, (l, c) in enumerate(STEPS):
                    n = tokens(c)[1]
                    pe.wait_ge(sem("g_cl"), gst(g, NS, s + 1))
                    if c in last_of:
                        pe.wait_ge(sem("g_u"), gst(g, NS, last_of[c] + 1))
                    else:
                        pe.wait_ge(sem("g_u0"), gst(g, CHUNKS, c + 1))
                    if s >= 2:
                        pe.wait_ge(sem("g_qs"), gst(g, NS, s - 1))
                    last_of[c] = s
                    carry_wait(pe, n)
                    for h in range(HG):
                        last = pe.matmul(quads(s % 2, h, n, n), CL[s % 2][0:n, h, 0:n], U[c][0:n, h, 0:n],
                                         start=True, stop=True)
                    last.then_inc(sem("g_q"), 1)
                    if s:
                        join(s - 1)
                join(NS - 1)
                pe.wait_ge(sem("g_u"), gst(g, NS, NS))

                def norm_o(c):
                    n = tokens(c)[1]
                    at = gst(g, CHUNKS, c + 1)
                    pe.wait_ge(sem("g_sqo"), at)
                    if c:
                        pe.wait_ge(sem("g_oln"), at - 1)
                    for h in range(HG):
                        last = pe.matmul(quads(7, h, P, n), mat(MEAN_128), SQO[:, h, 0:n], start=True, stop=True)
                    last.then_inc(sem("g_on"), 1)
                for c in range(CHUNKS):
                    o, n = tokens(c)
                    at = gst(g, CHUNKS, c + 1)
                    if c:
                        pe.wait_ge(sem("g_kd"), gst(g, 2 * CHUNKS, 2 * c))
                        pe.wait_ge(sem("g_vb"), at - 1)
                    for q in range(2):
                        pe.transpose(quads(0, q, n, P), QKV[:, 2 + q, o:o + n], mat(IDENT))
                    for h in range(HG):
                        last = pe.transpose(quads(1, h, n, P), QKV[:, 4 + h, o:o + n], mat(IDENT))
                    last.then_inc(sem("g_kt"), 1)
                    if c:
                        pe.wait_ge(sem("g_eg"), at - 1)
                    decay_rows(2, c).then_inc(sem("g_gr2"), 1)
                    pe.wait_ge(sem("g_s"), gst(g, CHUNKS + 1, c + 1))
                    if c:
                        pe.wait_ge(sem("g_r1"), at - 1)
                    for q in range(2):
                        last = pe.matmul(PS[0:n, 3, q * 256:(q + 1) * 256], QKV[:, 2 + q, o:o + n],
                                         S[:, 2 * q:2 * q + 2, :], start=True, stop=True)
                    last.then_inc(sem("g_ks"), 1)
                    if c:
                        norm_o(c - 1)
                    pe.wait_ge(sem("g_r"), at)
                    if c:
                        pe.wait_ge(sem("g_vns"), at - 1)
                    carry_wait(pe, n)
                    for h in range(HG):
                        last = pe.matmul(quads(4, h, n, P), U[c][0:n, h, 0:n], R[0:n, h, :], start=True, stop=True)
                    last.then_inc(sem("g_vn"), 1)
                    pe.wait_ge(sem("g_vns"), at)
                    pe.wait_ge(sem("g_qd"), at)
                    if c:
                        pe.wait_ge(sem("g_store"), at - 1)
                    for h in range(HG):
                        pe.matmul(quads(5, h, P, n), S[:, h, :], QD[:, h, 0:n], start=True, stop=False)
                        last = pe.matmul(quads(5, h, P, n), VN[0:n, h, :], AT[c][0:n, h, 0:n],
                                         start=False, stop=True)
                    last.then_inc(sem("g_o"), 1)
                    pe.wait_ge(sem("g_kd"), gst(g, 2 * CHUNKS, 2 * c + 2))
                    for h in range(HG):
                        last = pe.matmul(quads(6, h, P, P), KD[0:n, h, :], VN[0:n, h, :], start=True, stop=True)
                    last.then_inc(sem("g_su"), 1)
                norm_o(CHUNKS - 1)
                for t in range(4):
                    if t < 2:
                        pe.wait_ge(sem("g_store"), gst(g, CHUNKS, CHUNKS))
                    else:
                        pe.wait_ge(sem("z_silu"), gst(g, 4, t - 1))
                    tile_T(pe, P_GDN + 8 + t, 2 * (t % 2), HS, g, 16)
                pe.wait_ge(sem("z_lo"), gst(g, 4, 4))
                for t in range(4):
                    pe.wait_ge(lo_ready, turn(P_GDN + 12 + t + 1, g, 16))
                    for half in range(2):
                        m = 2 * t + half
                        if m >= 2:
                            pe.wait_ge(sem("g_add"), gst(g, 8, 8 + m - 1))
                        for kt in range(4):
                            last = mm3t(pe, 2 * half, *panel(P_GDN + 12 + t, 4 * half + kt), Y, kt,
                                        kt == 0, kt == 3)
                    last.then_inc(used, 1)
            norm_mean(pe, "nC", N2, True)
            norm_mean(pe, "n4", N2, True)
            tile_T(pe, P_KV, 0, HS, x_ready="n4")
            pe.wait_ge(sem("lat_act"), 1)
            for a in range(2):
                last = pe.matmul(PS[:, 6 + a, 0:HALF], mat(MEAN_128), N2["sq"][0][:, a * HALF:(a + 1) * HALF],
                                 start=True, stop=True)
            last.then_inc(sem("lat_pe"), 1)
            pe.wait_ge(sem("norm_rs"), nth("n4", 1, 1))
            for t in range(2):
                tile_T(pe, P_KV + 1 + t, 2 + 2 * t, HS)
            pe.wait_ge(sem("lat_dve"), 2)
            for t in range(2):
                tile_512(pe, P_KV + 3 + t, t, HS, x_ready="n5" if t == 0 else None)
            pe.wait_ge(sem("lat_act"), 6)
            pe.wait_ge(sem("lat_dve"), 5)
            for t in range(2):
                last = pe.matmul(PS[:, 4, :], mat(MEAN_256), N2r["sq"][t], start=t == 0, stop=t == 1)
            last.then_inc(sem("lat_pe"), 1)
            pe.wait_ge(sem("lat_dve"), 9)

            with pe.Fori(0, NG) as g:
                pe.wait_ge(sem("m_add"), gst(g, 8, 8))
                pe.wait_ge(lo_ready, turn(P_MLA + 1, g, 12))
                for h in range(HG):
                    for a in range(2):
                        c = slice(a * HALF, (a + 1) * HALF)
                        last = mm3(pe, PS[:, 2 * h + a, 0:HALF], *panel(P_MLA, h), ckv[:, 0, c], ckv[:, 1, c],
                                   True, True)
                last.then_inc(sem("m_kn"), 1)
                s = P_MLA % RING
                for c in range(CHUNKS):
                    o = tokens(c)[0]
                    pe.wait_ge(sem("kn_ev"), gst(g, 4, c // 2 + 1))
                    last = mm3(pe, PS[:, c, :], ckv[:, 0, o:o + P], ckv[:, 1, o:o + P],
                               wsp[:, s, 0, 512:1024], wsp[:, s, 1, 512:1024], True, True)
                last.then_inc(used, 1)
                for q in range(2):
                    pe.wait_ge(lo_ready, turn(P_MLA + 1 + q + 1, g, 12))
                    pe.wait_ge(sem("kn_ev"), gst(g, 4, 4))
                    if q:
                        pe.wait_ge(sem("v_ev"), gst(g, 5, 5))
                    for h in range(HG):
                        b = (5 + h) % 8 if q == 0 else 1 + h
                        if b == 0:
                            pe.wait_ge(sem("v_ev"), gst(g, 5, 1))
                        for kt in range(2):
                            last = mm3(pe, PS[:, b, :], *panel(P_MLA + 1 + q, 2 * h + kt),
                                       cq[:, 0, kt, :], cq[:, 1, kt, :], kt == 0, kt == 1)
                    last.then_inc(used, 1)
                pe.wait_ge(sem("qn_ev"), gst(g, 4, 4))
                pe.wait_ge(sem("qr_done"), gst(g, 2, 2))
                for u in range(18):
                    if u < 16:
                        h, i, b = u // 4, u % 4, u % 2
                        if u >= 2:
                            pe.wait_ge(sem("m_p"), gst(g, 16, u - 1))
                        o = META + P * i
                        qn, r = QN[:, h, P * i:P * i + P], slice(64 * (h % 2), 64 * (h % 2) + 64)
                        qr = QR[r, h // 2, P * i:P * i + P]
                        parts = [(4 + 2 * b, 0, o + P)] if i < 3 else \
                            [(4 + 2 * b, 0, HALF), (5 + 2 * b, HALF, T)]
                        for bank_, lo_, hi_ in parts:
                            w = hi_ - lo_
                            pe.matmul(PS[:, bank_, 0:w], qn, KN[:, h, lo_:hi_], start=True, stop=False)
                            last = pe.matmul(PS[:, bank_, 0:w], qr, krope[r, lo_:hi_], start=False, stop=True)
                            if hi_ == o + P:
                                last = pe.matmul(PS[:, bank_, w - P:w], mats_b[:, 0, :], mats_b[:, 2, :],
                                                 start=False, stop=True, skip_group_check=True)
                        last.then_inc(sem("m_s"), 1)
                    if 1 <= u <= 16:
                        v = u - 1
                        i, b = v % 4, v % 2
                        pe.wait_ge(sem("m_pn"), gst(g, 16, v + 1))
                        if v >= 2:
                            pe.wait_ge(sem("m_oev"), gst(g, 16, v - 1))
                            pe.wait_ge(sem("m_pts"), gst(g, 16, v - 1))
                        for c in range(i + 2):
                            o, n = tokens(c)
                            dst = PS[0:n, 1 + 2 * b, 0:P] if c == 0 else PS[:, 2 * b, (c - 1) * P:c * P]
                            last = pe.transpose(dst, PR[b][:, o:o + n], mat(IDENT))
                        last.then_inc(sem("m_pt"), 1)
                    if u >= 2:
                        v = u - 2
                        h, i, b = v // 4, v % 4, v % 2
                        pe.wait_ge(sem("m_pt0"), gst(g, 16, v + 1))
                        pe.wait_ge(sem("m_pts"), gst(g, 16, v + 1))
                        for c in range(i + 2):
                            n = tokens(c)[1]
                            last = pe.matmul(PS[:, 1 + 2 * b, 256:256 + P], VT[0:n, c, h * P:(h + 1) * P],
                                             PT[b][0:n, c, :], start=c == 0, stop=c == i + 1)
                        last.then_inc(sem("m_o"), 1)
                pe.wait_ge(sem("m_oev"), gst(g, 16, 16))
                for t in range(4):
                    if t >= 2:
                        pe.wait_ge(sem("z_silu"), gst(g, 4, 16 + t - 1))
                    tile_512(pe, P_MLA + 3 + t, t % 2, HS, g, 12)
                pe.wait_ge(sem("z_lo"), gst(g, 4, 16 + 4))
                for t in range(4):
                    pe.wait_ge(lo_ready, turn(P_MLA + 7 + t + 1, g, 12))
                    for half in range(2):
                        m = 2 * t + half
                        if m >= 4:
                            pe.wait_ge(sem("m_add"), gst(g, 8, 8 + m - 3))
                        for kt in range(4):
                            last = mm3(pe, PS[:, m % 4, :], *panel(P_MLA + 7 + t, 4 * half + kt),
                                       Y[:, 0, kt, REAL], Y[:, 1, kt, REAL], kt == 0, kt == 3)
                    last.then_inc(used, 1)
                pe.wait_ge(lo_ready, turn(P_MLA + 12, g, 12))
                pe.wait_ge(sem("m_add"), gst(g, 8, 8 + 8))
                pe.matmul(PS[:, 7, 0:2], panel(P_MLA + 11, 0)[0], cq[:, 0, 0, 0:2],
                          start=True, stop=True).then_inc(used, 1)
            norm_mean(pe, "nD", N2r, False)


def host_layout(inp):
    f = {k: np.asarray(v) for k, v in inp.items()}

    def feature_major(x):
        return np.ascontiguousarray(x.T.reshape(-1, P, x.shape[0]).transpose(1, 0, 2))

    def tiles(w):
        k, m = w.shape
        return w.reshape(k // P, P, m // P, P).transpose(2, 1, 0, 3)

    def whole(w):
        return tiles(w).reshape(-1, P, PW)

    def packed(w):
        t = tiles(w)
        per = KT // t.shape[2]
        t = t.reshape(t.shape[0] // per, per, P, t.shape[2], P).transpose(0, 2, 1, 3, 4)
        return t.reshape(-1, P, PW)

    out = []
    win = whole(f["w_in"])
    gate = whole(f["w_gate"])
    out.append(win[0:4])
    for i in range(4):
        out += [win[4 + i:5 + i], win[8 + i:9 + i], win[12 + i:13 + i], gate[i:i + 1]]
    out.append(gate[4:16])
    out.append(whole(np.concatenate([f["w_br_pool"], f["w_br_sb"]], axis=0)))
    out.append(whole(f["w_out"]))
    for r in range(4):
        out.append(whole(f["w_up"][:, 1024 * r:1024 * (r + 1)]))
        out.append(whole(f["w_down"][1024 * r:1024 * (r + 1)]))
    gin, gout = f["gdn_w_in_2"][0], f["gdn_w_out_2"][0]
    for g in range(NG):
        for a, n in ((256 * g, 256), (1024 + 256 * g, 256), (2048 + 512 * g, 512), (4096 + 512 * g, 512)):
            out.append(whole(gin[:, a:a + n]))
        out.append(packed(gout[512 * g:512 * (g + 1)]))
    down = f["kv_w_down_2"]
    x1, x2 = down[:, 128:160], down[:, 160:192]
    out.append(whole(np.concatenate([down[:, 0:128], x1, x2, x1, x2, x2, x1, x2, x1], axis=1)))
    win = f["mla_w_in_2"][0]
    out.append(whole(win[:, 0:256]))
    up = f["kv_w_up_2"].reshape(128, 16, 2, 128)
    qup = f["mla_w_q_up_2"][0].reshape(256, 16, 192)
    wo = f["mla_w_out_2"][0]
    for g in range(NG):
        h = slice(4 * g, 4 * g + 4)
        out.append(packed(np.concatenate([up[:, h, 0].reshape(128, 512), up[:, h, 1].reshape(128, 512)], axis=1)))
        out.append(packed(qup[:, h, 0:128].reshape(256, 512)))
        r = qup[:, h, 128:192]
        swapped = np.concatenate([r[:, :, 32:64], r[:, :, 0:32]], axis=2)
        out.append(packed(np.concatenate([r.reshape(256, 256), swapped.reshape(256, 256)], axis=1)))
        out.append(whole(win[:, 256 + 512 * g:256 + 512 * (g + 1)]))
        out.append(packed(wo[512 * g:512 * (g + 1)]))
        out.append(np.zeros((1, P, PW), np.float32))
    out.append(np.zeros((AHEAD, P, PW), np.float32))
    w = np.concatenate(out, axis=0)
    assert w.shape[0] == STREAM

    def column(v):
        return v.reshape(-1, P).T
    inv = (1.0 / np.arange(1, 17)).astype(np.float32)
    vec = [column(f["g_pre_mix"]), column(f["pool_scale"]), column(f["b_gate"]), column(f["g_post_mix"]),
           column(f["g_pre_mlp"]), column(f["g_post_mlp"]), column(f["pre_norm_2"][0]),
           column(f["post_norm_2"][0]), column(f["pre_norm_2"][1]), column(f["post_norm_2"][1]),
           column(f["kv_norm_2"]), column(f["kv_latent_norm_2"]), column(f["mla_q_latent_norm_2"][0]),
           column(f["gdn_out_norm_2"][0]), np.full((P, 1), 1e-6, np.float32), np.tile(inv, (P, 1))]
    conv = f["gdn_conv_w_2"][0].T.reshape(32, P, 4)
    order = [t for g in range(NG) for t in (2 * g, 2 * g + 1, 8 + 2 * g, 9 + 2 * g,
                                            16 + 4 * g, 17 + 4 * g, 18 + 4 * g, 19 + 4 * g)]
    conv = conv[order].transpose(1, 0, 2).reshape(P, NG * 32)
    rows = np.tile(np.concatenate([f["gdn_a_log_2"][0], f["gdn_dt_bias_2"][0]]), (P, 1))

    a, b = np.arange(P)[:, None], np.arange(P)[None, :]
    one = np.ones((P, P))
    mats = [a == b, a <= b, -1.0 * (a >= b), -one, one, np.where(a >= b, -1e30, 0.0),
            np.where(b > a, -1e30, 0.0), one / 1024, one / 128, one / 256]
    mats += [((a >> l) % 2 == 1) & ((b >> l) == (a >> l) - 1) for l in range(LEVELS)]
    mats = np.stack([np.asarray(m, np.float32) for m in mats], axis=1)
    freq = np.float32(10000.0) ** (-np.arange(0, 64, 2, dtype=np.float32) / np.float32(64))
    ang = np.arange(T, dtype=np.float32)[None, :] * freq[:, None]
    cos, sin = np.cos(ang), np.sin(ang)
    rope = np.stack([np.tile(cos, (4, 1)), np.tile(np.concatenate([-sin, sin]), (2, 1))], axis=1)

    arrays = {
        "x": feature_major(f["x"][0]), "meta": feature_major(f["meta_tokens_2"]), "w": w,
        "w_pool": f["w_pool_mix"].transpose(1, 0, 2).reshape(P, 512),
        "w_ba": gin[:, 6144:6176].reshape(KT, P, 32).transpose(1, 0, 2).reshape(P, 256),
        "cols": np.concatenate(vec, axis=1), "conv": conv, "rows": rows, "rope": rope, "mats": mats,
    }
    return {k: np.ascontiguousarray(v, dtype=np.float32) for k, v in arrays.items()}


def kernel(**inputs):
    from concourse import bacc
    from concourse.bass_utils import run_bass_kernel_spmd

    arrays = {f"in_{k}": v for k, v in host_layout(inputs).items()}
    nc = bacc.Bacc("TRN2", target_bir_lowering=False, num_devices=1)
    A = {k[3:]: nc.dram_tensor(k, v.shape, mybir.dt.from_np(v.dtype), kind="ExternalInput").ap()
         for k, v in arrays.items()}
    out = nc.dram_tensor("out", (P, KT, SEQ), F32, kind="ExternalOutput").ap()
    build(nc, A, out)
    r = run_bass_kernel_spmd(nc, [arrays], core_ids=[0])
    got = r.results[0]["out"]
    return np.ascontiguousarray(got.transpose(2, 1, 0).reshape(1, SEQ, D))
```

```python
import concourse.bass as bass
import numpy as np
from concourse import mybir
from contextlib import ExitStack

F32 = mybir.dt.float32
FR = mybir.dt.float32r
BF16 = mybir.dt.bfloat16
ALU = mybir.AluOpType
ACT = mybir.ActivationFunctionType
AX = mybir.AxisListType

P = 128
D = 1024
KT = D // P
SEQ, META = 512, 16
T = META + SEQ
HALF = T // 2
PW = KT * P
RING = 4
AHEAD = 2
NG = 4
HG = 4
QUERY_TILES = (0, 2, 1, 3)
CHUNKS = 5
LATER = CHUNKS - 1
BIG = 1.0e18

P_U = 0
P_PAIR = P_U + 4
P_GATE = P_PAIR + 16
P_BR = P_GATE + 12
P_OUT = P_BR + 8
P_FF = P_OUT + 8
P_GDN = P_FF + 64
P_KV = P_GDN + 64
P_MLA = P_KV + 5
PANELS = P_MLA + 48
STREAM = PANELS + AHEAD

NAMES = ("g_pre_mix", "pool_scale", "b_gate", "g_post_mix", "g_pre_mlp", "g_post_mlp",
         "pre_norm_0", "post_norm_0", "pre_norm_1", "post_norm_1", "kv_norm",
         "kv_latent_norm", "q_latent_norm", "out_norm", "eps", "inverse")
WIDTHS = (8, 4, 16, 8, 8, 8, 8, 8, 8, 8, 8, 1, 2, 1, 1, 16)
COL = {n: sum(WIDTHS[:i]) for i, n in enumerate(NAMES)}
NCOL = sum(WIDTHS)
(IDENT, TRI_U, NEG_TRI, NEG_ONES, ONES, MASK_SB, MASK_MLA, MEAN_D, MEAN_128, MEAN_256,
 LEVEL) = range(11)
LEVELS = 7
NMAT = LEVEL + LEVELS

STEPS = [(l, c) for l in range(1, LEVELS) for c in range(CHUNKS) if c or l < 4]
NS = len(STEPS)


def last_level(l, c):
    return l == (3 if c == 0 else LEVELS - 1)


TURNED = [s for s, (l, c) in enumerate(STEPS) if not last_level(l, c)]
NT = len(TURNED)


def tokens(c):
    return (0, META) if c == 0 else (META + P * (c - 1), P)


def two(ap):
    return ap.rearrange("p (a b) -> p a b", a=2)


def build(nc, A, out):
    ctx = ExitStack()
    with ctx:
        def sb(name, cols, dt=F32):
            return ctx.enter_context(nc.sbuf_tensor(name, [P, cols], dt))

        raw = sb("raw", RING * PW)[:].rearrange("p (s n) -> p s n", s=RING)
        wsp = sb("wsp", RING * 2 * PW, FR)[:].rearrange("p (s h n) -> p s h n", s=RING, h=2)
        X = sb("x_res", KT * T)[:].rearrange("p (k t) -> p k t", k=KT)
        mats = sb("mats", NMAT * P)[:].rearrange("p (m n) -> p m n", m=NMAT)
        cols = sb("cols", NCOL)
        conv_w = sb("conv_w", NG * 32)
        rows_ab = sb("rows_ab", 32)
        rope = sb("rope", 2 * T)[:].rearrange("p (a t) -> p a t", a=2)
        small = sb("small", 768)
        with nc.sbuf_tensor("wp_s", [P, 1024], FR) as wpt:
            wp_s = wpt[:].rearrange("p (h n) -> p h n", h=2)
        qs_f = sb("qs_f", 1024)
        wba_all = sb("wba_s", 2 * 256 + 96, FR)
        wba_s = wba_all[:, 0:512].rearrange("p (h k n) -> p h k n", h=2, k=KT)
        ones_r = sb("ones_r", 2 * P, FR)[:].rearrange("p (m n) -> p m n", m=2)
        mats_b = sb("mats_b", 3 * P, BF16)[:].rearrange("p (m n) -> p m n", m=3)
        HS = sb("h_split", 2 * KT * T, FR)[:].rearrange("p (h k t) -> p h k t", h=2, k=KT)
        sm = sb("sm", 6 * CHUNKS * 16)[:].rearrange("p (a c n) -> p a c n", a=6, c=CHUNKS)
        smg = sb("smg", 6 * CHUNKS * HG)[:].rearrange("p (a c n) -> p a c n", a=6, c=CHUNKS)
        cwg = sb("cwg", 32)
        negb = sb("negb", 16)
        tiny = sb("tiny", 16)
        F = sb("work", 9408)
        with nc.sbuf_tensor("y_split", [P, 2 * KT * T], FR) as yt:
            Y = yt[:].rearrange("p (h k t) -> p h k t", h=2, k=KT)
        OV = sb("ov", 2 * KT * T)
        with nc.sbuf_tensor("aux", [P, 3200], FR) as AUX:
            pass
        AX2 = sb("aux_f", 3200)

        wp_raw = small[:, 0:512]
        wba_raw = small[:, 512:768]
        krope = small[:, 0:T]

        PS = ctx.enter_context(nc.psum_tensor("ps", [P, 8, 512], F32))

        def acc2(b):
            return PS[:, b:b + 2, 0:HALF]

        def norm_scratch(t, base, n):
            v = [t[:, base + i * T:base + i * T + n] for i in range(6)]
            return dict(sq=v[0:2], sum=v[2], rs=v[3], tmp=v[4:6])
        N1 = norm_scratch(F, 6208, SEQ)
        N2 = norm_scratch(OV, 0, T)
        N2r = norm_scratch(OV, 0, SEQ)

        gates = F[:, 0:8192].rearrange("p (m t) -> p m t", m=16)
        att = F[:, 2048:8192].rearrange("p (m t) -> p m t", t=SEQ)
        qf, kf, vf, vtf, ab0, ab1, sp0, sp1 = (att[:, i, :] for i in range(8))
        vt = vtf.rearrange("p (s c) -> p s c", s=4)
        aprob = F[:, 2048 + 8 * SEQ:2048 + 8 * SEQ + 1280]
        ABS, SPF = (ab0, ab1), (sp0, sp1)
        ge = (F[:, 8192:8704], F[:, 8704:9216])
        TRI_OFF = [0, 512, 896, 1152]
        sph = AUX[:, 0:1280]
        spl = AUX[:, 1280:2560]
        PADC = 16
        pa, pb, pc = (F[:, 4096 + i * (PADC + SEQ):4096 + (i + 1) * (PADC + SEQ)] for i in range(3))
        pool_r = (F[:, 5680:5680 + SEQ], F[:, 8704:8704 + SEQ])
        POOL_BANKS = (0, 1, 2, 4)
        pool_c = tuple((AUX[:, i:i + 512], AUX[:, i + 512:i + 1024]) for i in (0, 1024))
        mixf = F[:, 0:4096].rearrange("p (k t) -> p k t", k=KT)
        acc1 = F[:, 0:4096].rearrange("p (k t) -> p k t", k=KT)
        relu = (F[:, 4096:4608], F[:, 4608:5120])
        relu2 = (F[:, 5120:5632], F[:, 5632:6144])
        br_a = (AX2[:, 0:512], AX2[:, 512:1024])
        br_b = (AX2[:, 1024:1536], AX2[:, 1536:2048])

        accT = F[:, 0:KT * T].rearrange("p (k t) -> p k t", k=KT)
        QKV = F[:, KT * T:2 * KT * T].rearrange("p (k t) -> p k t", k=KT)
        xp = (OV[:, 0:3 + T], OV[:, 532:532 + 3 + T])
        cv = (OV[:, 1064:1064 + T], OV[:, 1592:1592 + T])
        ee = (OV[:, 2120:2120 + T], OV[:, 2648:2648 + T])
        l2s = (OV[:, 3176:3176 + T], OV[:, 3704:3704 + T])
        l2r = (OV[:, 4232:4232 + T], OV[:, 4760:4760 + T])

        def quad(t, at):
            return t[:, at:at + 512].rearrange("p (h n) -> p h n", h=HG)
        M = [quad(OV, 512 * c) for c in range(CHUNKS)]
        TN = [quad(OV, 2560 + 512 * c) for c in range(CHUNKS)]
        AT = [quad(OV, 5120 + 512 * c) for c in range(CHUNKS)]
        U = [quad(AX2, 512 * c) for c in range(CHUNKS)]
        S = quad(OV, 7680)
        E = quad(F, 8448)
        CL = (E, quad(AX2, 2560))
        EE = (E, CL[1])
        QS = (quad(qs_f, 0), quad(qs_f, 512))
        C0 = QS
        VB, KD, R, VN, QD, SQO, RO = (quad(OV, 512 * i) for i in range(7))
        SD = quad(OV, 4112)
        zrow = (small[:, 0:T], qs_f[:, 0:T], F[:, 8448:8448 + T], AX2[:, 2560:2560 + T])
        zsig = OV[:, 3584:3584 + T]

        KN = F[:, 4224:4224 + 4 * T].rearrange("p (h t) -> p h t", h=HG)
        QN = F[:, 6336:6336 + 4 * SEQ].rearrange("p (h t) -> p h t", h=HG)
        QR = F[:, 8384:8384 + 2 * SEQ].rearrange("p (h t) -> p h t", h=2)
        VT = OV[:, 4224:4224 + 5 * 512].rearrange("p (c n) -> p c n", c=CHUNKS)
        PR = (OV[:, 0:T], OV[:, T:2 * T])
        PT = tuple(OV[:, 1100 + 640 * i:1740 + 640 * i].rearrange("p (c n) -> p c n", c=CHUNKS)
                   for i in range(2))
        rt = (OV[:, 2400:2400 + T], OV[:, 2930:2930 + T])
        rk = (OV[:, 3600:3600 + T], OV[:, 5000:5000 + T])
        ckv = AUX[:, 0:2 * T].rearrange("p (h t) -> p h t", h=2)
        cq = AUX[:, 2 * T:2 * T + 4 * SEQ].rearrange("p (h k t) -> p h k t", h=2, k=2)
        ba_e = OV[:, 3200:3440].rearrange("p (a c n) -> p a c n", a=3, c=CHUNKS)
        al_e = OV[:, 3440:3456]
        ba_f = OV[:, 3456:3456 + T]
        mz = tuple(OV[:, i:i + SEQ] for i in (7000, 7512, 3600, 2400))
        mzsig = OV[:, 2930:2930 + SEQ]

        sems = {}

        def sem(name):
            if name not in sems:
                sems[name] = ctx.enter_context(nc.semaphore(name))
            return sems[name]

        landed = [sem(f"landed{i}") for i in range(RING)]
        hi_ready = sem("hi_ready")
        lo_ready = sem("lo_ready")
        used = sem("panel_used")

        def mat(i, n=P):
            return mats[0:n, i, 0:n]

        def col(name, i=0, n=P):
            return cols[0:n, COL[name] + i:COL[name] + i + 1]

        def turn(p, i, length):
            return p if i is None else p + i * length

        def split_high(act, p, i=None, length=0):
            s = p % RING
            rounds = 16 * (p // RING + 1)
            act.wait_ge(landed[s], rounds if i is None else rounds + i * (16 * length // RING))
            if p >= RING:
                act.wait_ge(used, turn(p - RING + 1, i, length))
            act.activation(wsp[:, s, 0, :], raw[:, s, :], ACT.Copy).then_inc(hi_ready, 1)

        def split_low(pool, p, i=None, length=0):
            s = p % RING
            pool.wait_ge(hi_ready, turn(p + 1, i, length))
            pool.tensor_tensor(wsp[:, s, 1, :], raw[:, s, :], wsp[:, s, 0, :].bitcast(F32),
                               ALU.subtract).then_inc(lo_ready, 1)

        def mm3(pe, o, wh, wl, xh, xl, start, stop):
            pe.matmul(o, wh, xh, start=start, stop=False)
            pe.matmul(o, wh, xl, start=False, stop=False)
            return pe.matmul(o, wl, xh, start=False, stop=stop)

        def mm3t(pe, b, wh, wl, x, k, start, stop):
            for a in range(2):
                c = slice(a * HALF, (a + 1) * HALF)
                last = mm3(pe, PS[:, b + a, 0:HALF], wh, wl, x[:, 0, k, c], x[:, 1, k, c], start, stop)
            return last

        def panel(p, kt):
            s = p % RING
            c = slice(kt * P, (kt + 1) * P)
            return wsp[:, s, 0, c], wsp[:, s, 1, c]

        def tile_512(pe, p, b, x, i=None, length=0, x_ready=None, signal=True):
            pe.wait_ge(lo_ready, turn(p + 1, i, length))
            for kt in range(KT):
                if x_ready is not None:
                    pe.wait_ge(*split_ready(x_ready, kt + 1))
                last = mm3(pe, PS[:, b, :], *panel(p, kt), x[:, 0, kt, META:T], x[:, 1, kt, META:T],
                           kt == 0, kt == KT - 1)
            last.then_inc(used, 1)

        def tile_T(pe, p, b, x, i=None, length=0, x_ready=None):
            pe.wait_ge(lo_ready, turn(p + 1, i, length))
            for kt in range(KT):
                if x_ready is not None:
                    pe.wait_ge(*split_ready(x_ready, kt + 1))
                last = mm3t(pe, b, *panel(p, kt), x, kt, kt == 0, kt == KT - 1)
            last.then_inc(used, 1)

        NORMS = ["n1", "nA", "n2", "nB", "n3", "nC", "n4", "nD"]
        SPLITS = ["n1", "n2", "n3", "n4", "n5"]
        ADDS = ["nA", "nB", "nC", "nD"]
        ON_PE = ["n2", "n3", "n4"]
        ON_DVE = ["n1", "nA", "nB", "nC", "nD"]

        def nth(tag, k, per=KT, among=NORMS):
            return per * among.index(tag) + k

        def split_ready(tag, k):
            return sem("norm_lo"), nth(tag, k, among=SPLITS)

        def added(tag, k):
            return sem("norm_added_pool" if k % 2 else "norm_added"), nth(tag, k // 2 + 1, KT // 2, among=ADDS)

        def squares_read(tag, k):
            if tag in ON_PE:
                return sem("norm_acc"), nth(tag, k + 1, among=ON_PE)
            return sem("norm_sum"), nth(tag, max(1, k), KT - 1, among=ON_DVE)

        def norm_square(act, tag, src, N, kt, ready=None):
            if ready is not None:
                act.wait_ge(*ready(kt))
            if kt >= 2:
                act.wait_ge(*squares_read(tag, kt - 2))
            act.activation(N["sq"][kt % 2], src(kt), ACT.Square).then_inc(sem("norm_sq"), 1)

        def norm_squares(act, tag, src, N, ready=None):
            for kt in range(KT):
                norm_square(act, tag, src, N, kt, ready)

        def norm_sum_step(dve, tag, N, kt):
            dve.wait_ge(sem("norm_sq"), nth(tag, kt + 1))
            if kt > 1:
                dve.wait_ge(*squares_read(tag, kt - 1))
            dve.tensor_tensor(N["sum"], N["sq"][0] if kt == 1 else N["sum"], N["sq"][kt % 2],
                              ALU.add).then_inc(sem("norm_sum"), 1)

        def norm_sum(dve, tag, N):
            for kt in range(1, KT):
                norm_sum_step(dve, tag, N, kt)

        def norm_mean(pe, tag, N, wide, b=4, m=MEAN_D):
            if tag in ON_PE:
                for kt in range(KT):
                    pe.wait_ge(sem("norm_sq"), nth(tag, kt + 1))
                    for a in range(2 if wide else 1):
                        w = HALF if wide else SEQ
                        last = pe.matmul(PS[:, b + a, 0:w], mat(m), N["sq"][kt % 2][:, a * w:(a + 1) * w],
                                         start=kt == 0, stop=kt == KT - 1)
                    last.then_inc(sem("norm_acc"), 1)
                return
            pe.wait_ge(*squares_read(tag, KT - 1))
            if wide:
                pe.matmul(PS[:, b, 0:HALF], mat(m), N["sum"][:, 0:HALF], start=True, stop=True)
                last = pe.matmul(PS[:, b + 1, 0:HALF], mat(m), N["sum"][:, HALF:T], start=True, stop=True)
            else:
                last = pe.matmul(PS[:, b, :], mat(m), N["sum"], start=True, stop=True)
            last.then_inc(sem("norm_mean"), 1)

        def norm_rsqrt(act, tag, N, wide, b=4):
            if tag in ON_PE:
                act.wait_ge(*squares_read(tag, KT - 1))
            else:
                act.wait_ge(sem("norm_mean"), nth(tag, 1, 1, among=ON_DVE))
            src = acc2(b) if wide else PS[:, b, :]
            dst = two(N["rs"]) if wide else N["rs"]
            act.activation(dst, src, ACT.Ln, bias=col("eps")).then_inc(sem("norm_ln"), 1)
            act.wait_ge(sem("norm_ln"), nth(tag, 1, 1))
            act.activation(N["rs"], N["rs"], ACT.Exp, scale=-0.5).then_inc(sem("norm_rs"), 1)

        def norm_apply(dve, tag, src, gain, N, lo_at, need=None):
            dve.wait_ge(sem("norm_rs"), nth(need or tag, 1, 1))
            for kt in range(KT + 1):
                if kt < KT:
                    if kt >= 2:
                        dve.wait_ge(*split_ready(tag, kt - 1))
                    dve.scalar_tensor_tensor(out=N["tmp"][kt % 2], in0=src(kt), scalar=col(gain, kt),
                                             in1=N["rs"], op0=ALU.mult, op1=ALU.mult)\
                       .then_inc(sem("norm_scaled"), 1)
                if kt:
                    dve.wait_ge(sem("norm_hi"), nth(tag, kt, among=SPLITS))
                    dve.tensor_tensor(lo_at(1, kt - 1), N["tmp"][(kt - 1) % 2],
                                      lo_at(0, kt - 1).bitcast(F32), ALU.subtract)\
                       .then_inc(sem("norm_lo"), 1)

        def norm_high(act, tag, N, at):
            for kt in range(KT):
                act.wait_ge(sem("norm_scaled"), nth(tag, kt + 1, among=SPLITS))
                act.activation(at(0, kt), N["tmp"][kt % 2], ACT.Copy).then_inc(sem("norm_hi"), 1)

        def norm_add(dve, tag, src, gain, N, c):
            dve.wait_ge(sem("norm_rs"), nth(tag, 1, 1))
            for kt in range(KT):
                if kt >= 2:
                    dve.wait_ge(*added(tag, kt - 2))
                dve.scalar_tensor_tensor(out=N["tmp"][kt % 2], in0=src(kt), scalar=col(gain, kt),
                                         in1=N["rs"], op0=ALU.mult, op1=ALU.mult)\
                   .then_inc(sem("norm_branch"), 1)
                if kt % 2 == 0:
                    dve.wait_ge(sem("norm_branch"), nth(tag, kt + 1, among=ADDS))
                    dve.tensor_tensor(X[:, kt, c], X[:, kt, c], N["tmp"][0], ALU.add)\
                       .then_inc(sem("norm_added"), 1)
            dve.wait_ge(*added(tag, KT - 1))

        def norm_add_odd(pool, tag, N, c):
            for kt in range(1, KT, 2):
                pool.wait_ge(sem("norm_branch"), nth(tag, kt + 1, among=ADDS))
                pool.tensor_tensor(X[:, kt, c], X[:, kt, c], N["tmp"][1], ALU.add)\
                    .then_inc(sem("norm_added_pool"), 1)

        REAL, ALL = slice(META, T), slice(0, T)

        def hs(c):
            return lambda part, kt: HS[:, part, kt, c]

        def nth_conv(g, t):
            return gst(g, 12, 16 + t + 1)

        def nth_z(g, t):
            return gst(g, 12, 16 + 8 + t + 1)

        def nth_mz(g, t):
            return gst(g, 4, 16 + 48 + t + 1)

        def clamp(dve, count, buf):
            dve.wait_ge(sem("sig_exp"), count)
            dve.tensor_scalar(buf, buf, BIG, None, ALU.min).then_inc(sem("sig_min"), 1)

        def sigmoid(act, count, buf, out_ap):
            act.wait_ge(sem("sig_min"), count)
            act.activation(buf, buf, ACT.Ln, bias=1.0).then_inc(sem("sig_ln"), 1)
            act.wait_ge(sem("sig_ln"), count)
            act.activation(out_ap, buf, ACT.Exp, scale=-1.0).then_inc(sem("sigmoid"), 1)

        def carry_wait(pe, n):
            if n < P:
                pe.ldweights(mats_b[:, 0, :], tile_position=(0, 0))

        def joined(ap, l, odd):
            if len(ap.shape) == 2:
                return ap.rearrange("p (q two b) -> p q two b", two=2, b=2 ** l)[:, :, odd, :]
            return ap.rearrange("p h (q two b) -> p h q two b", two=2, b=2 ** l)[:, :, :, odd, :]

        def gst(i, n, k):
            return i * n + k

        block = ctx.enter_context(nc.Block())

        @block.sync
        def _(sp):
            for q in range(4):
                sp.dma_start(X[:, 2 * q:2 * q + 2, META:T], A["x"][:, 2 * q:2 * q + 2, :]).then_inc(sem(f"x_in{q}"), 16)
            sp.dma_start(cols[:, :], A["cols"]).then_inc(sem("consts_in"), 16)
            sp.dma_start(mats, A["mats"]).then_inc(sem("consts_in"), 16)
            for p in range(RING):
                sp.dma_start(raw[:, p, :], A["w"][p]).then_inc(landed[p], 16)
            sp.dma_start(wp_raw, A["w_pool"]).then_inc(sem("small_in"), 16)
            sp.dma_start(wba_raw, A["w_ba"]).then_inc(sem("small_in"), 16)
            sp.dma_start(X[:, :, 0:META], A["meta"]).then_inc(sem("late_in"), 16)
            sp.dma_start(conv_w[:, :], A["conv"]).then_inc(sem("late_in"), 16)
            sp.dma_start(rows_ab[:, :], A["rows"]).then_inc(sem("late_in"), 16)
            sp.dma_start(rope, A["rope"]).then_inc(sem("late_in"), 16)
            rounds = STREAM // RING
            with sp.Fori(0, rounds - 1) as i:
                for s in range(RING):
                    sp.wait_ge(lo_ready, i * RING + s + 1)
                    sp.dma_start(raw[:, s, :], A["w"][bass.ds(i * RING + RING + s, 1)]
                                 .rearrange("a p n -> p (a n)")).then_inc(landed[s], 16)
            for p in range(rounds * RING, STREAM):
                sp.wait_ge(lo_ready, p - RING + 1)
                sp.dma_start(raw[:, p % RING, :], A["w"][p]).then_inc(landed[p % RING], 16)
            for k in range(KT):
                sp.wait_ge(*added("nD", k))
                sp.dma_start(out[:, k, :], X[:, k, META:T]).then_inc(sem("stored"), 16)
            sp.wait_ge(sem("stored"), 16 * KT)

        @block.gpsimd
        def _(pool):
            for p in range(P_PAIR + AHEAD):
                split_low(pool, p)
            with pool.Fori(0, (P_FF - P_PAIR) // RING) as i:
                for j in range(RING):
                    split_low(pool, P_PAIR + AHEAD + j, i, RING)
            norm_add_odd(pool, "nA", N1, REAL)
            pool.memset(F[:, 0:KT * SEQ], 0.0).then_inc(sem("acc_zero"), 1)
            with pool.Fori(0, (P_GDN - P_FF) // RING) as i:
                for j in range(RING):
                    split_low(pool, P_FF + AHEAD + j, i, RING)
            norm_add_odd(pool, "nB", N1, REAL)
            pool.memset(F[:, 0:KT * T], 0.0).then_inc(sem("acc_zero"), 1)
            with pool.Fori(0, NG) as g:
                for j in range(8):
                    split_low(pool, P_GDN + AHEAD + j, g, 16)
                for c in range(CHUNKS):
                    n = tokens(c)[1]
                    at = gst(g, CHUNKS, c + 1)
                    m = M[c][0:n, :, 0:n]
                    pool.wait_ge(sem("g_m1"), at)
                    pool.tensor_tensor(m, m, smg[0:n, 0, c, :].unsqueeze(2).to_broadcast([n, HG, n]), ALU.mult)\
                        .then_inc(sem("g_m2"), 1)
                    pool.wait_ge(sem("g_m2"), at)
                    if c >= 2:
                        pool.wait_ge(sem("g_t0"), at - 2)
                    pool.tensor_tensor(C0[c % 2][0:n, :, 0:n], m,
                                       mats[0:n, LEVEL, 0:n].unsqueeze(1).to_broadcast([n, HG, n]),
                                       ALU.mult).then_inc(sem("g_c0"), 1)
                for s, (l, c) in enumerate(STEPS):
                    n = tokens(c)[1]
                    if s == 0:
                        pool.wait_ge(sem("g_at"), gst(g, CHUNKS, CHUNKS))
                    if s >= 2:
                        pool.wait_ge(sem("g_q"), gst(g, NS, s - 1))
                    pool.tensor_tensor(CL[s % 2][0:n, :, 0:n], M[c][0:n, :, 0:n],
                                       mats[0:n, LEVEL + l, 0:n].unsqueeze(1).to_broadcast([n, HG, n]),
                                       ALU.mult).then_inc(sem("g_cl"), 1)
                for j in range(8, 16):
                    split_low(pool, P_GDN + AHEAD + j, g, 16)
            norm_add_odd(pool, "nC", N2, ALL)
            pool.memset(F[:, 0:KT * T], 0.0).then_inc(sem("acc_zero"), 1)
            for p in range(P_KV + AHEAD, P_MLA + AHEAD):
                split_low(pool, p)
            with pool.Fori(0, NG) as g:
                for j in range(12):
                    split_low(pool, P_MLA + AHEAD + j, g, 12)
            norm_add_odd(pool, "nD", N2r, REAL)

        @block.scalar
        def _(act):
            act.preload_act_table_set("natural_log_exp_and_others")
            norm_squares(act, "n1", lambda k: X[:, k, REAL], N1, ready=lambda k: (sem(f"x_in{k // 2}"), 16))
            act.wait_ge(sem("consts_in"), 32)
            act.activation(ones_r[:, 0, :], mats[:, NEG_TRI, :], ACT.Copy).then_inc(sem("const_act"), 1)
            act.activation(ones_r[:, 1, :], mats[:, NEG_ONES, :], ACT.Copy).then_inc(sem("const_act"), 1)
            act.activation(mats_b[:, 0, :], mats[:, IDENT, :], ACT.Copy).then_inc(sem("const_act"), 1)
            act.activation(mats_b[:, 1, :], mats[:, MASK_SB, :], ACT.Copy).then_inc(sem("const_act"), 1)
            act.activation(mats_b[:, 2, :], mats[:, MASK_MLA, :], ACT.Copy).then_inc(sem("const_act"), 1)
            for p in range(AHEAD):
                split_high(act, p)
            norm_rsqrt(act, "n1", N1, False)
            norm_high(act, "n1", N1, hs(REAL))
            act.wait_ge(sem("small_in"), 32)
            act.activation(wp_s[:, 0, :], wp_raw, ACT.Copy).then_inc(sem("wp_hi"), 1)
            act.activation(wba_s[:, 0, :, :], wba_raw.rearrange("p (k n) -> p k n", k=KT), ACT.Copy)\
               .then_inc(sem("wp_hi"), 1)
            act.activation(wba_all[:, 512:608], mats[:, ONES, 0:96], ACT.Copy).then_inc(sem("wp_hi"), 1)
            for g in range(2):
                split_high(act, P_U + g + AHEAD)

            def pool_front(g):
                act.wait_ge(used, P_U + g + 1)
                if g:
                    act.wait_ge(sem("pool_lo"), g)
                act.activation(pa[:, PADC:], PS[:, POOL_BANKS[g], :], ACT.Copy).then_inc(sem("proj_ev"), 1)
                split_high(act, P_PAIR + g)
                act.wait_ge(sem("pooled"), g + 1)
                if g >= 2:
                    act.wait_ge(sem("pool_mm"), g - 1)
                act.activation(pool_c[g % 2][0], pool_r[g % 2], ACT.Copy).then_inc(sem("pool_hi"), 1)

            def pool_back(g):
                act.wait_ge(sem("pool_scaled"), g + 1)
                act.activation(Y[:, 0, g, REAL], pool_r[g % 2], ACT.Copy).then_inc(sem("pool_y"), 1)
            pool_front(0)
            for g in range(1, 4):
                pool_front(g)
                pool_back(g - 1)
            pool_back(3)
            def pair(i, first=False):
                for j, dst in enumerate((qf, kf, vf)):
                    if j == 2 or not first:
                        split_high(act, P_PAIR + AHEAD + j, i, 4)
                    act.wait_ge(used, turn(P_PAIR + j + 1, i, 4))
                    act.activation(dst, PS[:, j, :], ACT.Copy, scale=0.125 if j == 0 else 1.0)\
                       .then_inc(sem("proj_ev"), 1)
                split_high(act, P_PAIR + AHEAD + 3, i, 4)
                for j in range(2):
                    def step(k):
                        st = 3 - k
                        n = SEQ - P * st
                        return gst(i, 8, 4 * j + k + 1), slice(TRI_OFF[st], TRI_OFF[st] + n), ABS[k % 2][:, 0:n]
                    for k in range(5):
                        if k < 4:
                            c8, _, ab = step(k)
                            act.wait_ge(sem("z_ready"), c8)
                            if 4 * j + k >= 2:
                                act.wait_ge(sem("att_sp"), gst(i, 8, 4 * j + k - 1))
                            act.activation(ab, PS[:, 7 - k, P * (3 - k):SEQ], ACT.Abs).then_inc(sem("att_abs"), 1)
                        if k:
                            c8, _, ab = step(k - 1)
                            act.wait_ge(sem("att_e"), c8)
                            act.activation(ab, ab, ACT.Ln, bias=1.0).then_inc(sem("att_ln"), 1)
                        if k < 4:
                            c8, _, ab = step(k)
                            act.wait_ge(sem("att_abs"), c8)
                            act.activation(ab, ab, ACT.Exp, scale=-1.0).then_inc(sem("att_e"), 1)
                        if k:
                            c8, r, ab = step(k - 1)
                            act.wait_ge(sem("att_sp"), c8)
                            act.activation(sph[:, r], SPF[(k - 1) % 2][:, 0:r.stop - r.start], ACT.Copy)\
                               .then_inc(sem("att_hi"), 1)
                    for k in range(4):
                        st = 3 - k
                        act.wait_ge(sem("att_tri"), gst(i, 8, 4 * j + k + 1))
                        act.activation(aprob[:, TRI_OFF[st]:TRI_OFF[st] + SEQ - P * st],
                                       PS[:, 4 + st, P * st:SEQ], ACT.Exp).then_inc(sem("att_p"), 1)
                    if j == 0:
                        act.wait_ge(used, turn(P_PAIR + 4, i, 4))
                        act.activation(ge[0], PS[:, 0, :], ACT.Exp, scale=-1.0, bias=negb[:, bass.ds(i, 1)])\
                           .then_inc(sem("sig_exp"), 1)
                act.wait_ge(sem("att_pv"), gst(i, 2, 2))
                act.activation(Y[:, 0, bass.ds(4 + i, 1), REAL].rearrange("p a t -> p (a t)"),
                               PS[:, 3, :], ACT.Copy).then_inc(sem("o_hi"), 1)
                sigmoid(act, i + 1, ge[0], gates[:, bass.ds(i, 1), :].rearrange("p a t -> p (a t)"))
            pair(0, first=True)
            with act.Fori(1, 4) as i:
                pair(i)
            act.wait_ge(sem("sigmoid"), 4)
            with act.Fori(0, 3) as i:
                for j in range(4):
                    b = j % 2
                    split_high(act, P_GATE + AHEAD + j, i, 4)
                    act.wait_ge(used, turn(P_GATE + j + 1, i, 4))
                    act.activation(ge[b], PS[:, b, :], ACT.Exp, scale=-1.0, bias=negb[:, bass.ds(4 + 4 * i + j, 1)])\
                       .then_inc(sem("sig_exp"), 1)
                    sigmoid(act, gst(i, 4, 4 + j + 1), ge[b],
                            gates[:, bass.ds(4 + 4 * i + j, 1), :].rearrange("p a t -> p (a t)"))
            with act.Fori(0, 2) as i:
                for j in range(4):
                    split_high(act, P_BR + AHEAD + j, i, 4)
                    act.wait_ge(sem("br_sum"), gst(i, 4, j + 1))
                    act.activation(HS[:, 0, bass.ds(4 * i + j, 1), REAL].rearrange("p a t -> p (a t)"),
                                   br_a[j % 2], ACT.Copy).then_inc(sem("br_hi"), 1)
            def square_mix(m):
                norm_square(act, "nA", lambda k: mixf[:, k, :], N1, m, lambda k: (sem("mix_ev"), 2 + k + 1))
            for m in range(8):
                split_high(act, P_OUT + AHEAD + m)
                if m:
                    square_mix(m - 1)
            square_mix(7)
            norm_rsqrt(act, "nA", N1, False)
            norm_squares(act, "n2", lambda k: X[:, k, REAL], N1, ready=lambda k: added("nA", k))
            norm_rsqrt(act, "n2", N1, False)
            norm_high(act, "n2", N1, hs(REAL))
            def square_ff(m):
                norm_square(act, "nB", lambda k: acc1[:, k, :], N1, m, lambda k: (sem("ff_add"), 8 + 24 + k + 1))

            def ff_round(r, last=False):
                for m in range(8):
                    b = m % 2
                    c = gst(r, 8, m + 1)
                    split_high(act, P_FF + AHEAD + m, r, 16)
                    act.wait_ge(used, turn(P_FF + m + 1, r, 16))
                    if m >= 2:
                        act.wait_ge(sem("ff_sq"), gst(r, 8, m - 1))
                    act.activation(relu[b], PS[:, m % 4, :], ACT.Relu).then_inc(sem("ff_relu"), 1)
                    act.wait_ge(sem("ff_relu"), c)
                    act.activation(Y[:, 0, m, REAL], relu[b], ACT.Square).then_inc(sem("ff_hi"), 1)
                for m in range(8):
                    split_high(act, P_FF + AHEAD + 8 + m, r, 16)
                    if last and m:
                        square_ff(m - 1)
            with act.Fori(0, 3) as r:
                ff_round(r)
            ff_round(3, last=True)
            square_ff(7)
            norm_rsqrt(act, "nB", N1, False)

            act.wait_ge(sem("late_in"), 64)
            norm_squares(act, "n3", lambda k: X[:, k, :], N2, ready=lambda k: added("nB", k))
            norm_rsqrt(act, "n3", N2, True)
            norm_high(act, "n3", N2, hs(ALL))
            act.wait_ge(sem("ba_rows"), 1)
            act.activation(two(ba_f[0:32, :]), PS[0:32, 6:8, 0:HALF], ACT.Copy).then_inc(sem("ba_copy"), 1)
            act.wait_ge(sem("ba_pe"), 1)
            act.activation(ba_e[:, 0, :, :], PS[:, 6, 0:160].rearrange("p (c n) -> p c n", c=CHUNKS)[:, :, 0:16],
                           ACT.Exp, scale=-1.0).then_inc(sem("ba_act"), 1)
            act.activation(al_e, rows_ab[:, 0:16], ACT.Exp).then_inc(sem("ba_act"), 1)
            act.wait_ge(sem("ba_dve"), 1)
            act.activation(ba_e[:, 2, :, :], ba_e[:, 1, :, :], ACT.Abs).then_inc(sem("ba_act"), 1)
            act.wait_ge(sem("ba_act"), 3)
            act.activation(ba_e[:, 2, :, :], ba_e[:, 2, :, :], ACT.Exp, scale=-1.0).then_inc(sem("ba_act"), 1)
            act.wait_ge(sem("ba_act"), 4)
            act.activation(ba_e[:, 2, :, :], ba_e[:, 2, :, :], ACT.Ln, bias=1.0).then_inc(sem("ba_act"), 1)
            act.wait_ge(sem("ba_pe"), 2)
            gcp = PS[:, 6, 0:160].rearrange("p (c a n) -> p c a n", c=CHUNKS, a=2)
            act.activation(sm[:, 2, :, :], gcp[:, :, 0, :], ACT.Copy).then_inc(sem("ba_act"), 1)
            act.activation(sm[:, 5, :, :], gcp[:, :, 1, :], ACT.Exp).then_inc(sem("ba_act"), 1)
            act.wait_ge(sem("ba_act"), 7)
            act.activation(sm[:, 3, :, :], sm[:, 2, :, :], ACT.Exp).then_inc(sem("ba_act"), 1)
            act.wait_ge(sem("ba_dve"), 7)
            act.activation(sm[:, 4, :, :], sm[:, 4, :, :], ACT.Exp).then_inc(sem("ba_act"), 1)

            with act.Fori(0, NG) as g:
                def lnexp(t):
                    sigmoid(act, nth_conv(g, t), ee[t % 2], ee[t % 2])

                def l2_square(t):
                    act.wait_ge(sem("g_act"), gst(g, 8, t + 1))
                    if t >= 2:
                        act.wait_ge(sem("l2_ps"), gst(g, 4, t - 1))
                    act.activation(l2s[t % 2], QKV[:, t, :], ACT.Square).then_inc(sem("l2_sq"), 1)

                def l2_rsqrt(t):
                    c = gst(g, 4, t + 1)
                    act.wait_ge(sem("l2_ps"), c)
                    if t >= 2:
                        act.wait_ge(sem("l2_done"), gst(g, 4, t - 1))
                    act.activation(two(l2r[t % 2]), acc2(4 + 2 * (t % 2)), ACT.Ln, bias=col("eps"))\
                       .then_inc(sem("l2_ln"), 1)
                    act.wait_ge(sem("l2_ln"), c)
                    act.activation(l2r[t % 2], l2r[t % 2], ACT.Exp, scale=-0.5).then_inc(sem("l2_rs"), 1)
                for t in range(8):
                    split_high(act, P_GDN + AHEAD + t, g, 16)
                    act.wait_ge(used, turn(P_GDN + t + 1, g, 16))
                    if t >= 2:
                        act.wait_ge(sem("g_conv"), gst(g, 8, t - 1))
                    act.activation(two(xp[t % 2][:, 3:]), acc2(2 * (t % 2)), ACT.Copy)\
                       .then_inc(sem("g_xp"), 1)
                    if t:
                        lnexp(t - 1)
                    if 3 <= t < 7:
                        l2_square(t - 3)
                    if t >= 5:
                        l2_rsqrt(t - 5)
                    if t == 7:
                        l2_rsqrt(3)
                    act.wait_ge(sem("g_conv"), gst(g, 8, t + 1))
                    if t >= 2:
                        act.wait_ge(sem("g_act"), gst(g, 8, t - 1))
                    act.activation(ee[t % 2], cv[t % 2], ACT.Exp, scale=-1.0).then_inc(sem("sig_exp"), 1)

                def bank(b, w, parts=P):
                    return PS[0:parts, b, :].rearrange("p (h n) -> p h n", h=HG)[:, :, 0:w]

                def level_0(c):
                    n = tokens(c)[1]
                    act.wait_ge(sem("g_u0ps"), gst(g, CHUNKS, c + 1))
                    act.activation(U[c][0:n, :, 0:n], bank(6 + c % 2, n, n), ACT.Copy).then_inc(sem("g_u0"), 1)

                def decays(c):
                    n = tokens(c)[1]
                    at = gst(g, CHUNKS, c + 1)
                    e = EE[c % 2]
                    act.wait_ge(sem("g_gr"), at)
                    if c >= 2:
                        act.wait_ge(sem("g_at"), at - 2)
                    for h in range(HG):
                        act.activation(e[0:n, h, 0:n], PS[0:n, c % 2, h * P:h * P + n], ACT.Abs,
                                       scale=-1.0, bias=smg[0:n, 2, c, h:h + 1]).then_inc(sem("g_eabs"), 1)
                    act.wait_ge(sem("g_eabs"), gst(g, CHUNKS * HG, (c + 1) * HG))
                    act.activation(e[0:n, :, 0:n], e[0:n, :, 0:n], ACT.Exp, scale=-1.0).then_inc(sem("g_e"), 1)
                decays(0)
                lnexp(7)
                for c in range(1, CHUNKS):
                    decays(c)
                    if c >= 3:
                        level_0(c - 3)
                for c in range(CHUNKS - 3, CHUNKS):
                    level_0(c)
                for s, (l, c) in enumerate(STEPS):
                    n = tokens(c)[1]
                    act.wait_ge(sem("g_q"), gst(g, NS, s + 1))
                    if s >= 2:
                        act.wait_ge(sem("g_d2"), gst(g, NS, s - 1))
                    else:
                        act.wait_ge(sem("g_t0"), gst(g, CHUNKS, CHUNKS))
                    rows = n // 2 if l == LEVELS - 1 else n
                    start = n // 2 if l == LEVELS - 1 else 0
                    act.activation(QS[s % 2][0:rows, :, start:n],
                                   PS[0:rows, s % 2, :].rearrange("p (h n) -> p h n", h=HG)[:, :, start:n],
                                   ACT.Copy).then_inc(sem("g_qs"), 1)
                def norm_o(c):
                    n = tokens(c)[1]
                    at = gst(g, CHUNKS, c + 1)
                    act.wait_ge(sem("g_on"), at)
                    if c:
                        act.wait_ge(sem("g_store"), at - 1)
                    act.activation(RO[:, :, 0:n], bank(2, n), ACT.Ln, bias=col("eps")).then_inc(sem("g_oln"), 1)
                    act.wait_ge(sem("g_oln"), at)
                    act.activation(RO[:, :, 0:n], RO[:, :, 0:n], ACT.Exp, scale=-0.5)\
                       .then_inc(sem("g_ro"), 1)

                def exp_z(t):
                    act.wait_ge(sem("z_copy"), gst(g, 4, t + 1))
                    if t:
                        act.wait_ge(sem("z_silu"), gst(g, 4, t))
                    act.activation(zsig, zrow[t], ACT.Exp, scale=-1.0).then_inc(sem("sig_exp"), 1)

                def sigmoid_z(t):
                    sigmoid(act, nth_z(g, t), zsig, zsig)

                def high_y(t):
                    act.wait_ge(sem("z_y0"), gst(g, 4, t + 1))
                    act.wait_ge(sem("z_y"), gst(g, 4, t + 1))
                    act.activation(Y[:, 0, t, :], zrow[t], ACT.Copy).then_inc(sem("z_hi"), 1)
                for c in range(CHUNKS):
                    n = tokens(c)[1]
                    at = gst(g, CHUNKS, c + 1)
                    if c < 4:
                        split_high(act, P_GDN + AHEAD + 8 + c, g, 16)
                    if c:
                        act.wait_ge(sem("g_gr2"), gst(g, LATER, c))
                        if c > 1:
                            act.wait_ge(sem("g_o"), at - 1)
                        act.activation(QD[:, :, 0:n], bank(2, n), ACT.Exp).then_inc(sem("g_eg"), 1)
                        norm_o(c - 1)
                    act.wait_ge(sem("g_vn"), at)
                    if c:
                        act.wait_ge(sem("g_o"), at - 1)
                    act.activation(VN[0:n, :, :], PS[0:n, 3, :].rearrange("p (h n) -> p h n", h=HG),
                                   ACT.Copy).then_inc(sem("g_vns"), 1)
                    if c != 3:
                        exp_z(min(c, 3))
                    act.wait_ge(sem("g_o"), at)
                    act.activation(SQO[:, :, 0:n], bank(4, n), ACT.Square).then_inc(sem("g_sqo"), 1)
                    if c != 3:
                        sigmoid_z(min(c, 3))
                norm_o(CHUNKS - 1)
                split_high(act, P_GDN + AHEAD + 12, g, 16)
                for t in range(4):
                    high_y(t)
                for t in range(1, 4):
                    split_high(act, P_GDN + AHEAD + 12 + t, g, 16)
            norm_squares(act, "nC", lambda k: accT[:, k, :], N2, ready=lambda k: (sem("g_add"), 8 * (NG + 1)))
            norm_rsqrt(act, "nC", N2, True)
            norm_squares(act, "n4", lambda k: X[:, k, :], N2, ready=lambda k: added("nC", k))
            norm_rsqrt(act, "n4", N2, True)
            split_high(act, P_KV + AHEAD)
            norm_high(act, "n4", N2, hs(ALL))
            act.wait_ge(used, P_KV + 1)
            act.activation(two(N2["sq"][0]), acc2(0), ACT.Square).then_inc(sem("lat_act"), 1)
            act.wait_ge(sem("lat_pe"), 1)
            act.activation(two(rt[0]), acc2(6), ACT.Ln, bias=col("eps")).then_inc(sem("lat_act"), 1)
            act.wait_ge(sem("lat_act"), 2)
            act.activation(rt[0], rt[0], ACT.Exp, scale=-0.5).then_inc(sem("lat_act"), 1)
            act.wait_ge(sem("lat_dve"), 1)
            act.activation(ckv[:, 0, :], rt[1], ACT.Copy).then_inc(sem("lat_act"), 1)
            split_high(act, P_KV + AHEAD + 1)
            split_high(act, P_KV + AHEAD + 2)
            act.wait_ge(used, P_KV + 3)
            norm_high(act, "n5", N2, hs(ALL))
            for t in range(2):
                split_high(act, P_KV + AHEAD + 3 + t)
                act.wait_ge(used, P_KV + 3 + t + 1)
                act.activation(N2r["sq"][t], PS[:, t, :], ACT.Square).then_inc(sem("lat_act"), 1)
            act.wait_ge(sem("lat_pe"), 2)
            act.activation(N2r["rs"], PS[:, 4, :], ACT.Ln, bias=col("eps")).then_inc(sem("lat_act"), 1)
            act.wait_ge(sem("lat_act"), 7)
            act.activation(N2r["rs"], N2r["rs"], ACT.Exp, scale=-0.5).then_inc(sem("lat_act"), 1)
            for t in range(2):
                act.wait_ge(sem("lat_dve"), 6 + 2 * t)
                act.activation(cq[:, 0, t, :], N2r["tmp"][t], ACT.Copy).then_inc(sem("lat_act"), 1)

            SCALE = float(192 ** -0.5)
            with act.Fori(0, NG) as g:
                split_high(act, P_MLA + AHEAD, g, 12)
                act.wait_ge(sem("m_kn"), g + 1)
                for h in range(HG):
                    act.activation(two(KN[:, h, :]), acc2(2 * h), ACT.Copy).then_inc(sem("kn_ev"), 1)
                split_high(act, P_MLA + AHEAD + 1, g, 12)
                act.wait_ge(used, turn(P_MLA + 2, g, 12))
                for h in range(HG):
                    act.activation(QN[:, h, :], PS[:, (5 + h) % 8, :], ACT.Copy, scale=SCALE)\
                       .then_inc(sem("qn_ev"), 1)
                split_high(act, P_MLA + AHEAD + 2, g, 12)
                def exp_z(t):
                    act.wait_ge(sem("z_copy"), gst(g, 4, 16 + t + 1))
                    if t:
                        act.wait_ge(sem("z_silu"), gst(g, 4, 16 + t))
                    act.activation(mzsig, mz[t], ACT.Exp, scale=-1.0).then_inc(sem("sig_exp"), 1)
                for t in range(4):
                    split_high(act, P_MLA + AHEAD + 3 + t, g, 12)
                    if t < 3:
                        exp_z(t)
                        sigmoid(act, nth_mz(g, t), mzsig, mzsig)
                for u in range(18):
                    if u < 16:
                        b, i = u % 2, QUERY_TILES[u % 4]
                        act.wait_ge(sem("m_nmx"), gst(g, 16, u + 1))
                        if u >= 2:
                            act.wait_ge(sem("m_pt"), gst(g, 16, u - 1))
                        if i < 3:
                            s_ap = PS[:, 4 + 2 * b, 0:META + P * (i + 1)]
                            p_ap = PR[b][:, 0:META + P * (i + 1)]
                        else:
                            s_ap, p_ap = acc2(4 + 2 * b), two(PR[b])
                        act.activation(p_ap, s_ap, ACT.Exp, bias=tiny[:, b:b + 1],
                                       accum_out=tiny[:, 2 + b:3 + b]).then_inc(sem("m_p"), 1)
                        if u == 1:
                            exp_z(3)
                        if u == 2:
                            sigmoid(act, nth_mz(g, 3), mzsig, mzsig)
                        if u in (4, 8):
                            split_high(act, P_MLA + AHEAD + 6 + u // 4, g, 12)
                    if 1 <= u <= 16:
                        v = u - 1
                        b = v % 2
                        act.wait_ge(sem("m_pt"), gst(g, 16, v + 1))
                        if v >= 2:
                            act.wait_ge(sem("m_o"), gst(g, 16, v - 1))
                        act.activation(PT[b][0:META, 0, :], PS[0:META, 1 + 2 * b, 0:P], ACT.Copy)\
                           .then_inc(sem("m_pt0"), 1)
                    if u >= 2:
                        v = u - 2
                        b, h, i = v % 2, v // 4, QUERY_TILES[v % 4]
                        act.wait_ge(sem("m_o"), gst(g, 16, v + 1))
                        act.activation(QN[:, h, P * i:P * i + P], PS[:, 1 + 2 * b, 256:256 + P], ACT.Copy)\
                           .then_inc(sem("m_oev"), 1)
                for t in range(4):
                    act.wait_ge(sem("z_y"), gst(g, 4, 16 + t + 1))
                    if t == 0:
                        act.wait_ge(sem("m_o"), gst(g, 16, 16))
                    act.activation(Y[:, 0, t, REAL], mz[t], ACT.Copy).then_inc(sem("z_hi"), 1)
                for t in range(2, 5):
                    split_high(act, P_MLA + AHEAD + 7 + t, g, 12)
            norm_squares(act, "nD", lambda k: accT[:, k, REAL], N2r, ready=lambda k: (sem("m_add"), 8 * (NG + 1)))
            norm_rsqrt(act, "nD", N2r, False)

        @block.vector
        def _(dve):
            def heads(ap, n, w):
                return ap.unsqueeze(2).to_broadcast([n, HG, w])

            def mat_h(i, n):
                return mats[0:n, i, 0:n].unsqueeze(1).to_broadcast([n, HG, n])

            def pairs(ap, n, w):
                return ap.unsqueeze(2).to_broadcast([n, 2, 2, w])

            def by_pair(ap):
                return ap.rearrange("p (a b) n -> p a b n", a=2)

            def bank(b, n, w, parts=HG):
                return PS[0:n, b, 0:parts * P].rearrange("p (h n) -> p h n", h=parts)[:, :, 0:w]

            dve.memset(tiny[:, 8:9], 0.0).then_inc(sem("br_free"), 2)
            dve.memset(tiny[:, 9:10], 0.0).then_inc(sem("mix_ev"), 2)
            norm_sum(dve, "n1", N1)
            dve.wait_ge(sem("consts_in"), 32)
            dve.tensor_scalar(negb[:, :], cols[:, COL["b_gate"]:COL["b_gate"] + 16], -1.0, None, ALU.mult)\
               .then_inc(sem("negb"), 1)
            norm_apply(dve, "n1", lambda k: X[:, k, REAL], "g_pre_mix", N1, hs(REAL))
            dve.wait_ge(sem("wp_hi"), 2)
            dve.tensor_tensor(wp_s[:, 1, :], wp_raw, wp_s[:, 0, :].bitcast(F32), ALU.subtract)\
               .then_inc(sem("wp_lo"), 1)
            dve.tensor_tensor(wba_s[:, 1, :, :], wba_raw.rearrange("p (k n) -> p k n", k=KT),
                              wba_s[:, 0, :, :].bitcast(F32), ALU.subtract).then_inc(sem("wp_lo"), 1)
            for r in (pa, pb, pc):
                dve.memset(r[:, 0:PADC], 0.0).then_inc(sem("pads"), 1)
            dve.wait_ge(sem("pads"), 3)

            def pool_front(g):
                steps = g * (g + 1) // 2
                dve.wait_ge(sem("proj_ev"), g + 1)
                src, w = pa, 1
                for k in range(g + 1):
                    dst = (pb, pc)[k % 2]
                    if k:
                        dve.wait_ge(sem("double"), steps)
                    dve.tensor_tensor(dst[:, PADC:], src[:, PADC:], src[:, PADC - w:PADC - w + SEQ], ALU.add)\
                       .then_inc(sem("double"), 1)
                    steps += 1
                    src, w = dst, 2 * w
                dve.wait_ge(sem("double"), steps)
                r = pool_r[g % 2]
                if g >= 2:
                    dve.wait_ge(sem("pool_y_lo"), g - 1)
                dve.scalar_tensor_tensor(out=r, in0=src[:, PADC:], scalar=1.0 / w, in1=pa[:, PADC:],
                                         op0=ALU.mult, op1=ALU.subtract).then_inc(sem("pool_a"), 1)
                dve.wait_ge(sem("pool_a"), 2 * g + 1)
                dve.tensor_tensor(src[:, PADC:PADC + w], src[:, PADC:PADC + w],
                                  cols[:, COL["inverse"]:COL["inverse"] + w], ALU.mult)\
                   .then_inc(sem("pool_a"), 1)
                dve.wait_ge(sem("pool_a"), 2 * g + 2)
                dve.tensor_tensor(r[:, 0:w], src[:, PADC:PADC + w], pa[:, PADC:PADC + w], ALU.subtract)\
                   .then_inc(sem("pooled"), 1)
                dve.wait_ge(sem("pool_hi"), g + 1)
                dve.tensor_tensor(pool_c[g % 2][1], r, pool_c[g % 2][0].bitcast(F32), ALU.subtract)\
                   .then_inc(sem("pool_lo"), 1)

            def pool_back(g):
                r = pool_r[g % 2]
                dve.wait_ge(sem("pool_mm"), g + 1)
                dve.tensor_scalar(r, PS[:, 3, :], col("pool_scale", g), None, ALU.mult)\
                   .then_inc(sem("pool_scaled"), 1)
                dve.wait_ge(sem("pool_y"), g + 1)
                dve.tensor_tensor(Y[:, 1, g, REAL], r, Y[:, 0, g, REAL].bitcast(F32), ALU.subtract)\
                   .then_inc(sem("pool_y_lo"), 1)
            pool_front(0)
            for g in range(1, 4):
                pool_front(g)
                pool_back(g - 1)
            pool_back(3)
            with dve.Fori(0, 4) as i:
                for j in range(2):
                    for k in range(4):
                        st = 3 - k
                        n = SEQ - P * st
                        c8 = gst(i, 8, 4 * j + k + 1)
                        dve.wait_ge(sem("att_ln"), c8)
                        dve.scalar_tensor_tensor(out=SPF[k % 2][:, 0:n], in0=PS[:, 4 + st, P * st:SEQ],
                                                 scalar=0.0, in1=ABS[k % 2][:, 0:n], op0=ALU.max, op1=ALU.add)\
                           .then_inc(sem("att_sp"), 1)
                        dve.wait_ge(sem("att_hi"), c8)
                        o = TRI_OFF[st]
                        dve.tensor_tensor(spl[:, o:o + n], SPF[k % 2][:, 0:n], sph[:, o:o + n].bitcast(F32),
                                          ALU.subtract).then_inc(sem("att_lo"), 1)
                    if j == 0:
                        dve.wait_ge(sem("vt_ps"), i + 1)
                        dve.tensor_copy(vt, PS[:, 1, :].rearrange("p (s c) -> p s c", s=4))\
                           .then_inc(sem("vt_sb"), 1)
                        clamp(dve, i + 1, ge[0])
                dve.wait_ge(sem("o_hi"), i + 1)
                dve.tensor_tensor(Y[:, 1, bass.ds(4 + i, 1), REAL].rearrange("p a t -> p (a t)"), PS[:, 3, :],
                                  Y[:, 0, bass.ds(4 + i, 1), REAL].rearrange("p a t -> p (a t)").bitcast(F32),
                                  ALU.subtract).then_inc(sem("o_lo"), 1)
            with dve.Fori(0, 3) as i:
                for j in range(4):
                    clamp(dve, gst(i, 4, 4 + j + 1), ge[j % 2])
            dve.wait_ge(sem("sigmoid"), 16)
            with dve.Fori(0, 2) as i:
                for j in range(4):
                    b, c = j % 2, gst(i, 4, j + 1)

                    def gate(at):
                        return gates[:, bass.ds(4 * i + j + at, 1), :].rearrange("p a t -> p (a t)")
                    dve.wait_ge(used, turn(P_BR + j + 1, i, 4))
                    dve.tensor_tensor(br_a[b], PS[:, 2 * b, :], gate(0), ALU.mult).then_inc(sem("br_t"), 1)
                    dve.tensor_tensor(br_b[b], PS[:, 2 * b + 1, :], gate(8), ALU.mult)\
                       .then_inc(sem("br_free"), 1)
                    dve.wait_ge(sem("br_t"), c)
                    dve.wait_ge(sem("br_free"), gst(i, 4, 2 + j + 1))
                    dve.tensor_tensor(br_a[b], br_a[b], br_b[b], ALU.add).then_inc(sem("br_sum"), 1)
                    dve.wait_ge(sem("br_hi"), c)

                    def at(part):
                        return HS[:, part, bass.ds(4 * i + j, 1), REAL].rearrange("p a t -> p (a t)")
                    dve.tensor_tensor(at(1), br_a[b], at(0).bitcast(F32), ALU.subtract)\
                       .then_inc(sem("br_lo"), 1)
            for m in range(8):
                dve.wait_ge(used, P_OUT + m + 1)
                dve.tensor_copy(mixf[:, m, :], PS[:, m % 2, :]).then_inc(sem("mix_ev"), 1)
                if m >= 2:
                    norm_sum_step(dve, "nA", N1, m - 1)
            norm_sum_step(dve, "nA", N1, 7)
            norm_add(dve, "nA", lambda k: mixf[:, k, :], "g_post_mix", N1, REAL)
            dve.memset(tiny[:, 8:9], 0.0).then_inc(sem("ff_add"), 8)
            norm_apply(dve, "n2", lambda k: X[:, k, REAL], "g_pre_mlp", N1, hs(REAL))
            dve.wait_ge(sem("acc_zero"), 1)
            def ff_round(r, last=False):
                for m in range(8):
                    b, c = m % 2, gst(r, 8, m + 1)
                    dve.wait_ge(sem("ff_relu"), c)
                    dve.tensor_tensor(relu2[b], relu[b], relu[b], ALU.mult).then_inc(sem("ff_sq"), 1)
                    dve.wait_ge(sem("ff_sq"), c)
                    dve.wait_ge(sem("ff_hi"), c)
                    dve.tensor_tensor(Y[:, 1, m, REAL], relu2[b], Y[:, 0, m, REAL].bitcast(F32), ALU.subtract)\
                       .then_inc(sem("ff_lo"), 1)
                for m in range(8):
                    dve.wait_ge(used, turn(P_FF + 8 + m + 1, r, 16))
                    dve.wait_ge(sem("ff_add"), gst(r, 8, m + 1))
                    dve.tensor_tensor(acc1[:, m, :], acc1[:, m, :], PS[:, m % 4, :], ALU.add)\
                       .then_inc(sem("ff_add"), 1)
                    if last and m >= 2:
                        norm_sum_step(dve, "nB", N1, m - 1)
            with dve.Fori(0, 3) as r:
                ff_round(r)
            ff_round(3, last=True)
            norm_sum_step(dve, "nB", N1, 7)
            norm_add(dve, "nB", lambda k: acc1[:, k, :], "g_post_mlp", N1, REAL)

            dve.wait_ge(sem("late_in"), 64)
            dve.memset(tiny[:, 8:9], 0.0).then_inc(sem("g_add"), 8)
            norm_apply(dve, "n3", lambda k: X[:, k, :], "pre_norm_0", N2, hs(ALL))
            ba = PS[:, 6, 0:160].rearrange("p (c n) -> p c n", c=CHUNKS)
            dve.wait_ge(sem("ba_act"), 1)
            dt_row = rows_ab[:, 16:32].unsqueeze(1).to_broadcast([P, CHUNKS, 16])
            dve.tensor_tensor(ba_e[:, 1, :, :], ba[:, :, 16:32], dt_row, ALU.add).then_inc(sem("ba_dve"), 1)
            dve.tensor_scalar(ba_e[:, 0, :, :], ba_e[:, 0, :, :], 1.0, None, ALU.add).then_inc(sem("ba_dve"), 1)
            dve.wait_ge(sem("ba_dve"), 2)
            dve.reciprocal(sm[:, 0, :, :], ba_e[:, 0, :, :]).then_inc(sem("ba_dve"), 1)
            dve.wait_ge(sem("ba_act"), 5)
            dve.wait_ge(sem("ba_dve"), 1)
            dve.scalar_tensor_tensor(out=ba_e[:, 1, :, :], in0=ba_e[:, 1, :, :], scalar=0.0,
                                     in1=ba_e[:, 2, :, :], op0=ALU.max, op1=ALU.add).then_inc(sem("ba_dve"), 1)
            dve.wait_ge(sem("ba_dve"), 4)
            dve.wait_ge(sem("ba_act"), 2)
            dve.tensor_tensor(ba_e[:, 1, :, :], ba_e[:, 1, :, :],
                              al_e.unsqueeze(1).to_broadcast([P, CHUNKS, 16]), ALU.mult).then_inc(sem("ba_dve"), 1)
            dve.wait_ge(sem("ba_dve"), 5)
            dve.tensor_scalar(sm[:, 1, :, :], ba_e[:, 1, :, :], -1.0, None, ALU.mult).then_inc(sem("ba_dve"), 1)
            gcp = PS[:, 6, 0:160].rearrange("p (c a n) -> p c a n", c=CHUNKS, a=2)
            dve.wait_ge(sem("ba_act"), 7)
            dve.tensor_tensor(sm[:, 4, :, :], gcp[:, :, 1, :], sm[:, 2, :, :], ALU.subtract)\
               .then_inc(sem("ba_dve"), 1)
            dve.wait_ge(sem("ba_act"), 8)
            dve.tensor_tensor(sm[:, 3, :, :], sm[:, 3, :, :], sm[:, 0, :, :], ALU.mult).then_inc(sem("ba_dve"), 1)
            dve.wait_ge(sem("ba_dve"), 8)
            dve.wait_ge(sem("ba_act"), 9)
            dve.wait_ge(sem("acc_zero"), 2)

            with dve.Fori(0, NG) as g:
                dve.tensor_copy(smg[:, :, :, :].rearrange("p a c n -> p (a c) n"),
                                sm[:, :, :, bass.ds(4 * g, 4)].rearrange("p a c n -> p (a c) n"))\
                   .then_inc(sem("g_smg"), 1)
                dve.tensor_copy(cwg[:, :], conv_w[:, bass.ds(32 * g, 32)]).then_inc(sem("g_smg"), 1)
                dve.wait_ge(sem("g_smg"), gst(g, 2, 2))
                for b in range(2):
                    dve.memset(xp[b][:, 0:3], 0.0).then_inc(sem("xp_pad"), 1)
                dve.wait_ge(sem("xp_pad"), gst(g, 2, 2))

                def gated(t):
                    dve.wait_ge(sem("sigmoid"), nth_conv(g, t))
                    dve.tensor_tensor(QKV[:, t, :], cv[t % 2], ee[t % 2], ALU.mult).then_inc(sem("g_act"), 1)

                def l2_scale(t):
                    dve.wait_ge(sem("l2_rs"), gst(g, 4, t + 1))
                    dve.wait_ge(sem("g_act"), gst(g, 8, t + 1))
                    dve.scalar_tensor_tensor(out=QKV[:, t, :], in0=QKV[:, t, :],
                                             scalar=float(128 ** -0.5) if t < 2 else 1.0, in1=l2r[t % 2],
                                             op0=ALU.mult, op1=ALU.mult).then_inc(sem("l2_done"), 1)
                for t in range(8):
                    x, y = xp[t % 2], cv[t % 2]
                    if t >= 2:
                        dve.wait_ge(sem("g_act"), gst(g, 8, t - 1))
                    dve.wait_ge(sem("g_xp"), gst(g, 8, t + 1))
                    dve.tensor_scalar(y, x[:, 0:T], cwg[:, 4 * t:4 * t + 1], None, ALU.mult)\
                       .then_inc(sem("g_taps"), 1)
                    for k in range(1, 4):
                        dve.wait_ge(sem("g_taps"), gst(g, 24, 3 * t + k))
                        dve.scalar_tensor_tensor(out=y, in0=x[:, k:k + T], scalar=cwg[:, 4 * t + k:4 * t + k + 1],
                                                 in1=y, op0=ALU.mult, op1=ALU.add)\
                           .then_inc(sem("g_taps") if k < 3 else sem("g_conv"), 1)
                    if t:
                        gated(t - 1)
                    if t >= 6:
                        l2_scale(t - 6)
                    clamp(dve, nth_conv(g, t), ee[t % 2])
                l2_scale(2)
                l2_scale(3)
                gated(7)
                def level_0(c):
                    n = tokens(c)[1]
                    dve.wait_ge(sem("g_c0"), gst(g, CHUNKS, c + 1))
                    dve.tensor_tensor(TN[c][0:n, :, 0:n], mat_h(IDENT, n), C0[c % 2][0:n, :, 0:n], ALU.subtract)\
                       .then_inc(sem("g_t0"), 1)
                for c in range(CHUNKS):
                    n = tokens(c)[1]
                    at = gst(g, CHUNKS, c + 1)
                    e = EE[c % 2][0:n, :, 0:n]
                    dve.wait_ge(sem("g_kk"), at)
                    dve.wait_ge(sem("g_e"), at)
                    kk = bank(4 + c % 2, n, n)
                    m = M[c][0:n, :, 0:n]
                    a = AT[c][0:n, :, 0:n]
                    dve.tensor_tensor(by_pair(m), pairs(kk[:, 0:2, :], n, n), by_pair(e), ALU.mult)\
                       .then_inc(sem("g_m1"), 1)
                    dve.tensor_tensor(by_pair(a), pairs(kk[:, 2:4, :], n, n), by_pair(e), ALU.mult)\
                       .then_inc(sem("g_at"), 1)
                    if c >= 2:
                        level_0(c - 2)
                level_0(CHUNKS - 2)
                level_0(CHUNKS - 1)

                def copy_z(t):
                    dve.wait_ge(used, turn(P_GDN + 8 + t + 1, g, 16))
                    dve.tensor_copy(two(zrow[t]), acc2(6 if t else 2)).then_inc(sem("z_copy"), 1)
                copy_z(0)
                prev = {}
                for s in range(NS + 1):
                    if s < NS:
                        l, c = STEPS[s]
                        n = tokens(c)[1]
                        dve.wait_ge(sem("g_d2"), gst(g, NS, s + 1))
                        if c in prev:
                            dve.wait_ge(sem("g_u"), gst(g, NS, prev[c] + 1))
                        else:
                            dve.wait_ge(sem("g_u0"), gst(g, CHUNKS, CHUNKS))
                        prev[c] = s
                        rows = n // 2 if l == LEVELS - 1 else n
                        u = joined(U[c][0:rows, :, 0:n], l, 1)
                        dve.tensor_tensor(u, u, joined(bank(2 + s % 2, rows, n), l, 1), ALU.subtract)\
                           .then_inc(sem("g_u"), 1)
                    if s < CHUNKS:
                        n = tokens(s)[1]
                        a = AT[s][0:n, :, 0:n]
                        dve.wait_ge(sem("g_at"), gst(g, CHUNKS, s + 1))
                        dve.tensor_tensor(a, a, mat_h(TRI_U, n), ALU.mult).then_inc(sem("g_at2"), 1)
                    if s - 1 in TURNED:
                        k = TURNED.index(s - 1)
                        l, c = STEPS[s - 1]
                        n = tokens(c)[1]
                        dve.wait_ge(sem("g_tr"), gst(g, NT, k + 1))
                        if k == 0:
                            dve.wait_ge(sem("g_t0"), gst(g, CHUNKS, CHUNKS))
                        dve.tensor_copy(joined(TN[c][0:n, :, 0:n], l, 0), joined(bank(4 + k % 2, n, n), l, 0))\
                           .then_inc(sem("g_tn"), 1)
                def store(c):
                    o, n = tokens(c)
                    dve.wait_ge(sem("g_ro"), gst(g, CHUNKS, c + 1))
                    dve.tensor_tensor(QKV[:, 4:8, o:o + n], bank(4, P, n), RO[:, :, 0:n], ALU.mult)\
                       .then_inc(sem("g_store"), 1)

                def silu_z(t):
                    dve.wait_ge(sem("z_copy"), gst(g, 4, t + 1))
                    dve.wait_ge(sem("sigmoid"), nth_z(g, t))
                    dve.tensor_tensor(zrow[t], zrow[t], zsig, ALU.mult).then_inc(sem("z_silu"), 1)

                def gate_y(t, c):
                    r = slice(0, T - P) if c < LATER else slice(T - P, T)
                    dve.wait_ge(sem("z_silu"), gst(g, 4, t + 1))
                    dve.wait_ge(sem("g_store"), gst(g, CHUNKS, c + 1))
                    dve.scalar_tensor_tensor(out=zrow[t][:, r], in0=QKV[:, 4 + t, r], scalar=col("out_norm"),
                                             in1=zrow[t][:, r], op0=ALU.mult, op1=ALU.mult)\
                       .then_inc(sem("z_y0") if c < LATER else sem("z_y"), 1)

                def low_y(t):
                    dve.wait_ge(sem("z_hi"), gst(g, 4, t + 1))
                    dve.tensor_tensor(Y[:, 1, t, :], zrow[t], Y[:, 0, t, :].bitcast(F32), ALU.subtract)\
                       .then_inc(sem("z_lo"), 1)
                for c in range(CHUNKS):
                    o, n = tokens(c)
                    at, later = gst(g, CHUNKS, c + 1), gst(g, LATER, c)
                    if c == 1:
                        dve.wait_ge(sem("g_vn"), at - 1)
                    if c > 1:
                        dve.wait_ge(sem("g_r"), later - 1)
                    dve.wait_ge(sem("g_kt"), at)
                    dve.tensor_tensor(VB[0:n, :, :], bank(1, n, P), heads(smg[0:n, 0, c, :], n, P), ALU.mult)\
                       .then_inc(sem("g_vb"), 1)
                    if c:
                        dve.wait_ge(sem("g_ks"), later)
                        dve.tensor_tensor(R[0:n, :, :], bank(3, n, P), heads(smg[0:n, 3, c, :], n, P), ALU.mult)\
                           .then_inc(sem("g_r1"), 1)
                        dve.wait_ge(sem("g_r1"), later)
                        dve.wait_ge(sem("g_vb"), at)
                        dve.tensor_tensor(R[0:n, :, :], VB[0:n, :, :], R[0:n, :, :], ALU.subtract)\
                           .then_inc(sem("g_r"), 1)
                    if c < LATER:
                        if c:
                            dve.wait_ge(sem("g_su"), later)
                        for q in range(2):
                            dve.tensor_tensor(KD[0:n, 2 * q:2 * q + 2, :],
                                              PS[0:n, 0, q * P:(q + 1) * P].unsqueeze(1).to_broadcast([n, 2, P]),
                                              smg[0:n, 4, c, 2 * q:2 * q + 2].unsqueeze(2).to_broadcast([n, 2, P]),
                                              ALU.mult).then_inc(sem("g_kd"), 1)
                    if c:
                        if c < LATER:
                            dve.wait_ge(sem("g_s"), later)
                            dve.tensor_tensor(SD, S, heads(smg[:, 5, c, :], P, P), ALU.mult)\
                               .then_inc(sem("g_s1"), 1)
                        dve.wait_ge(sem("g_eg"), later)
                        dve.tensor_tensor(by_pair(QD[:, :, 0:n]), by_pair(QD[:, :, 0:n]),
                                          pairs(QKV[:, 0:2, o:o + n], P, n), ALU.mult).then_inc(sem("g_qd"), 1)
                        store(c - 1)
                    if 1 <= c < 4:
                        silu_z(c - 1)
                    if c in (1, 2, 4):
                        copy_z(min(c, 3))
                    if c < LATER:
                        dve.wait_ge(sem("g_su"), gst(g, LATER, c + 1))
                        if c:
                            dve.wait_ge(sem("g_s1"), gst(g, LATER - 1, c))
                            dve.tensor_tensor(S, SD, bank(5, P, P), ALU.add).then_inc(sem("g_s"), 1)
                        else:
                            dve.tensor_copy(S, bank(5, P, P)).then_inc(sem("g_s"), 1)
                    if c != 3:
                        clamp(dve, nth_z(g, min(c, 3)), zsig)
                for t in range(3):
                    gate_y(t, LATER - 1)
                silu_z(3)
                gate_y(3, LATER - 1)
                store(LATER)
                gate_y(0, LATER)
                gate_y(1, LATER)
                gate_y(2, LATER)
                low_y(0)
                gate_y(3, LATER)
                low_y(1)
                low_y(2)
                low_y(3)
                for m in range(8):
                    if m % 2 == 0:
                        dve.wait_ge(used, turn(P_GDN + 12 + m // 2 + 1, g, 16))
                    dve.wait_ge(sem("g_add"), gst(g, 8, m + 1))
                    dve.tensor_tensor(two(accT[:, m, :]), two(accT[:, m, :]), acc2(2 * (m % 2)), ALU.add)\
                       .then_inc(sem("g_add"), 1)
            norm_sum(dve, "nC", N2)
            norm_add(dve, "nC", lambda k: accT[:, k, :], "post_norm_0", N2, ALL)
            dve.memset(tiny[:, 8:9], 0.0).then_inc(sem("m_add"), 8)
            norm_apply(dve, "n4", lambda k: X[:, k, :], "kv_norm", N2, hs(ALL))
            dve.wait_ge(sem("lat_act"), 3)
            dve.scalar_tensor_tensor(out=two(rt[1]), in0=acc2(0), scalar=col("kv_latent_norm"), in1=two(rt[0]),
                                     op0=ALU.mult, op1=ALU.mult).then_inc(sem("lat_dve"), 1)
            dve.wait_ge(sem("lat_act"), 4)
            dve.tensor_tensor(ckv[:, 1, :], rt[1], ckv[:, 0, :].bitcast(F32), ALU.subtract)\
               .then_inc(sem("lat_dve"), 1)
            dve.wait_ge(used, P_KV + 3)
            dve.tensor_tensor(two(rk[0]), acc2(2), two(rope[:, 0, :]), ALU.mult).then_inc(sem("lat_dve"), 1)
            dve.tensor_tensor(two(rk[1]), acc2(4), two(rope[:, 1, :]), ALU.mult).then_inc(sem("lat_dve"), 1)
            dve.wait_ge(sem("lat_dve"), 4)
            dve.tensor_tensor(krope, rk[0], rk[1], ALU.add).then_inc(sem("lat_dve"), 1)
            norm_apply(dve, "n5", lambda k: X[:, k, :], "pre_norm_1", N2, hs(ALL), need="n4")
            for t in range(2):
                dve.wait_ge(sem("lat_act"), 8)
                dve.scalar_tensor_tensor(out=N2r["tmp"][t], in0=PS[:, t, :], scalar=col("q_latent_norm", t),
                                         in1=N2r["rs"], op0=ALU.mult, op1=ALU.mult).then_inc(sem("lat_dve"), 1)
                dve.wait_ge(sem("lat_act"), 9 + t)
                dve.tensor_tensor(cq[:, 1, t, :], N2r["tmp"][t], cq[:, 0, t, :].bitcast(F32), ALU.subtract)\
                   .then_inc(sem("lat_dve"), 1)
            dve.wait_ge(sem("acc_zero"), 3)

            with dve.Fori(0, NG) as g:
                dve.wait_ge(used, turn(P_MLA + 1, g, 12))
                for c in range(CHUNKS):
                    n = tokens(c)[1]
                    dve.tensor_copy(VT[0:n, c, :], PS[0:n, c, :]).then_inc(sem("v_ev"), 1)
                dve.wait_ge(used, turn(P_MLA + 3, g, 12))
                for q in range(2):
                    if q:
                        dve.wait_ge(sem("qr_done"), gst(g, 2, 1))
                    dve.scalar_tensor_tensor(out=rt[0][:, 0:SEQ], in0=PS[:, 1 + q, :], scalar=float(192 ** -0.5),
                                             in1=rope[:, 0, META:T], op0=ALU.mult, op1=ALU.mult)\
                       .then_inc(sem("qr_t"), 1)
                    dve.scalar_tensor_tensor(out=rt[1][:, 0:SEQ], in0=PS[:, 3 + q, :], scalar=float(192 ** -0.5),
                                             in1=rope[:, 1, META:T], op0=ALU.mult, op1=ALU.mult)\
                       .then_inc(sem("qr_t"), 1)
                    dve.wait_ge(sem("qr_t"), gst(g, 4, 2 * q + 2))
                    dve.tensor_tensor(QR[:, q, :], rt[0][:, 0:SEQ], rt[1][:, 0:SEQ], ALU.add)\
                       .then_inc(sem("qr_done"), 1)
                def silu_z(t):
                    dve.wait_ge(sem("sigmoid"), nth_mz(g, t))
                    dve.tensor_tensor(mz[t], mz[t], mzsig, ALU.mult).then_inc(sem("z_silu"), 1)

                def gate_y(t):
                    dve.wait_ge(sem("z_silu"), gst(g, 4, 16 + t + 1))
                    dve.wait_ge(sem("m_oev"), gst(g, 16, 4 * t + 4))
                    dve.tensor_tensor(mz[t], QN[:, t, :], mz[t], ALU.mult).then_inc(sem("z_y"), 1)
                for t in range(4):
                    dve.wait_ge(used, turn(P_MLA + 3 + t + 1, g, 12))
                    if t == 0:
                        dve.wait_ge(sem("qr_done"), gst(g, 2, 2))
                    dve.tensor_copy(mz[t], PS[:, 5 + t % 2, :]).then_inc(sem("z_copy"), 1)
                    dve.wait_ge(sem("z_copy"), gst(g, 4, 16 + t + 1))
                    if t:
                        silu_z(t - 1)
                    if t < 3:
                        clamp(dve, nth_mz(g, t), mzsig)
                for u in range(17):
                    if u < 16:
                        b, i, at = u % 2, QUERY_TILES[u % 4], gst(g, 16, u + 1)
                        dve.wait_ge(sem("m_s"), at)
                        s_ap = PS[:, 4 + 2 * b, 0:META + P * (i + 1)] if i < 3 else acc2(4 + 2 * b)
                        dve.tensor_reduce(tiny[:, 4 + b:5 + b], s_ap, AX.X if i < 3 else AX.XY, ALU.max)\
                           .then_inc(sem("m_mx"), 1)
                        dve.wait_ge(sem("m_mx"), at)
                        dve.tensor_scalar(tiny[:, b:b + 1], tiny[:, 4 + b:5 + b], -1.0, None, ALU.mult)\
                           .then_inc(sem("m_nmx"), 1)
                        dve.wait_ge(sem("m_p"), at)
                        dve.reciprocal(tiny[:, 6 + b:7 + b], tiny[:, 2 + b:3 + b]).then_inc(sem("m_rd"), 1)
                        dve.wait_ge(sem("m_rd"), at)
                        w = META + P * (i + 1)
                        dve.tensor_scalar(PR[b][:, 0:w], PR[b][:, 0:w], tiny[:, 6 + b:7 + b], None, ALU.mult)\
                           .then_inc(sem("m_pn"), 1)
                        if u == 1:
                            clamp(dve, nth_mz(g, 3), mzsig)
                        if u == 3:
                            silu_z(3)
                    if u:
                        v = u - 1
                        b, i = v % 2, QUERY_TILES[v % 4]
                        dve.wait_ge(sem("m_pt"), gst(g, 16, v + 1))
                        if v >= 2:
                            dve.wait_ge(sem("m_o"), gst(g, 16, v - 1))
                        dve.tensor_copy(PT[b][:, 1:i + 2, :],
                                        PS[:, 2 * b, 0:P * (i + 1)].rearrange("p (c n) -> p c n", n=P))\
                           .then_inc(sem("m_pts"), 1)
                    if u in (6, 10, 14):
                        gate_y(u // 4 - 1)
                gate_y(3)
                for t in range(4):
                    dve.wait_ge(sem("z_hi"), gst(g, 4, 16 + t + 1))
                    dve.tensor_tensor(Y[:, 1, t, REAL], mz[t], Y[:, 0, t, REAL].bitcast(F32), ALU.subtract)\
                       .then_inc(sem("z_lo"), 1)
                for m in range(8):
                    if m % 2 == 0:
                        dve.wait_ge(used, turn(P_MLA + 7 + m // 2 + 1, g, 12))
                    dve.wait_ge(sem("m_add"), gst(g, 8, m + 1))
                    dve.tensor_tensor(accT[:, m, REAL], accT[:, m, REAL], PS[:, m % 4, :], ALU.add)\
                       .then_inc(sem("m_add"), 1)
            norm_sum(dve, "nD", N2r)
            norm_add(dve, "nD", lambda k: accT[:, k, REAL], "post_norm_1", N2r, REAL)

        @block.tensor
        def _(pe):
            def quads(b, h, n, w):
                return PS[0:n, b, h * P:h * P + w]

            def pool_map(g):
                pe.wait_ge(sem("wp_lo"), 1)
                pe.wait_ge(sem("pool_lo"), g + 1)
                if g:
                    pe.wait_ge(sem("pool_scaled"), g)
                c = slice(g * P, (g + 1) * P)
                mm3(pe, PS[:, 3, :], wp_s[:, 0, c], wp_s[:, 1, c], pool_c[g % 2][0], pool_c[g % 2][1], True, True)\
                    .then_inc(sem("pool_mm"), 1)

            pe.wait_ge(sem("consts_in"), 32)
            norm_mean(pe, "n1", N1, False)
            pe.wait_ge(lo_ready, P_U + 2)
            for kt in range(KT):
                pe.wait_ge(*split_ready("n1", kt + 1))
                for m in range(2):
                    last = mm3(pe, PS[:, m, :], *panel(P_U + m, kt), HS[:, 0, kt, REAL], HS[:, 1, kt, REAL],
                               kt == 0, kt == KT - 1)
                    if kt == KT - 1:
                        last.then_inc(used, 1)
            for g in range(2, 4):
                tile_512(pe, P_U + g, POOL_BANKS[g], HS)
                pool_map(g - 2)
            pe.wait_ge(sem("const_act"), 5)
            def pair(i, first=False):
                for j in range(3):
                    if first:
                        pe.wait_ge(sem("proj_ev"), j + 1)
                    tile_512(pe, P_PAIR + j, j, HS, i, 4)
                    if first and j:
                        pool_map(j + 1)
                if first:
                    pe.wait_ge(sem("pool_y_lo"), 4)
                def scores(j):
                    r = slice(64 * j, 64 * j + 64)
                    for k in range(4):
                        st = 3 - k
                        if j:
                            pe.wait_ge(sem("att_p"), gst(i, 8, k + 1))
                        pe.matmul(PS[:, 4 + st, P * st:SEQ], kf[r, st * P:(st + 1) * P], qf[r, P * st:SEQ],
                                  start=True, stop=True)
                        pe.matmul(PS[:, 4 + st, P * st:P * st + P], mats_b[:, 0, :], mats_b[:, 1, :],
                                  start=False, stop=True, skip_group_check=True).then_inc(sem("z_ready"), 1)

                def tails(j):
                    for k in range(4):
                        st = 3 - k
                        pe.wait_ge(sem("att_lo"), gst(i, 8, 4 * j + k + 1))
                        for part in (sph, spl):
                            for s2 in range(st, 4):
                                x = part[:, TRI_OFF[s2]:TRI_OFF[s2] + SEQ - P * s2]
                                last = pe.matmul(PS[:, 4 + st, P * s2:SEQ], ones_r[:, 0 if s2 == st else 1, :], x,
                                                 start=False, stop=True, skip_group_check=True)
                        last.then_inc(sem("att_tri"), 1)

                def values(j):
                    pe.wait_ge(sem("att_p"), gst(i, 8, 4 * j + 4))
                    pe.wait_ge(sem("vt_sb"), i + 1)
                    for st in range(4):
                        last = pe.matmul(PS[64 * j:64 * j + 64, 3, P * st:SEQ], vt[:, st, 64 * j:64 * j + 64],
                                         aprob[:, TRI_OFF[st]:TRI_OFF[st] + SEQ - P * st],
                                         start=st == 0, stop=st == 3, skip_group_check=True)
                    last.then_inc(sem("att_pv"), 1)
                pe.wait_ge(sem("proj_ev"), gst(i, 3, 4 + 2))
                scores(0)
                tile_512(pe, P_PAIR + 3, 0, HS, i, 4)
                pe.wait_ge(sem("proj_ev"), gst(i, 3, 4 + 3))
                for st in range(4):
                    last = pe.transpose(PS[:, 1, st * P:(st + 1) * P], vf[:, st * P:(st + 1) * P], mat(IDENT))
                last.then_inc(sem("vt_ps"), 1)
                tails(0)
                scores(1)
                values(0)
                tails(1)
                values(1)
            pair(0, first=True)
            with pe.Fori(1, 4) as i:
                pair(i)
            with pe.Fori(0, 3) as i:
                for j in range(4):
                    pe.wait_ge(sem("sig_exp"), gst(i, 4, 4 + j - 1))
                    tile_512(pe, P_GATE + j, j % 2, HS, i, 4)
            pe.wait_ge(sem("sig_exp"), 16)
            pe.wait_ge(sem("pool_y_lo"), 4)
            pe.wait_ge(sem("o_lo"), 4)
            with pe.Fori(0, 2) as i:
                for j in range(4):
                    pe.wait_ge(lo_ready, turn(P_BR + j + 1, i, 4))
                    pe.wait_ge(sem("br_free"), gst(i, 4, j + 1))
                    for kt in range(KT):
                        last = mm3(pe, PS[:, 2 * (j % 2) + kt // 4, :], *panel(P_BR + j, kt),
                                   Y[:, 0, kt, REAL], Y[:, 1, kt, REAL], kt % 4 == 0, kt % 4 == 3)
                    last.then_inc(used, 1)
            pe.wait_ge(sem("br_lo"), 8)
            with pe.Fori(0, 2) as i:
                for j in range(4):
                    pe.wait_ge(sem("mix_ev"), gst(i, 4, j + 1))
                    tile_512(pe, P_OUT + j, j % 2, HS, i, 4)
            norm_mean(pe, "nA", N1, False)
            norm_mean(pe, "n2", N1, False)
            def ff_round(r, last=False):
                pe.wait_ge(lo_ready, turn(P_FF + 2, r, 16))
                pe.wait_ge(sem("ff_add"), gst(r, 8, 6))
                for kt in range(KT):
                    pe.wait_ge(*split_ready("n2", kt + 1))
                    for m in range(2):
                        last = mm3(pe, PS[:, m, :], *panel(P_FF + m, kt), HS[:, 0, kt, REAL], HS[:, 1, kt, REAL],
                                   kt == 0, kt == KT - 1)
                        if kt == KT - 1:
                            last.then_inc(used, 1)
                for m in range(2, 8):
                    if m >= 4:
                        pe.wait_ge(sem("ff_relu"), gst(r, 8, m - 3))
                    else:
                        pe.wait_ge(sem("ff_add"), gst(r, 8, m + 5))
                    tile_512(pe, P_FF + m, m % 4, HS, r, 16)
                pe.wait_ge(sem("ff_relu"), gst(r, 8, 8))
                for m in range(8):
                    if m >= 4:
                        pe.wait_ge(sem("ff_add"), gst(r, 8, 8 + m - 3))
                    pe.wait_ge(lo_ready, turn(P_FF + 8 + m + 1, r, 16))
                    for kt in range(KT):
                        if m == 0:
                            pe.wait_ge(sem("ff_lo"), gst(r, 8, kt + 1))
                        last = mm3(pe, PS[:, m % 4, :], *panel(P_FF + 8 + m, kt), Y[:, 0, kt, REAL], Y[:, 1, kt, REAL],
                                   kt == 0, kt == KT - 1)
                    last.then_inc(used, 1)
            with pe.Fori(0, 3) as r:
                ff_round(r)
            ff_round(3, last=True)
            norm_mean(pe, "nB", N1, False)

            norm_mean(pe, "n3", N2, True)
            for kt in range(KT):
                pe.wait_ge(*split_ready("n3", kt + 1))
                w = [wba_all[:, part * 256 + 32 * kt:part * 256 + 32 * kt + P] for part in range(2)]
                last = mm3t(pe, 6, *w, HS, kt, kt == 0, kt == KT - 1)
            last.then_inc(sem("ba_rows"), 1)
            pe.wait_ge(sem("ba_copy"), 1)
            for c in range(CHUNKS):
                o = tokens(c)[0]
                last = pe.transpose(PS[:, 6, 32 * c:32 * c + 32], ba_f[0:32, o:o + P], mat(IDENT, 32))
            last.then_inc(sem("ba_pe"), 1)
            pe.wait_ge(sem("ba_dve"), 6)
            gcp = PS[:, 6, 0:160].rearrange("p (c a n) -> p c a n", c=CHUNKS, a=2)
            for n, cs in ((META, slice(0, 1)), (P, slice(1, CHUNKS))):
                for a, m in enumerate((TRI_U, ONES)):
                    last = pe.matmul(gcp[:, cs, a, :], mats[0:n, m, :], sm[0:n, 1, cs, :], start=True, stop=True)
            last.then_inc(sem("ba_pe"), 1)

            with pe.Fori(0, NG) as g:
                def l2_sum(t):
                    pe.wait_ge(sem("l2_sq"), gst(g, 4, t + 1))
                    if t >= 2:
                        pe.wait_ge(sem("l2_ln"), gst(g, 4, t - 1))
                    for a in range(2):
                        last = pe.matmul(PS[:, 4 + 2 * (t % 2) + a, 0:HALF], mat(ONES),
                                         l2s[t % 2][:, a * HALF:(a + 1) * HALF], start=True, stop=True)
                    last.then_inc(sem("l2_ps"), 1)
                for t in range(8):
                    if t < 2:
                        pe.wait_ge(sem("g_add"), gst(g, 8, 8))
                    else:
                        pe.wait_ge(sem("g_xp"), gst(g, 8, t - 1))
                    tile_T(pe, P_GDN + t, 2 * (t % 2), HS, g, 16)
                    if t >= 4:
                        l2_sum(t - 4)
                pe.wait_ge(sem("g_smg"), gst(g, 2, 2))

                def decay_rows(b, c):
                    n = tokens(c)[1]
                    for h in range(HG):
                        last = pe.matmul(quads(b, h, P, n), smg[0:n, 1, c, h:h + 1].to_broadcast([n, P]),
                                         mat(TRI_U, n), start=True, stop=True)
                    return last
                def z_part(t, a, k0=0, k1=KT):
                    if a == 0 and k0 == 0:
                        pe.wait_ge(lo_ready, turn(P_GDN + 8 + t + 1, g, 16))
                        if t > 1:
                            pe.wait_ge(sem("z_copy"), gst(g, 4, t))
                    for kt in range(k0, k1):
                        c = slice(a * HALF, (a + 1) * HALF)
                        last = mm3(pe, PS[:, (6 if t else 2) + a, 0:HALF], *panel(P_GDN + 8 + t, kt),
                                   HS[:, 0, kt, c], HS[:, 1, kt, c], kt == 0, kt == KT - 1)
                    if a == 1 and k1 == KT:
                        last.then_inc(used, 1)

                def level_0(c):
                    n = tokens(c)[1]
                    pe.wait_ge(sem("g_t0"), gst(g, CHUNKS, c + 1))
                    if c >= 2:
                        pe.wait_ge(sem("g_u0"), gst(g, CHUNKS, c - 1))
                    carry_wait(pe, n)
                    for h in range(HG):
                        last = pe.transpose(quads(6 + c % 2, h, n, n), TN[c][0:n, h, 0:n], mat(IDENT, n))
                    last.then_inc(sem("g_u0ps"), 1)
                pe.wait_ge(sem("g_xp"), gst(g, 8, 8))
                for c in range(CHUNKS):
                    o, n = tokens(c)
                    at = gst(g, CHUNKS, c + 1)
                    if c >= 2:
                        pe.wait_ge(sem("g_eabs"), gst(g, CHUNKS * HG, (c - 1) * HG))
                    if c != 1:
                        decay_rows(c % 2, c).then_inc(sem("g_gr"), 1)
                    if c == 0:
                        decay_rows(1, 1).then_inc(sem("g_gr"), 1)
                        z_part(0, 0)
                        z_part(0, 1, 0, 2)
                        pe.wait_ge(sem("l2_done"), gst(g, 4, 4))
                    if c >= 2:
                        pe.wait_ge(sem("g_m1"), at - 2)
                        pe.wait_ge(sem("g_at"), at - 2)
                    for q in range(2):
                        k = QKV[:, 2 + q, o:o + n]
                        pe.matmul(quads(4 + c % 2, q, n, n), k, k, start=True, stop=True)
                        last = pe.matmul(quads(4 + c % 2, 2 + q, n, n), k, QKV[:, q, o:o + n],
                                         start=True, stop=True)
                    last.then_inc(sem("g_kk"), 1)
                    if c >= 1:
                        z_part(0, 1, (2, 4, 6, 7)[c - 1], (4, 6, 7, 8)[c - 1])
                    if c >= 3:
                        level_0(c - 3)
                for c in range(CHUNKS - 3, CHUNKS):
                    level_0(c)
                last_of = {}

                def blocks(l, c):
                    n = tokens(c)[1]
                    whole = l != LEVELS - 1
                    return n, slice(0, n if whole else n // 2), slice(0 if whole else n // 2, n)

                def join(s):
                    l, c = STEPS[s]
                    n, first, second = blocks(l, c)
                    b = s % 2
                    pe.wait_ge(sem("g_qs"), gst(g, NS, s + 1))
                    if s == 0:
                        pe.wait_ge(sem("z_copy"), gst(g, 4, 1))
                    if l > 1:
                        pe.wait_ge(sem("g_tn"), gst(g, NT, TURNED.index(STEPS.index((l - 1, c))) + 1))
                    else:
                        pe.wait_ge(sem("g_t0"), gst(g, CHUNKS, c + 1))
                    if s >= 2:
                        pe.wait_ge(sem("g_u"), gst(g, NS, s - 1))
                    carry_wait(pe, first.stop)
                    for h in range(HG):
                        last = pe.matmul(PS[first, 2 + b, h * P + second.start:h * P + n], TN[c][first, h, first],
                                         QS[b][first, h, second], start=True, stop=True)
                    last.then_inc(sem("g_d2"), 1)

                def turn_u(s):
                    l, c = STEPS[s]
                    n = tokens(c)[1]
                    k = TURNED.index(s)
                    pe.wait_ge(sem("g_u"), gst(g, NS, s + 1))
                    if k >= 2:
                        pe.wait_ge(sem("g_tn"), gst(g, NT, k - 1))
                    carry_wait(pe, n)
                    for h in range(HG):
                        last = pe.transpose(quads(4 + k % 2, h, n, n), U[c][0:n, h, 0:n], mat(IDENT, n))
                    last.then_inc(sem("g_tr"), 1)
                for s, (l, c) in enumerate(STEPS):
                    n, first, second = blocks(l, c)
                    pe.wait_ge(sem("g_cl"), gst(g, NS, s + 1))
                    if c in last_of:
                        pe.wait_ge(sem("g_u"), gst(g, NS, last_of[c] + 1))
                    else:
                        pe.wait_ge(sem("g_u0"), gst(g, CHUNKS, c + 1))
                    if s >= 2:
                        pe.wait_ge(sem("g_qs"), gst(g, NS, s - 1))
                    last_of[c] = s
                    carry_wait(pe, first.stop)
                    for h in range(HG):
                        last = pe.matmul(PS[first, s % 2, h * P + second.start:h * P + n],
                                         CL[s % 2][second, h, first], U[c][second, h, second],
                                         start=True, stop=True)
                    last.then_inc(sem("g_q"), 1)
                    if s:
                        join(s - 1)
                    if s - 2 in TURNED:
                        turn_u(s - 2)
                join(NS - 1)
                pe.wait_ge(sem("g_u"), gst(g, NS, NS))

                def norm_o(c):
                    n = tokens(c)[1]
                    at = gst(g, CHUNKS, c + 1)
                    pe.wait_ge(sem("g_sqo"), at)
                    if c < CHUNKS - 1:
                        pe.wait_ge(sem("g_eg"), gst(g, LATER, c + 1))
                    for h in range(HG):
                        last = pe.matmul(quads(2, h, P, n), mat(MEAN_128), SQO[:, h, 0:n], start=True, stop=True)
                    last.then_inc(sem("g_on"), 1)

                before = {1: (1, 0), 2: (2, 0), 3: (3, 0), 4: (3, 1)}
                after = {1: (1, 1), 2: (2, 1)}
                for c in range(CHUNKS):
                    o, n = tokens(c)
                    at, later = gst(g, CHUNKS, c + 1), gst(g, LATER, c)
                    if c:
                        pe.wait_ge(sem("g_kd"), gst(g, 2 * LATER, 2 * c))
                        pe.wait_ge(sem("g_vb"), at - 1)
                    if c < LATER:
                        for q in range(2):
                            pe.transpose(quads(0, q, n, P), QKV[:, 2 + q, o:o + n], mat(IDENT))
                    for h in range(HG):
                        last = pe.transpose(quads(1, h, n, P), QKV[:, 4 + h, o:o + n], mat(IDENT))
                    last.then_inc(sem("g_kt"), 1)
                    if c:
                        if c > 1:
                            pe.wait_ge(sem("g_oln"), at - 2)
                        decay_rows(2, c).then_inc(sem("g_gr2"), 1)
                        pe.wait_ge(sem("g_s"), later)
                        pe.wait_ge(sem("g_vns"), at - 1)
                        for q in range(2):
                            last = pe.matmul(PS[0:n, 3, q * 256:(q + 1) * 256], QKV[:, 2 + q, o:o + n],
                                             S[:, 2 * q:2 * q + 2, :], start=True, stop=True)
                        last.then_inc(sem("g_ks"), 1)
                        z_part(*before[c], 0, 2)
                        norm_o(c - 1)
                        z_part(*before[c], 2)
                    if c:
                        pe.wait_ge(sem("g_r"), later)
                    else:
                        pe.wait_ge(sem("g_vb"), at)
                    carry_wait(pe, n)
                    for h in range(HG):
                        last = pe.matmul(quads(3, h, n, P), U[c][0:n, h, 0:n], (R if c else VB)[0:n, h, :],
                                         start=True, stop=True)
                    last.then_inc(sem("g_vn"), 1)
                    if c in after:
                        z_part(*after[c])
                    if c:
                        pe.wait_ge(sem("g_qd"), later)
                        pe.wait_ge(sem("g_store"), at - 1)
                        for h in range(HG):
                            pe.matmul(quads(4, h, P, n), S[:, h, :], QD[:, h, 0:n], start=h == 0, stop=False,
                                      skip_group_check=True)
                    pe.wait_ge(sem("g_vns"), at)
                    if c < LATER:
                        pe.wait_ge(sem("g_kd"), gst(g, 2 * LATER, 2 * c + 2))
                        if c:
                            pe.wait_ge(sem("g_s"), later)
                        for h in range(HG):
                            last = pe.matmul(quads(5, h, P, P), KD[0:n, h, :], VN[0:n, h, :], start=True, stop=True)
                        last.then_inc(sem("g_su"), 1)
                    for h in range(HG):
                        last = pe.matmul(quads(4, h, P, n), VN[0:n, h, :], AT[c][0:n, h, 0:n],
                                         start=c == 0, stop=True, skip_group_check=True)
                    last.then_inc(sem("g_o"), 1)
                norm_o(CHUNKS - 1)
                for t in range(4):
                    pe.wait_ge(lo_ready, turn(P_GDN + 12 + t + 1, g, 16))
                    for half in range(2):
                        m = 2 * t + half
                        if m >= 2:
                            pe.wait_ge(sem("g_add"), gst(g, 8, 8 + m - 1))
                        for kt in range(4):
                            if m == 0:
                                pe.wait_ge(sem("z_lo"), gst(g, 4, kt + 1))
                            last = mm3t(pe, 2 * half, *panel(P_GDN + 12 + t, 4 * half + kt), Y, kt,
                                        kt == 0, kt == 3)
                    last.then_inc(used, 1)
            norm_mean(pe, "nC", N2, True)
            norm_mean(pe, "n4", N2, True)
            pe.wait_ge(lo_ready, P_KV + 3)
            pe.wait_ge(sem("norm_rs"), nth("n4", 1, 1))
            for kt in range(KT):
                pe.wait_ge(*split_ready("n4", kt + 1))
                for t in range(3):
                    last = mm3t(pe, 2 * t, *panel(P_KV + t, kt), HS, kt, kt == 0, kt == KT - 1)
                    if kt == KT - 1:
                        last.then_inc(used, 1)
            pe.wait_ge(sem("lat_act"), 1)
            for a in range(2):
                last = pe.matmul(PS[:, 6 + a, 0:HALF], mat(MEAN_128), N2["sq"][0][:, a * HALF:(a + 1) * HALF],
                                 start=True, stop=True)
            last.then_inc(sem("lat_pe"), 1)
            pe.wait_ge(sem("lat_dve"), 2)
            for t in range(2):
                tile_512(pe, P_KV + 3 + t, t, HS, x_ready="n5" if t == 0 else None)
            pe.wait_ge(sem("lat_act"), 6)
            pe.wait_ge(sem("lat_dve"), 5)
            for t in range(2):
                last = pe.matmul(PS[:, 4, :], mat(MEAN_256), N2r["sq"][t], start=t == 0, stop=t == 1)
            last.then_inc(sem("lat_pe"), 1)
            pe.wait_ge(sem("lat_dve"), 9)

            with pe.Fori(0, NG) as g:
                pe.wait_ge(lo_ready, turn(P_MLA + 1, g, 12))
                for h in (2, 3, 0, 1):
                    if h == 0:
                        pe.wait_ge(sem("m_add"), gst(g, 8, 8))
                    for a in range(2):
                        c = slice(a * HALF, (a + 1) * HALF)
                        last = mm3(pe, PS[:, 2 * h + a, 0:HALF], *panel(P_MLA, h), ckv[:, 0, c], ckv[:, 1, c],
                                   True, True)
                last.then_inc(sem("m_kn"), 1)
                s = P_MLA % RING
                for c in range(CHUNKS):
                    o = tokens(c)[0]
                    pe.wait_ge(sem("kn_ev"), gst(g, 4, c // 2 + 1))
                    last = mm3(pe, PS[:, c, :], ckv[:, 0, o:o + P], ckv[:, 1, o:o + P],
                               wsp[:, s, 0, 512:1024], wsp[:, s, 1, 512:1024], True, True)
                last.then_inc(used, 1)
                for q in range(2):
                    pe.wait_ge(lo_ready, turn(P_MLA + 1 + q + 1, g, 12))
                    pe.wait_ge(sem("kn_ev"), gst(g, 4, 4))
                    if q:
                        pe.wait_ge(sem("v_ev"), gst(g, 5, 5))
                    for h in range(HG):
                        b = (5 + h) % 8 if q == 0 else 1 + h
                        if b == 0:
                            pe.wait_ge(sem("v_ev"), gst(g, 5, 1))
                        for kt in range(2):
                            last = mm3(pe, PS[:, b, :], *panel(P_MLA + 1 + q, 2 * h + kt),
                                       cq[:, 0, kt, :], cq[:, 1, kt, :], kt == 0, kt == 1)
                    last.then_inc(used, 1)
                pe.wait_ge(sem("qn_ev"), gst(g, 4, 4))
                for t in range(4):
                    if t >= 2:
                        pe.wait_ge(sem("z_copy"), gst(g, 4, 16 + t - 1))
                    tile_512(pe, P_MLA + 3 + t, 5 + t % 2, HS, g, 12)
                pe.wait_ge(sem("z_copy"), gst(g, 4, 16 + 4))
                pe.wait_ge(sem("qr_done"), gst(g, 2, 2))
                for u in range(18):
                    if u < 16:
                        h, i, b = u // 4, QUERY_TILES[u % 4], u % 2
                        if u >= 2:
                            pe.wait_ge(sem("m_p"), gst(g, 16, u - 1))
                        o = META + P * i
                        qn, r = QN[:, h, P * i:P * i + P], slice(64 * (h % 2), 64 * (h % 2) + 64)
                        qr = QR[r, h // 2, P * i:P * i + P]
                        parts = [(4 + 2 * b, 0, o + P)] if i < 3 else \
                            [(4 + 2 * b, 0, HALF), (5 + 2 * b, HALF, T)]
                        for bank_, lo_, hi_ in parts:
                            w = hi_ - lo_
                            pe.matmul(PS[:, bank_, 0:w], qn, KN[:, h, lo_:hi_], start=True, stop=False)
                            last = pe.matmul(PS[:, bank_, 0:w], qr, krope[r, lo_:hi_], start=False, stop=True)
                            if hi_ == o + P:
                                last = pe.matmul(PS[:, bank_, w - P:w], mats_b[:, 0, :], mats_b[:, 2, :],
                                                 start=False, stop=True, skip_group_check=True)
                        last.then_inc(sem("m_s"), 1)
                    if 1 <= u <= 16:
                        v = u - 1
                        i, b = QUERY_TILES[v % 4], v % 2
                        pe.wait_ge(sem("m_pn"), gst(g, 16, v + 1))
                        if v >= 2:
                            pe.wait_ge(sem("m_oev"), gst(g, 16, v - 1))
                            pe.wait_ge(sem("m_pts"), gst(g, 16, v - 1))
                        for c in range(i + 2):
                            o, n = tokens(c)
                            dst = PS[0:n, 1 + 2 * b, 0:P] if c == 0 else PS[:, 2 * b, (c - 1) * P:c * P]
                            last = pe.transpose(dst, PR[b][:, o:o + n], mat(IDENT))
                        last.then_inc(sem("m_pt"), 1)
                    if u >= 2:
                        v = u - 2
                        h, i, b = v // 4, QUERY_TILES[v % 4], v % 2
                        pe.wait_ge(sem("m_pt0"), gst(g, 16, v + 1))
                        pe.wait_ge(sem("m_pts"), gst(g, 16, v + 1))
                        for c in range(i + 2):
                            n = tokens(c)[1]
                            last = pe.matmul(PS[:, 1 + 2 * b, 256:256 + P], VT[0:n, c, h * P:(h + 1) * P],
                                             PT[b][0:n, c, :], start=c == 0, stop=c == i + 1)
                        last.then_inc(sem("m_o"), 1)
                pe.wait_ge(sem("m_oev"), gst(g, 16, 16))
                for t in range(4):
                    pe.wait_ge(lo_ready, turn(P_MLA + 7 + t + 1, g, 12))
                    for half in range(2):
                        m = 2 * t + half
                        if m >= 4:
                            pe.wait_ge(sem("m_add"), gst(g, 8, 8 + m - 3))
                        for kt in range(4):
                            if m == 0:
                                pe.wait_ge(sem("z_lo"), gst(g, 4, 16 + kt + 1))
                            last = mm3(pe, PS[:, m % 4, :], *panel(P_MLA + 7 + t, 4 * half + kt),
                                       Y[:, 0, kt, REAL], Y[:, 1, kt, REAL], kt == 0, kt == 3)
                    last.then_inc(used, 1)
                pe.wait_ge(lo_ready, turn(P_MLA + 12, g, 12))
                pe.matmul(PS[:, 7, 0:2], panel(P_MLA + 11, 0)[0], cq[:, 0, 0, 0:2],
                          start=True, stop=True).then_inc(used, 1)
            norm_mean(pe, "nD", N2r, False)


def host_layout(inp):
    f = {k: np.asarray(v) for k, v in inp.items()}

    def feature_major(x):
        return np.ascontiguousarray(x.T.reshape(-1, P, x.shape[0]).transpose(1, 0, 2))

    def tiles(w):
        k, m = w.shape
        return w.reshape(k // P, P, m // P, P).transpose(2, 1, 0, 3)

    def whole(w):
        return tiles(w).reshape(-1, P, PW)

    def packed(w):
        t = tiles(w)
        per = KT // t.shape[2]
        t = t.reshape(t.shape[0] // per, per, P, t.shape[2], P).transpose(0, 2, 1, 3, 4)
        return t.reshape(-1, P, PW)

    out = []
    win = whole(f["w_in"])
    gate = whole(f["w_gate"])
    out.append(win[0:4])
    for i in range(4):
        out += [win[4 + i:5 + i], win[8 + i:9 + i], win[12 + i:13 + i], gate[i:i + 1]]
    out.append(gate[4:16])
    out.append(whole(np.concatenate([f["w_br_pool"], f["w_br_sb"]], axis=0)))
    out.append(whole(f["w_out"]))
    for r in range(4):
        out.append(whole(f["w_up"][:, 1024 * r:1024 * (r + 1)]))
        out.append(whole(f["w_down"][1024 * r:1024 * (r + 1)]))
    gin, gout = f["gdn_w_in_2"][0], f["gdn_w_out_2"][0]
    for g in range(NG):
        for a, n in ((256 * g, 256), (1024 + 256 * g, 256), (2048 + 512 * g, 512), (4096 + 512 * g, 512)):
            out.append(whole(gin[:, a:a + n]))
        out.append(packed(gout[512 * g:512 * (g + 1)]))
    down = f["kv_w_down_2"]
    x1, x2 = down[:, 128:160], down[:, 160:192]
    out.append(whole(np.concatenate([down[:, 0:128], x1, x2, x1, x2, x2, x1, x2, x1], axis=1)))
    win = f["mla_w_in_2"][0]
    out.append(whole(win[:, 0:256]))
    up = f["kv_w_up_2"].reshape(128, 16, 2, 128)
    qup = f["mla_w_q_up_2"][0].reshape(256, 16, 192)
    wo = f["mla_w_out_2"][0]
    for g in range(NG):
        h = slice(4 * g, 4 * g + 4)
        out.append(packed(np.concatenate([up[:, h, 0].reshape(128, 512), up[:, h, 1].reshape(128, 512)], axis=1)))
        out.append(packed(qup[:, h, 0:128].reshape(256, 512)))
        r = qup[:, h, 128:192]
        swapped = np.concatenate([r[:, :, 32:64], r[:, :, 0:32]], axis=2)
        out.append(packed(np.concatenate([r.reshape(256, 256), swapped.reshape(256, 256)], axis=1)))
        out.append(whole(win[:, 256 + 512 * g:256 + 512 * (g + 1)]))
        out.append(packed(wo[512 * g:512 * (g + 1)]))
        out.append(np.zeros((1, P, PW), np.float32))
    out.append(np.zeros((AHEAD, P, PW), np.float32))
    w = np.concatenate(out, axis=0)
    assert w.shape[0] == STREAM

    def column(v):
        return v.reshape(-1, P).T
    inv = (1.0 / np.arange(1, 17)).astype(np.float32)
    vec = [column(f["g_pre_mix"]), column(f["pool_scale"]), column(f["b_gate"]), column(f["g_post_mix"]),
           column(f["g_pre_mlp"]), column(f["g_post_mlp"]), column(f["pre_norm_2"][0]),
           column(f["post_norm_2"][0]), column(f["pre_norm_2"][1]), column(f["post_norm_2"][1]),
           column(f["kv_norm_2"]), column(f["kv_latent_norm_2"]), column(f["mla_q_latent_norm_2"][0]),
           column(f["gdn_out_norm_2"][0]), np.full((P, 1), 1e-6, np.float32), np.tile(inv, (P, 1))]
    conv = f["gdn_conv_w_2"][0].T.reshape(32, P, 4)
    order = [t for g in range(NG) for t in (2 * g, 2 * g + 1, 8 + 2 * g, 9 + 2 * g,
                                            16 + 4 * g, 17 + 4 * g, 18 + 4 * g, 19 + 4 * g)]
    conv = conv[order].transpose(1, 0, 2).reshape(P, NG * 32)
    rows = np.tile(np.concatenate([f["gdn_a_log_2"][0], f["gdn_dt_bias_2"][0]]), (P, 1))

    a, b = np.arange(P)[:, None], np.arange(P)[None, :]
    one = np.ones((P, P))
    mats = [a == b, a <= b, -1.0 * (a >= b), -one, one, np.where(a >= b, -1e30, 0.0),
            np.where(b > a, -1e30, 0.0), one / 1024, one / 128, one / 256]
    mats += [((a >> l) % 2 == 1) & ((b >> l) == (a >> l) - 1) for l in range(LEVELS)]
    mats = np.stack([np.asarray(m, np.float32) for m in mats], axis=1)
    freq = np.float32(10000.0) ** (-np.arange(0, 64, 2, dtype=np.float32) / np.float32(64))
    ang = np.arange(T, dtype=np.float32)[None, :] * freq[:, None]
    cos, sin = np.cos(ang), np.sin(ang)
    rope = np.stack([np.tile(cos, (4, 1)), np.tile(np.concatenate([-sin, sin]), (2, 1))], axis=1)

    arrays = {
        "x": feature_major(f["x"][0]), "meta": feature_major(f["meta_tokens_2"]), "w": w,
        "w_pool": f["w_pool_mix"].transpose(1, 0, 2).reshape(P, 512),
        "w_ba": gin[:, 6144:6176].reshape(KT, P, 32).transpose(1, 0, 2).reshape(P, 256),
        "cols": np.concatenate(vec, axis=1), "conv": conv, "rows": rows, "rope": rope, "mats": mats,
    }
    return {k: np.ascontiguousarray(v, dtype=np.float32) for k, v in arrays.items()}


def kernel(**inputs):
    from concourse import bacc
    from concourse.bass_utils import run_bass_kernel_spmd

    arrays = {f"in_{k}": v for k, v in host_layout(inputs).items()}
    nc = bacc.Bacc("TRN2", target_bir_lowering=False, num_devices=1)
    A = {k[3:]: nc.dram_tensor(k, v.shape, mybir.dt.from_np(v.dtype), kind="ExternalInput").ap()
         for k, v in arrays.items()}
    out = nc.dram_tensor("out", (P, KT, SEQ), F32, kind="ExternalOutput").ap()
    build(nc, A, out)
    r = run_bass_kernel_spmd(nc, [arrays], core_ids=[0])
    got = r.results[0]["out"]
    return np.ascontiguousarray(got.transpose(2, 1, 0).reshape(1, SEQ, D))
```
